# Optimizing a Trainium2 kernel written in Bass

```python
import math
import jax, jax.numpy as jnp
from jax import lax
import numpy as np

D_MODEL = 1024
BATCH = 1
SEQ = 256
DEPTH = 2

N_EVEN = (DEPTH + 1) // 2
N_ODD = DEPTH // 2
EPS = 1e-6

GM_GROUPS = 4
GM_CH = D_MODEL // 8
GM_WIDTH = GM_GROUPS * GM_CH
GM_CHUNK = 128
POOL_WINDOWS = (2, 4, 8, 16)
POOL_GROUPS = len(POOL_WINDOWS)
POOL_CH = D_MODEL // 8
POOL_WIDTH = POOL_GROUPS * POOL_CH
POOL_MAXW = max(POOL_WINDOWS)
EVEN_IN = 2 * GM_WIDTH + POOL_WIDTH
EVEN_MIX = GM_WIDTH + POOL_WIDTH

DA_HEADS = D_MODEL // 128
DA_QK_DIM = 64
DA_V_DIM = 2 * DA_QK_DIM
DA_Q_WIDTH = DA_HEADS * 2 * DA_QK_DIM
DA_V_WIDTH = DA_HEADS * DA_V_DIM
ODD_IN = 2 * DA_Q_WIDTH + DA_V_WIDTH
Q_BLOCK = 128
ROPE_THETA = 10000.0

PEER_HEADS = 8
PEER_NKEYS = 128
PEER_EXPERTS = PEER_NKEYS * PEER_NKEYS
PEER_QDIM = 256
PEER_HALF = PEER_QDIM // 2
PEER_TOPK = 16
PEER_TOKEN_BLOCK = 128


def rmsnorm(x, g):
    xf = x.astype(jnp.float32)
    y = xf * lax.rsqrt(jnp.mean(xf * xf, axis=-1, keepdims=True) + EPS) * g
    return y.astype(x.dtype)

def apply_rope(t, cos, sin):
    t1, t2 = jnp.split(t, 2, axis=-1)
    return jnp.concatenate([t1 * cos - t2 * sin, t2 * cos + t1 * sin], axis=-1)

def chunked_spatial_gating(u, v, w_s, b_s, g_v):
    B, S, _ = v.shape
    vf = v.astype(jnp.float32)
    mu = jnp.mean(vf, axis=-1, keepdims=True)
    var = jnp.mean((vf - mu) ** 2, axis=-1, keepdims=True)
    vn = ((vf - mu) * lax.rsqrt(var + EPS) * g_v).astype(v.dtype)
    vn = vn.reshape(B, S // GM_CHUNK, GM_CHUNK, GM_GROUPS, GM_CH)
    causal = jnp.tril(jnp.ones((GM_CHUNK, GM_CHUNK), dtype=bool))
    w = jnp.where(causal[None], w_s, 0)
    sv = jnp.einsum('gts,bnsgc->bntgc', w, vn) + b_s.T[None, None, :, :, None]
    return u * sv.reshape(B, S, GM_WIDTH)

def multiscale_pool(p, w_pool, ls):
    B, S, _ = p.shape
    pf = p.astype(jnp.float32)
    cs = jnp.cumsum(pf, axis=1)
    cs_pad = jnp.pad(cs, ((0, 0), (POOL_MAXW, 0), (0, 0)))
    t = jnp.arange(S)
    outs = []
    for g, w in enumerate(POOL_WINDOWS):
        sl = slice(g * POOL_CH, (g + 1) * POOL_CH)
        lag = cs_pad[:, POOL_MAXW - w:POOL_MAXW - w + S, sl]
        cnt = jnp.minimum(t + 1, w).astype(jnp.float32)[None, :, None]
        outs.append((cs[..., sl] - lag) / cnt - pf[..., sl])
    pooled = jnp.stack(outs, axis=2).astype(p.dtype)
    mixed = jnp.einsum('bsgc,gcd->bsgd', pooled, w_pool).reshape(B, S, POOL_WIDTH)
    return mixed * ls

def diff_attention(h, w_in, lam_q1, lam_k1, lam_q2, lam_k2, g_sub, w_out, cos, sin, lam_init):
    B, S, _ = h.shape
    proj = h @ w_in
    q = proj[..., :DA_Q_WIDTH].reshape(B, S, DA_HEADS, 2, DA_QK_DIM)
    k = proj[..., DA_Q_WIDTH:2 * DA_Q_WIDTH].reshape(B, S, DA_HEADS, 2, DA_QK_DIM)
    v = proj[..., 2 * DA_Q_WIDTH:].reshape(B, S, DA_HEADS, DA_V_DIM)
    q = apply_rope(q, cos, sin)
    k = apply_rope(k, cos, sin)
    lam = (jnp.exp(jnp.sum(lam_q1.astype(jnp.float32) * lam_k1.astype(jnp.float32)))
           - jnp.exp(jnp.sum(lam_q2.astype(jnp.float32) * lam_k2.astype(jnp.float32)))
           + lam_init)
    scale = DA_QK_DIM ** -0.5
    outs = []
    for i in range(S // Q_BLOCK):
        kv_len = (i + 1) * Q_BLOCK
        q_i = q[:, i * Q_BLOCK:kv_len]
        s = jnp.einsum('bqhmd,bkhmd->bhmqk', q_i, k[:, :kv_len]).astype(jnp.float32) * scale
        q_pos = i * Q_BLOCK + jnp.arange(Q_BLOCK)
        mask = jnp.arange(kv_len)[None, :] <= q_pos[:, None]
        s = jnp.where(mask, s, -jnp.inf)
        pr = jax.nn.softmax(s, axis=-1)
        a = pr[:, :, 0] - lam * pr[:, :, 1]
        outs.append(jnp.einsum('bhqk,bkhd->bqhd', a.astype(v.dtype), v[:, :kv_len]))
    o = jnp.concatenate(outs, axis=1).astype(jnp.float32)
    o = o * lax.rsqrt(jnp.mean(o * o, axis=-1, keepdims=True) + EPS) * g_sub * (1.0 - lam_init)
    return o.astype(h.dtype).reshape(B, S, DA_V_WIDTH) @ w_out

def peer(h, w_q, sub_keys, u_emb, v_emb):
    B, S, D = h.shape
    T = PEER_TOKEN_BLOCK
    K = PEER_TOPK
    hb = h.reshape(B * S // T, T, D)

    def block(x_t):
        q = jnp.einsum('td,dhk->thk', x_t, w_q).reshape(T, PEER_HEADS, 2, PEER_HALF)
        s = jnp.einsum('thpk,hpnk->thpn', q, sub_keys).astype(jnp.float32)
        sv, si = lax.top_k(s, K)
        cand = (sv[:, :, 0, :, None] + sv[:, :, 1, None, :]).reshape(T, PEER_HEADS, K * K)
        cidx = (si[:, :, 0, :, None] * PEER_NKEYS + si[:, :, 1, None, :]).reshape(T, PEER_HEADS, K * K)
        fv, fpos = lax.top_k(cand, K)
        eidx = jnp.take_along_axis(cidx, fpos, axis=-1)
        gate = jax.nn.softmax(fv, axis=-1)
        u = u_emb[eidx]
        v = v_emb[eidx]
        act = jax.nn.gelu(jnp.einsum('thkd,td->thk', u, x_t).astype(jnp.float32), approximate=False)
        return jnp.einsum('thk,thkd->td', (gate * act).astype(x_t.dtype), v)

    return lax.map(block, hb).reshape(B, S, D)

def first_inputs(seed: int = 0) -> dict:
    key = jax.random.key(seed)
    ks = jax.random.split(key, 32)
    f32 = jnp.float32
    D = D_MODEL

    def nrm(k, shape, scale):
        return jax.random.normal(k, shape, f32) * scale

    def gain(k, shape):
        return 1.0 + 0.02 * jax.random.normal(k, shape, f32)

    return {
        "x": nrm(ks[0], (BATCH, SEQ, D), 1.0),
        "c": nrm(ks[1], (BATCH, D), 1.0),
        "positions": jnp.tile(jnp.arange(SEQ, dtype=jnp.int32)[None, :], (BATCH, 1)),
        "ada_w": nrm(ks[2], (DEPTH, D, 6 * D), 0.5 * D ** -0.5),
        "ada_b": nrm(ks[3], (DEPTH, 6 * D), 0.02),
        "norm_mix": gain(ks[4], (DEPTH, D)),
        "norm_ffn": gain(ks[5], (DEPTH, D)),
        "ev_w_in": nrm(ks[6], (N_EVEN, D, EVEN_IN), D ** -0.5),
        "ev_g_v": gain(ks[7], (N_EVEN, GM_WIDTH)),
        "ev_w_s": nrm(ks[8], (N_EVEN, GM_GROUPS, GM_CHUNK, GM_CHUNK), GM_CHUNK ** -0.5),
        "ev_b_s": gain(ks[9], (N_EVEN, GM_GROUPS, GM_CHUNK)),
        "ev_w_pool": nrm(ks[10], (N_EVEN, POOL_GROUPS, POOL_CH, POOL_CH), POOL_CH ** -0.5),
        "ev_pool_scale": gain(ks[11], (N_EVEN, POOL_WIDTH)),
        "ev_w_out": nrm(ks[12], (N_EVEN, EVEN_MIX, D), EVEN_MIX ** -0.5),
        "od_w_in": nrm(ks[13], (N_ODD, D, ODD_IN), D ** -0.5),
        "od_lam_q1": nrm(ks[14], (N_ODD, DA_QK_DIM), 0.1),
        "od_lam_k1": nrm(ks[15], (N_ODD, DA_QK_DIM), 0.1),
        "od_lam_q2": nrm(ks[16], (N_ODD, DA_QK_DIM), 0.1),
        "od_lam_k2": nrm(ks[17], (N_ODD, DA_QK_DIM), 0.1),
        "od_g_sub": gain(ks[18], (N_ODD, DA_V_DIM)),
        "od_w_out": nrm(ks[19], (N_ODD, DA_V_WIDTH, D), DA_V_WIDTH ** -0.5),
        "peer_w_q": nrm(ks[20], (DEPTH, D, PEER_HEADS, PEER_QDIM), D ** -0.5),
        "peer_sub_keys": nrm(ks[21], (DEPTH, PEER_HEADS, 2, PEER_NKEYS, PEER_HALF), PEER_HALF ** -0.5),
        "peer_u": nrm(ks[22], (DEPTH, PEER_EXPERTS, D), D ** -0.5),
        "peer_v": nrm(ks[23], (DEPTH, PEER_EXPERTS, D), PEER_HEADS ** -0.5),
        "final_norm": gain(ks[24], (D,)),
    }

def first_block(x, c, positions, ada_w, ada_b, norm_mix, norm_ffn,
              ev_w_in, ev_g_v, ev_w_s, ev_b_s, ev_w_pool, ev_pool_scale, ev_w_out,
              od_w_in, od_lam_q1, od_lam_k1, od_lam_q2, od_lam_k2, od_g_sub, od_w_out,
              peer_w_q, peer_sub_keys, peer_u, peer_v, final_norm):
    B, S, D = x.shape
    inv_freq = 1.0 / (ROPE_THETA ** (jnp.arange(0, DA_QK_DIM, 2, dtype=jnp.float32) / DA_QK_DIM))
    ang = positions.astype(jnp.float32)[..., None] * inv_freq
    cos = jnp.cos(ang)[:, :, None, None, :].astype(x.dtype)
    sin = jnp.sin(ang)[:, :, None, None, :].astype(x.dtype)
    c_act = jax.nn.silu(c)
    for l in range(DEPTH):
        mod = (c_act @ ada_w[l] + ada_b[l]).reshape(B, 6, D)[:, :, None, :]
        sh1, sc1, g1, sh2, sc2, g2 = (mod[:, i] for i in range(6))
        h = rmsnorm(x, norm_mix[l]) * (1 + sc1) + sh1
        if l % 2 == 0:
            e = l // 2
            proj = h @ ev_w_in[e]
            z = jax.nn.gelu(proj[..., :2 * GM_WIDTH], approximate=False)
            ya = chunked_spatial_gating(z[..., :GM_WIDTH], z[..., GM_WIDTH:],
                                        ev_w_s[e], ev_b_s[e], ev_g_v[e])
            yb = multiscale_pool(proj[..., 2 * GM_WIDTH:], ev_w_pool[e], ev_pool_scale[e])
            y = jnp.concatenate([ya, yb], axis=-1) @ ev_w_out[e]
        else:
            o = l // 2
            lam_init = 0.8 - 0.6 * math.exp(-0.3 * l)
            y = diff_attention(h, od_w_in[o], od_lam_q1[o], od_lam_k1[o], od_lam_q2[o],
                               od_lam_k2[o], od_g_sub[o], od_w_out[o], cos, sin, lam_init)
        x = x + g1 * y
        h = rmsnorm(x, norm_ffn[l]) * (1 + sc2) + sh2
        x = x + g2 * peer(h, peer_w_q[l], peer_sub_keys[l], peer_u[l], peer_v[l])
    return rmsnorm(x, final_norm)


DEPTH_2 = 1

N_MEM = 256
D_MIX = D_MODEL
HEAD_DIM = 64
RET_WIDTH = D_MIX // 2
RWKV_WIDTH = D_MIX - RET_WIDTH
RET_HEADS = RET_WIDTH // HEAD_DIM
RWKV_HEADS = RWKV_WIDTH // HEAD_DIM
RET_CHUNK = 128
ROPE_BASE = 10000.0
DECAY_LORA = 64
AAA_LORA = 64
GATE_LORA = 160
RET_PROJ = 4 * RET_WIDTH
RWKV_PROJ = 3 * RWKV_WIDTH + DECAY_LORA + AAA_LORA + GATE_LORA
D_IN_PROJ = RET_PROJ + RWKV_PROJ
XATTN_HEADS = 4
XATTN_HEAD_DIM = D_MODEL // XATTN_HEADS
D_FF = 4 * D_MODEL
RMS_EPS = 1e-6
GN_EPS_RET = 1e-5
GN_EPS_RWKV = 64e-5


def rmsnorm_2(x, g):
    xf = x.astype(jnp.float32)
    y = xf * lax.rsqrt(jnp.mean(jnp.square(xf), axis=-1, keepdims=True) + RMS_EPS)
    return (y * g.astype(jnp.float32)).astype(x.dtype)

def head_group_norm(y, w, b, eps):
    B, S, H, d = y.shape
    yf = y.astype(jnp.float32)
    mu = jnp.mean(yf, axis=-1, keepdims=True)
    var = jnp.mean(jnp.square(yf - mu), axis=-1, keepdims=True)
    yn = ((yf - mu) * lax.rsqrt(var + eps)).reshape(B, S, H * d)
    return yn * w.astype(jnp.float32) + b.astype(jnp.float32)

def rope(x, positions):
    d = x.shape[-1]
    half = d // 2
    inv_freq = ROPE_BASE ** (-jnp.arange(half, dtype=jnp.float32) / half)
    ang = positions.astype(jnp.float32)[..., None] * inv_freq
    cos = jnp.cos(ang)[:, :, None, :]
    sin = jnp.sin(ang)[:, :, None, :]
    xf = x.astype(jnp.float32)
    x1, x2 = xf[..., :half], xf[..., half:]
    return jnp.concatenate([x1 * cos - x2 * sin, x2 * cos + x1 * sin], axis=-1)

def retention_chunkwise(q, k, v):
    B, S, H, d = q.shape
    C = RET_CHUNK
    N = S // C
    log_g = jnp.log(1.0 - 2.0 ** (-5.0 - jnp.arange(H, dtype=jnp.float32)))
    idx = jnp.arange(C, dtype=jnp.float32)
    diff = idx[:, None] - idx[None, :]
    causal = diff >= 0
    dmask = jnp.where(causal[None], jnp.exp(log_g[:, None, None] * jnp.where(causal, diff, 0.0)[None]), 0.0)
    xi = jnp.exp(log_g[:, None] * (idx + 1.0)[None])
    zeta = jnp.exp(log_g[:, None] * (C - 1.0 - idx)[None])
    g_chunk = jnp.exp(log_g * C)
    qc = q.reshape(B, N, C, H, d)
    kc = k.reshape(B, N, C, H, d)
    vc = v.reshape(B, N, C, H, d)
    s = jnp.einsum('bnihd,bnjhd->bnhij', qc, kc) * dmask[None, None]
    intra = jnp.einsum('bnhij,bnjhe->bnihe', s, vc)
    kv = jnp.einsum('bnjhd,hj,bnjhe->bnhde', kc, zeta, vc)

    def step(R, kv_n):
        return R * g_chunk[None, :, None, None] + kv_n, R

    _, R_prev = lax.scan(step, jnp.zeros((B, H, d, d), jnp.float32), jnp.moveaxis(kv, 1, 0))
    R_prev = jnp.moveaxis(R_prev, 0, 1)
    inter = jnp.einsum('bnihd,hi,bnhde->bnihe', qc, xi, R_prev)
    return (intra + inter).reshape(B, S, H, d)

def retention_mixer(p, positions, gn_w, gn_b):
    B, S, _ = p.shape
    q, k, v, g = jnp.split(p, 4, axis=-1)
    q = rope(q.reshape(B, S, RET_HEADS, HEAD_DIM), positions)
    k = rope(k.reshape(B, S, RET_HEADS, HEAD_DIM), positions) * (HEAD_DIM ** -0.5)
    v = v.reshape(B, S, RET_HEADS, HEAD_DIM).astype(jnp.float32)
    y = retention_chunkwise(q, k, v)
    return jax.nn.silu(g.astype(jnp.float32)) * head_group_norm(y, gn_w, gn_b, GN_EPS_RET)

def token_shift(p, mu):
    prev = jnp.pad(p, ((0, 0), (1, 0), (0, 0)))[:, :-1]
    return p + (prev - p) * mu

def wkv7_scan(r, w, k, v, a_vec, b_vec):
    B, S, H, d = r.shape

    def step(state, inp):
        r_t, w_t, k_t, v_t, a_t, b_t = inp
        sa = jnp.einsum('bhvk,bhk->bhv', state, a_t)
        state = (state * w_t[:, :, None, :] + sa[..., None] * b_t[:, :, None, :]
                 + v_t[..., None] * k_t[:, :, None, :])
        return state, jnp.einsum('bhvk,bhk->bhv', state, r_t)

    xs = (jnp.moveaxis(r, 1, 0), jnp.moveaxis(w, 1, 0), jnp.moveaxis(k, 1, 0),
          jnp.moveaxis(v, 1, 0), jnp.moveaxis(a_vec, 1, 0), jnp.moveaxis(b_vec, 1, 0))
    _, y = lax.scan(step, jnp.zeros((B, H, d, d), jnp.float32), xs)
    return jnp.moveaxis(y, 0, 1)

def rwkv7_mixer(p, mu, w0, w_up, a0, a_up, g_up, k_k, k_a, r_k, gn_w, gn_b):
    B, S, _ = p.shape
    H, d, W = RWKV_HEADS, HEAD_DIM, RWKV_WIDTH
    p = token_shift(p.astype(jnp.float32), mu.astype(jnp.float32))
    r, k, v, w_lr, a_lr, g_lr = jnp.split(
        p, [W, 2 * W, 3 * W, 3 * W + DECAY_LORA, 3 * W + DECAY_LORA + AAA_LORA], axis=-1)
    w_log = -jax.nn.softplus(-(w0 + jnp.tanh(w_lr) @ w_up)) - 0.5
    decay = jnp.exp(-jnp.exp(w_log))
    a = jax.nn.sigmoid(a0 + a_lr @ a_up)
    g = jax.nn.sigmoid(g_lr) @ g_up
    kk = (k * k_k).reshape(B, S, H, d)
    kk = kk / jnp.maximum(jnp.sqrt(jnp.sum(jnp.square(kk), axis=-1, keepdims=True)), 1e-12)
    k = k * (1.0 + (a - 1.0) * k_a)
    rh = r.reshape(B, S, H, d)
    kh = k.reshape(B, S, H, d)
    vh = v.reshape(B, S, H, d)
    ah = a.reshape(B, S, H, d)
    y = wkv7_scan(rh, decay.reshape(B, S, H, d), kh, vh, -kk, kk * ah)
    y = head_group_norm(y, gn_w, gn_b, GN_EPS_RWKV)
    bonus = jnp.sum(rh * kh * r_k.astype(jnp.float32), axis=-1, keepdims=True) * vh
    return (y + bonus.reshape(B, S, W)) * g

def memory_cross_attention(h, mem_n, w_q, w_kv, w_o):
    B, S, _ = h.shape
    M = mem_n.shape[1]
    q = (h @ w_q).reshape(B, S, XATTN_HEADS, XATTN_HEAD_DIM)
    k, v = jnp.split(mem_n @ w_kv, 2, axis=-1)
    k = k.reshape(B, M, XATTN_HEADS, XATTN_HEAD_DIM)
    v = v.reshape(B, M, XATTN_HEADS, XATTN_HEAD_DIM)
    s = jnp.einsum('bshd,bmhd->bhsm', q.astype(jnp.float32), k.astype(jnp.float32)) * (XATTN_HEAD_DIM ** -0.5)
    prob = jax.nn.softmax(s, axis=-1).astype(v.dtype)
    o = jnp.einsum('bhsm,bmhd->bshd', prob, v).reshape(B, S, D_MODEL)
    return o @ w_o

def second_inputs(seed: int = 0) -> dict:
    key = jax.random.key(seed)
    ks = jax.random.split(key, 32)
    f32 = jnp.float32
    L = DEPTH_2

    def nrm(k, shape, scale):
        return jax.random.normal(k, shape, f32) * scale

    def gain(k, shape):
        return 1.0 + 0.05 * jax.random.normal(k, shape, f32)

    x = jax.random.normal(ks[0], (BATCH, SEQ, D_MODEL), f32)
    mem = jax.random.normal(ks[1], (BATCH, N_MEM, D_MODEL), f32)
    positions = jnp.broadcast_to(jnp.arange(SEQ, dtype=jnp.int32)[None], (BATCH, SEQ))
    return {
        "x": x,
        "mem": mem,
        "positions": positions,
        "norm_mix": gain(ks[2], (L, D_MODEL)),
        "w_in": nrm(ks[3], (L, D_MODEL, D_IN_PROJ), D_MODEL ** -0.5),
        "ret_gn_w": gain(ks[4], (L, RET_WIDTH)),
        "ret_gn_b": nrm(ks[5], (L, RET_WIDTH), 0.02),
        "rwkv_mu": jax.random.uniform(ks[6], (L, RWKV_PROJ), f32),
        "rwkv_w0": jax.random.uniform(ks[7], (L, RWKV_WIDTH), f32, -6.5, -1.5),
        "rwkv_w_up": nrm(ks[8], (L, DECAY_LORA, RWKV_WIDTH), 0.1 * DECAY_LORA ** -0.5),
        "rwkv_a0": nrm(ks[9], (L, RWKV_WIDTH), 0.1),
        "rwkv_a_up": nrm(ks[10], (L, AAA_LORA, RWKV_WIDTH), 0.1 * AAA_LORA ** -0.5),
        "rwkv_g_up": nrm(ks[11], (L, GATE_LORA, RWKV_WIDTH), GATE_LORA ** -0.5),
        "rwkv_k_k": 0.85 + 0.05 * jax.random.normal(ks[12], (L, RWKV_WIDTH), f32),
        "rwkv_k_a": gain(ks[13], (L, RWKV_WIDTH)),
        "rwkv_r_k": nrm(ks[14], (L, RWKV_HEADS, HEAD_DIM), 0.1),
        "rwkv_gn_w": gain(ks[15], (L, RWKV_WIDTH)),
        "rwkv_gn_b": nrm(ks[16], (L, RWKV_WIDTH), 0.02),
        "w_out": nrm(ks[17], (L, D_MIX, D_MODEL), D_MIX ** -0.5),
        "norm_xattn": gain(ks[18], (L, D_MODEL)),
        "norm_mem": gain(ks[19], (L, D_MODEL)),
        "xattn_w_q": nrm(ks[20], (L, D_MODEL, D_MODEL), D_MODEL ** -0.5),
        "xattn_w_kv": nrm(ks[21], (L, D_MODEL, 2 * D_MODEL), D_MODEL ** -0.5),
        "xattn_w_o": nrm(ks[22], (L, D_MODEL, D_MODEL), D_MODEL ** -0.5),
        "norm_mlp": gain(ks[23], (L, D_MODEL)),
        "mlp_w_up": nrm(ks[24], (L, D_MODEL, D_FF), D_MODEL ** -0.5),
        "mlp_w_down": nrm(ks[25], (L, D_FF, D_MODEL), D_FF ** -0.5),
        "norm_final": gain(ks[26], (D_MODEL,)),
    }

def second_block(x, mem, positions, norm_mix, w_in, ret_gn_w, ret_gn_b, rwkv_mu, rwkv_w0,
              rwkv_w_up, rwkv_a0, rwkv_a_up, rwkv_g_up, rwkv_k_k, rwkv_k_a, rwkv_r_k,
              rwkv_gn_w, rwkv_gn_b, w_out, norm_xattn, norm_mem, xattn_w_q, xattn_w_kv,
              xattn_w_o, norm_mlp, mlp_w_up, mlp_w_down, norm_final):
    dt = x.dtype
    for l in range(DEPTH_2):
        h = rmsnorm_2(x, norm_mix[l])
        p = h @ w_in[l]
        y_ret = retention_mixer(p[..., :RET_PROJ], positions, ret_gn_w[l], ret_gn_b[l])
        y_rwkv = rwkv7_mixer(p[..., RET_PROJ:], rwkv_mu[l], rwkv_w0[l], rwkv_w_up[l], rwkv_a0[l],
                             rwkv_a_up[l], rwkv_g_up[l], rwkv_k_k[l], rwkv_k_a[l], rwkv_r_k[l],
                             rwkv_gn_w[l], rwkv_gn_b[l])
        y = jnp.concatenate([y_ret, y_rwkv], axis=-1).astype(dt)
        x = x + y @ w_out[l]
        x = x + memory_cross_attention(rmsnorm_2(x, norm_xattn[l]), rmsnorm_2(mem, norm_mem[l]),
                                       xattn_w_q[l], xattn_w_kv[l], xattn_w_o[l])
        h = rmsnorm_2(x, norm_mlp[l])
        x = x + jnp.square(jax.nn.relu(h @ mlp_w_up[l])) @ mlp_w_down[l]
    return rmsnorm_2(x, norm_final)


def setup_inputs(seed=0):
    out = dict(first_inputs(seed))
    for name, value in second_inputs(seed + 1).items():
        if name != "x":
            out[name + "_2"] = value
    return out


def reference(
    x, c, positions, ada_w, ada_b, norm_mix, norm_ffn, ev_w_in, ev_g_v, ev_w_s, ev_b_s,
    ev_w_pool, ev_pool_scale, ev_w_out, od_w_in, od_lam_q1, od_lam_k1, od_lam_q2, od_lam_k2,
    od_g_sub, od_w_out, peer_w_q, peer_sub_keys, peer_u, peer_v, final_norm, mem_2, positions_2,
    norm_mix_2, w_in_2, ret_gn_w_2, ret_gn_b_2, rwkv_mu_2, rwkv_w0_2, rwkv_w_up_2, rwkv_a0_2,
    rwkv_a_up_2, rwkv_g_up_2, rwkv_k_k_2, rwkv_k_a_2, rwkv_r_k_2, rwkv_gn_w_2, rwkv_gn_b_2,
    w_out_2, norm_xattn_2, norm_mem_2, xattn_w_q_2, xattn_w_kv_2, xattn_w_o_2, norm_mlp_2,
    mlp_w_up_2, mlp_w_down_2, norm_final_2,
):
    x = first_block(
        x, c, positions, ada_w, ada_b, norm_mix, norm_ffn, ev_w_in, ev_g_v, ev_w_s, ev_b_s,
        ev_w_pool, ev_pool_scale, ev_w_out, od_w_in, od_lam_q1, od_lam_k1, od_lam_q2, od_lam_k2,
        od_g_sub, od_w_out, peer_w_q, peer_sub_keys, peer_u, peer_v, final_norm,
    )
    return second_block(
        x, mem_2, positions_2, norm_mix_2, w_in_2, ret_gn_w_2, ret_gn_b_2, rwkv_mu_2, rwkv_w0_2,
        rwkv_w_up_2, rwkv_a0_2, rwkv_a_up_2, rwkv_g_up_2, rwkv_k_k_2, rwkv_k_a_2, rwkv_r_k_2,
        rwkv_gn_w_2, rwkv_gn_b_2, w_out_2, norm_xattn_2, norm_mem_2, xattn_w_q_2, xattn_w_kv_2,
        xattn_w_o_2, norm_mlp_2, mlp_w_up_2, mlp_w_down_2, norm_final_2,
    )


_drawn_inputs = setup_inputs


def setup_inputs(seed=0):
    import zlib

    import numpy as np

    out = dict(_drawn_inputs(seed))
    spreads = {}
    factors = {'norm_mix': 3.981,
     'norm_ffn': 3.41,
     'ev_g_v': 8.0,
     'ev_b_s': 7.454,
     'ev_pool_scale': 6.049,
     'od_lam_q1': 8.0,
     'od_g_sub': 7.06,
     'ret_gn_w_2': 2.876,
     'ret_gn_b_2': 7.042,
     'rwkv_w_up_2': 8.0,
     'rwkv_a0_2': 3.865,
     'rwkv_a_up_2': 3.745,
     'rwkv_k_k_2': 3.352,
     'rwkv_k_a_2': 2.755,
     'rwkv_gn_w_2': 3.26,
     'rwkv_gn_b_2': 7.379,
     'norm_xattn_2': 8.0,
     'norm_mem_2': 7.089,
     'norm_mlp_2': 5.928}
    for name, (base, spread) in spreads.items():
        noise = np.random.default_rng([zlib.crc32(name.encode()), seed]).standard_normal(out[name].shape)
        drawn = base * np.exp(spread * noise) if base else spread * noise
        out[name] = __import__('jax').numpy.asarray(drawn.astype(out[name].dtype))
    for name, factor in factors.items():
        out[name] = (out[name] * factor).astype(out[name].dtype)
    return out
```

```python
import math

import numpy as np

import concourse.bass as bass
from concourse import mybir

F32 = mybir.dt.float32
I32 = mybir.dt.int32
U32 = mybir.dt.uint32
ALU = mybir.AluOpType
ACT = mybir.ActivationFunctionType
AX_X = mybir.AxisListType.X

P = 128
D = 1024
KB = D // P
T = 256
TT = T // P
BANK = 512
RING = 4
HEADS, TOPK, KEYS = 8, 16, 128
CHUNK = 64
CHUNKS = T // CHUNK
EPS = 1e-6
LAM_INIT = 0.8 - 0.6 * math.exp(-0.3)
LOWEST = -3.0e38
ROUND = 1.5 * 2.0 ** 23

CONST = {}
COLS = {}


def shape_constants():
    eye = np.eye(P, dtype=np.float32)
    p = np.arange(P)
    same_half = (p[:, None] // 64 == p[None, :] // 64)
    rot = np.zeros((P, P), np.float32)
    for m in range(P):
        if m % 64 < 32:
            rot[m + 32, m] = -1.0
        else:
            rot[m - 32, m] = 1.0
    half = (p % 32).astype(np.float32)
    inv_a = (np.float32(1.0) / (np.float32(10000.0) ** ((2 * half).astype(np.float32) / np.float32(64)))).astype(np.float32)
    inv_b = (np.float32(10000.0) ** (-(half / np.float32(32)))).astype(np.float32)
    parts = [
        ("ident", eye), ("ones", np.ones((P, P))), ("half_ones", same_half), ("rot", rot),
        ("iota", np.tile(p, (P, 1))), ("iota16", np.tile(np.arange(16), (P, 1))),
        ("eye2", np.concatenate([np.eye(64), np.eye(64)])),
        ("inv_freq_a", inv_a[:, None]), ("inv_freq_b", inv_b[:, None]),
        ("eps", np.full((P, 1), EPS)), ("eps_ret", np.full((P, 1), 1e-5)), ("eps_rwkv", np.full((P, 1), 64e-5)),
        ("zeros", np.zeros((P, P))),
    ]
    at = 0
    for name, a in parts:
        CONST[name] = (at, at + a.shape[1])
        at += a.shape[1]
    resident = np.concatenate([np.asarray(a, np.float32) for _, a in parts], axis=1)

    s, t = p[:, None], p[None, :]
    even_mask = (s <= t).astype(np.float32)
    inv_count = np.zeros((P, 4, T), np.float32)
    for g, w in enumerate((2, 4, 8, 16)):
        inv_count[:, g, :] = 1.0 / np.minimum(np.arange(T) + 1, w)
    diag = np.where(t <= s, 0.0, LOWEST).astype(np.float32)
    attn_mask = np.concatenate([diag, np.zeros((P, P), np.float32), diag], axis=1)
    decay = np.zeros((P, 8, 3 * P), np.float64)
    j = p[:, None]
    for h in range(8):
        lg = np.log(1.0 - 2.0 ** (-5.0 - h))
        i0 = np.arange(T)[None, :]
        decay[:, h, 0:T] = np.where(i0 >= j, np.exp(lg * np.maximum(i0 - j, 0)), 0.0) / 8.0
        i1 = np.arange(P)[None, :]
        decay[:, h, T:] = np.where(i1 >= j, np.exp(lg * np.maximum(i1 - j, 0)), 0.0) / 8.0
    levels = []
    for lv in range(6):
        b = 2 ** lv
        levels.append((t // (2 * b) == s // (2 * b)) & (s // b == t // b + 1) & (s // CHUNK == t // CHUNK))
    chunk_same = s // CHUNK == t // CHUNK
    before = (s < t) & chunk_same
    upto = (s <= t) & chunk_same
    rwkv_masks = np.concatenate([np.concatenate(levels, 1), before, upto], 1).astype(np.float32)
    reset = np.ones((P, 4 * T), np.float32)
    reset[:, ::CHUNK] = 0.0
    return {
        "resident": resident, "even_mask": even_mask, "inv_count": inv_count.reshape(P, -1),
        "attn_mask": attn_mask, "decay": decay.reshape(P, -1).astype(np.float32),
        "rwkv_masks": rwkv_masks, "reset": reset,
    }


class Signal:

    def __init__(self, nc, name):
        self.sem = nc.alloc_semaphore(name)
        self.base = 0

    def at(self, n):
        return n + self.base

    def close(self, raised):
        self.base += raised


class Chain:

    def __init__(self, signal, engine):
        self.steps, self.engine, self.n = signal, engine, 0

    def __call__(self, instruction):
        self.n += 1
        instruction.then_inc(self.steps.sem, 1)
        self.engine.wait_ge(self.steps.sem, self.steps.at(self.n))


class Segment:

    def __init__(self, tiles, count, first):
        self.tiles, self.count, self.first = tiles, count, first


def view(t, at, n, w):
    return t[:, at:at + n * w].rearrange("p (n w) -> p n w", w=w)


class Picks:

    def __init__(self, sb):
        self.keys = sb("pick_keys", [P, TT, 2, KEYS])
        self.rest = sb("pick_rest", [P, TT, 2, KEYS])
        self.top = sb("pick_top", [P, TT, 2, TOPK])
        self.at = sb("pick_at", [P, TT, 2, TOPK], U32)
        self.at_f = sb("pick_at_f", [P, TT, 2, TOPK])
        self.sums = sb("pick_sums", [P, TT, TOPK, TOPK])
        self.sums_rest = sb("pick_sums_rest", [P, TT, TOPK, TOPK])
        self.best = sb("pick_best", [P, TT, TOPK])
        self.place = sb("pick_place", [P, TT, TOPK], U32)
        self.digit = sb("pick_digit", [P, 2, TT, TOPK], U32)
        self.digit_f = sb("pick_digit_f", [P, 2, TT, TOPK])
        self.onehot = sb("pick_onehot", [P, TT, TOPK, TOPK])
        self.chosen = sb("pick_chosen", [P, 2, TT, HEADS * TOPK])
        self.expo = sb("pick_expo", [P, TT, HEADS, TOPK])
        self.total = sb("pick_total", [P, TT * HEADS])
        self.by_pick = sb("by_pick", [P, 3, T])


class Core:

    def __init__(self, nc, dram):
        self.nc, self.dram = nc, dram
        sb = lambda name, shape, dt=F32: nc.alloc_sbuf_tensor(name, shape, dt)
        self.arena = sb("arena", [P, P * T])
        self.x = sb("x_T", [P, KB, T])
        self.h = sb("h_T", [P, KB, T])
        self.h_flat = self.h[:].rearrange("p n t -> p (n t)")
        self.ring = sb("weight_ring", [P, RING, KB * P])
        self.work = sb("work", [P, 4096])
        self.const = sb("const", [P, dram["resident"].shape[1]])
        self.cols = sb("cols", [P, dram["cols"].shape[1]])
        self.mod = sb("mod", [P, 2, 48])
        self.gain = sb("gain", [P, 4, KB])
        self.trig = sb("trig", [P, 4, T])
        self.pick = Picks(sb)
        self.bank = [nc.alloc_psum_tensor(f"bank{i}", [P, BANK], F32) for i in range(8)]
        self.flags = {}
        self.segments = []
        self.next_segment = 0

    def sig(self, name):
        if name not in self.flags:
            self.flags[name] = Signal(self.nc, name)
        return self.flags[name]

    def c(self, name):
        a, b = CONST[name]
        return self.const[:, a:b]

    def col(self, name, n=None):
        a, b = COLS[name]
        return self.cols[:, a:b] if n is None else self.cols[:, a + n:a + n + 1]

    def add_segment(self, name):
        tiles = self.dram[name]
        first = self.segments[-1].first + self.segments[-1].count if self.segments else 0
        self.segments.append(Segment(tiles, tiles.shape[0], first))

    def load_tile(self, sp, seg, n, slot):
        sp.wait_ge(self.sig("tiles_used").sem, n + (seg.first + 1))
        sp.dma_start(self.ring[:, slot, :], seg.tiles[n]).then_inc(self.sig(f"slot{slot}_loaded").sem, 16)

    def first_tiles(self, sp, k):
        if k < len(self.segments):
            for slot in range(RING):
                self.load_tile(sp, self.segments[k], slot, slot)

    def stream(self, sp, seg, k):
        if seg.count > RING:
            with sp.Fori(1, seg.count // RING) as g:
                for slot in range(RING):
                    self.load_tile(sp, seg, g * RING + slot, slot)
        self.first_tiles(sp, k + 1)

    def take_segment(self):
        k = self.next_segment
        self.next_segment += 1
        return self.segments[k], k

    def wait_tile(self, pe, seg, n, slot):
        pe.wait_ge(self.sig(f"slot{slot}_loaded").sem, n * (16 // RING) + 16 * (seg.first // RING + 1))

    def norm(self, src, dst, gain, shift, squares):
        nc, sig = self.nc, self.sig
        squared, summed, rooted, scaled, step = (sig(n) for n in ("squared", "square_sums", "rooted", "scaled", "dve_step"))
        sums = self.bank[4][:, 0:T]
        root = self.work[:, 0:T]
        with nc.Block() as block:
            @block.vector
            def _(dve):
                link = Chain(step, dve)
                for half in range(2):
                    s = slice(half * KB // 2, (half + 1) * KB // 2)
                    nc.vector.tensor_tensor(squares[:, s], src[:, s], src[:, s], ALU.mult).then_inc(squared.sem, 1)
                dve.wait_ge(rooted.sem, rooted.at(1))
                link(nc.vector.reciprocal(root, root))
                for k in range(KB):
                    nc.vector.scalar_tensor_tensor(out=dst[:, k, :], in0=src[:, k, :], scalar=gain[:, k:k + 1], in1=root,
                                                   op0=ALU.mult, op1=ALU.mult).then_inc(scaled.sem, 1)
                step.used = link.n

            @block.tensor
            def _(pe):
                for k in range(KB):
                    if k % (KB // 2) == 0:
                        pe.wait_ge(squared.sem, squared.at(k // (KB // 2) + 1))
                    mm = nc.tensor.matmul(sums, self.c("ones"), squares[:, k, :], start=(k == 0), stop=(k == KB - 1))
                mm.then_inc(summed.sem, 1)

            @block.scalar
            def _(act):
                act.wait_ge(summed.sem, summed.at(1))
                nc.scalar.activation(root, sums, ACT.Sqrt, bias=self.c("eps"), scale=1.0 / D).then_inc(rooted.sem, 1)
                if shift is not None:
                    for k in range(KB):
                        act.wait_ge(scaled.sem, scaled.at(k + 1))
                        nc.scalar.activation(dst[:, k, :], dst[:, k, :], ACT.Identity, bias=shift[:, k:k + 1])
        step.close(step.used)
        for s, n in ((squared, 2), (summed, 1), (rooted, 1), (scaled, KB)):
            s.close(n)

    def linear(self, rhs, engine, parts, groups=1):
        nc, sig = self.nc, self.sig
        free, used = sig("bank_free"), sig("tiles_used")
        seg, k = self.take_segment()
        blocks = seg.count // groups
        with nc.Block() as block:
            @block.sync
            def _(sp):
                self.stream(sp, seg, k)

            @block.tensor
            def _(pe):
                with pe.Fori(0, blocks // RING) as turn:
                    for b in range(RING):
                        pe.wait_ge(free.sem, turn * RING + free.at(b + 1 - RING))
                        for g in range(groups):
                            slot = (b * groups + g) % RING
                            tile = turn * (RING * groups) + (b * groups + g - slot)
                            self.wait_tile(pe, seg, tile, slot)
                            for c in range(KB):
                                mm = nc.tensor.matmul(self.bank[b][:, 0:T], self.ring[:, slot, c * P:(c + 1) * P],
                                                      rhs[:, g * KB + c, :], start=(g + c == 0),
                                                      stop=(g == groups - 1 and c == KB - 1))
                            mm.then_inc(used.sem, 1)

            def take_out(eng):
                for first, count, fn in parts:
                    with eng.Fori(first // RING, (first + count) // RING) as turn:
                        for b in range(RING):
                            eng.wait_ge(used.sem, turn * (RING * groups) + (seg.first + RING + (b + 1) * groups))
                            fn(turn * RING + b, self.bank[b][:, 0:T]).then_inc(free.sem, 1)

            if engine == "scalar":
                block.scalar(take_out)
            else:
                block.vector(take_out)
        free.close(blocks)

    def copy_to(self, dst, func=ACT.Identity, offset=0):
        return lambda n, bank: self.nc.scalar.activation(dst[:, n + offset, :], bank, func)

    def add_to_x(self, gate=None):
        def fn(n, bank):
            x = self.x[:, n, :]
            if gate is None:
                return self.nc.vector.tensor_tensor(x, bank, x, ALU.add)
            return self.nc.vector.scalar_tensor_tensor(out=x, in0=bank, scalar=gate(n), in1=x, op0=ALU.mult, op1=ALU.add)
        return fn

    def load(self, eng, pairs):
        loaded = self.sig("small_loaded")
        for dst, name in pairs:
            eng.dma_start(dst, self.dram[name]).then_inc(loaded.sem, 16)
        eng.wait_ge(loaded.sem, loaded.at(16 * len(pairs)))
        return 16 * len(pairs)


def setup(core):
    nc, sig = core.nc, core.sig
    loaded, step, sined = sig("small_loaded"), sig("dve_step"), sig("angles_ready")
    pos = core.work[:, 0:2 * T].bitcast(I32)
    pos_f = view(core.work, 2 * T, 2, T)
    turns = core.work[:, 4 * T:5 * T]
    angle = view(core.work, 5 * T, 4, T)
    n = [0]
    with nc.Block() as block:
        @block.sync
        def _(sp):
            core.first_tiles(sp, 0)

        @block.scalar
        def _(act):
            n[0] = core.load(act, [(core.const[:], "resident"), (core.cols[:], "cols"), (pos, "positions")] +
                             [(core.x[:], "x")])
            nc.scalar.activation(core.gain[:, 0, :], core.col("c"), ACT.Silu)
            act.wait_ge(sined.sem, sined.at(1))
            nc.scalar.activation(core.trig[:], angle, ACT.Sin)

        @block.vector
        def _(dve):
            link = Chain(step, dve)
            nc.vector.memset(core.work[:, 9 * T:9 * T + 1], 0.0).then_inc(sig("bank_free").sem, RING)
            nc.vector.memset(core.work[:, 12 * T:12 * T + 1], 0.0).then_inc(sig("gates_taken").sem, 2)
            nc.vector.memset(core.work[:, 13 * T:13 * T + 1], 0.0).then_inc(sig("gates_spread").sem, 2)
            nc.vector.memset(core.work[:, 10 * T:10 * T + 1], 0.0).then_inc(sig("tiles_used").sem, RING)
            dve.wait_ge(loaded.sem, loaded.at(16 * 4))
            link(nc.vector.tensor_copy(pos_f, pos.rearrange("p (n t) -> p n t", n=2)))
            for which, freq in enumerate(("inv_freq_a", "inv_freq_b")):
                for quarter in range(2):
                    out = angle[:, 2 * which + quarter, :]
                    link(nc.vector.tensor_scalar(out, pos_f[:, which, :], core.c(freq), None, ALU.mult))
                    link(nc.vector.tensor_scalar(turns, out, 1.0 / (2 * math.pi), 0.25 * quarter, ALU.mult, ALU.add))
                    link(nc.vector.tensor_scalar(turns, turns, ROUND, None, ALU.add))
                    link(nc.vector.tensor_scalar(turns, turns, ROUND, None, ALU.subtract))
                    high = 6.28125
                    mid = float(np.float32(np.round((2 * math.pi - high) * 2 ** 20) / 2 ** 20))
                    low = 2 * math.pi - high - mid
                    for part in (high, mid, low):
                        link(nc.vector.scalar_tensor_tensor(out=out, in0=turns, scalar=-part, in1=out,
                                                            op0=ALU.mult, op1=ALU.add))
                    if quarter:
                        link(nc.vector.tensor_scalar(out, out, math.pi / 2, None, ALU.add))
                    link(nc.vector.tensor_scalar(out, out, 3.1415925, -3.1415925, ALU.min, ALU.max))
            nc.vector.memset(core.work[:, 11 * T:11 * T + 1], 0.0).then_inc(sined.sem, 1)
            step.used = link.n
    step.close(step.used)
    sined.close(1)
    loaded.close(n[0])
    sig("bank_free").close(RING)


def modulation(core, layer):
    nc, sig = core.nc, core.sig
    used, step, silu_kept = sig("tiles_used"), sig("dve_step"), sig("silu_kept")
    seg, k = core.take_segment()
    silu = core.work[:, 4000:4000 + KB]
    out = core.bank[4]
    mod = core.mod[:, layer, :]
    with nc.Block() as block:
        @block.sync
        def _(sp):
            core.stream(sp, seg, k)

        @block.scalar
        def _(act):
            nc.scalar.activation(silu, core.col("c"), ACT.Silu).then_inc(silu_kept.sem, 1)

        @block.tensor
        def _(pe):
            pe.wait_ge(silu_kept.sem, silu_kept.at(1))
            with pe.Fori(0, seg.count // RING) as turn:
                for slot in range(RING):
                    core.wait_tile(pe, seg, turn * RING, slot)
                    for c in range(KB):
                        mm = nc.tensor.matmul(out[:, bass.ds(turn * RING + slot, 1)], core.ring[:, slot, c * P:(c + 1) * P],
                                              silu[:, c:c + 1], start=(c == 0), stop=(c == KB - 1))
                    mm.then_inc(used.sem, 1)

        @block.vector
        def _(dve):
            link = Chain(step, dve)
            dve.wait_ge(used.sem, seg.first + RING + seg.count)
            link(nc.vector.tensor_tensor(mod, out[:, 0:48], core.col(f"ada_b{layer}"), ALU.add))
            for which, name in enumerate(("norm_mix", "norm_ffn")):
                scale = mod[:, (3 * which + 1) * KB:(3 * which + 2) * KB]
                link(nc.vector.scalar_tensor_tensor(out=core.gain[:, 2 * layer + which, :], in0=scale, scalar=1.0,
                                                    in1=core.col(f"{name}{layer}"), op0=ALU.add, op1=ALU.mult))
            step.used = link.n
    step.close(step.used)
    silu_kept.close(1)


def transposes(core, pe, src, dst_banks, raised):
    for n, block in enumerate(src):
        mm = core.nc.tensor.transpose(dst_banks[n // 4][:, (n % 4) * P:(n % 4 + 1) * P], block, core.c("ident"))
        if n % 4 == 3 or n == len(src) - 1:
            mm.then_inc(raised.sem, 1)


def token_major(core, jobs):
    nc, sig = core.nc, core.sig
    turned, kept = sig("turned"), sig("turned_kept")
    groups = []
    for src, dst in jobs:
        blocks = src.shape[1]
        for t in range(TT):
            for b in range(0, blocks, 4):
                groups.append((src, dst, t, b))
    with nc.Block() as block:
        @block.tensor
        def _(pe):
            for n, (src, dst, t, b) in enumerate(groups):
                if n >= 4:
                    pe.wait_ge(kept.sem, kept.at(n - 3))
                transposes(core, pe, [src[:, b + i, t * P:(t + 1) * P] for i in range(4)], [core.bank[n % 4]], turned)

        @block.scalar
        def _(act):
            for n, (src, dst, t, b) in enumerate(groups):
                act.wait_ge(turned.sem, turned.at(n + 1))
                nc.scalar.activation(dst[:, t, b * P:(b + 4) * P], core.bank[n % 4][:], ACT.Identity).then_inc(kept.sem, 1)
    turned.close(len(groups))
    kept.close(len(groups))


def even_mixer(core):
    nc, sig, A = core.nc, core.sig, core.arena
    proj = view(A, 2048, 12, T)
    core.linear(core.h, "scalar", [(0, 8, core.copy_to(proj, ACT.Gelu)), (8, 4, core.copy_to(proj))])
    u, v, p = proj[:, 0:4], proj[:, 4:8], proj[:, 8:12]
    centred, squares, tokens = view(A, 5120, 4, T), view(A, 6144, 4, T), view(A, 7168, 2, 4 * P)
    spatial, bias = view(A, 8192, 4, P), view(A, 8704, 4, P)
    ping, pong = view(A, 9216, 4, T + 16), view(A, 10304, 4, T + 16)
    pooled, inv_count, w_pool = view(A, 11392, 4, T), A[:, 12416:13440], view(A, 13440, 4, P)
    mask, cat = A[:, 13952:14080], view(A, 14336, 8, T)
    step, loaded = sig("dve_step"), sig("small_loaded")
    n = [0]
    mean, var = core.bank[4][:, 0:T], core.bank[5][:, 0:T]
    means, cent, vars_, rooted = sig("mean_ready"), sig("centred_squared"), sig("variance_ready"), sig("rooted")
    wide = [P, 4, T]
    root = core.work[:, 0:T]
    with nc.Block() as block:
        @block.sync
        def _(sp):
            n[0] = core.load(sp, [(spatial, "ev_w_s"), (bias, "ev_b_s"), (inv_count, "inv_count"),
                                    (w_pool, "ev_w_pool"), (mask, "even_mask")])

        @block.tensor
        def _(pe):
            for g in range(4):
                mm = nc.tensor.matmul(mean, core.c("ones"), v[:, g, :], start=(g == 0), stop=(g == 3))
            mm.then_inc(means.sem, 1)
            pe.wait_ge(cent.sem, cent.at(1))
            for g in range(4):
                mm = nc.tensor.matmul(var, core.c("ones"), squares[:, g, :], start=(g == 0), stop=(g == 3))
            mm.then_inc(vars_.sem, 1)

        @block.scalar
        def _(act):
            act.wait_ge(vars_.sem, vars_.at(1))
            nc.scalar.activation(root, var, ACT.Sqrt, bias=core.c("eps"), scale=1.0 / 512).then_inc(rooted.sem, 1)

        @block.vector
        def _(dve):
            link = Chain(step, dve)
            dve.wait_ge(means.sem, means.at(1))
            link(nc.vector.scalar_tensor_tensor(out=centred, in0=mean.unsqueeze(1).to_broadcast(wide), scalar=-1.0 / 512,
                                                in1=v, op0=ALU.mult, op1=ALU.add))
            nc.vector.tensor_tensor(squares, centred, centred, ALU.mult).then_inc(cent.sem, 1)
            link(nc.vector.memset(ping[:, :, 0:16], 0.0))
            link(nc.vector.memset(pong[:, :, 0:16], 0.0))
            link(nc.vector.tensor_copy(ping[:, :, 16:], p))
            src, dst = ping, pong
            for g in range(4):
                shift = 1 << g
                link(nc.vector.tensor_tensor(dst[:, g:4, 16:], src[:, g:4, 16:], src[:, g:4, 16 - shift:16 - shift + T], ALU.add))
                link(nc.vector.tensor_tensor(pooled[:, g, :], dst[:, g, 16:], dst[:, g, 16:], ALU.max))
                src, dst = dst, src
            dve.wait_ge(loaded.sem, loaded.at(16 * 5))
            link(nc.vector.tensor_tensor(pooled, pooled, inv_count.rearrange("p (g t) -> p g t", g=4), ALU.mult))
            link(nc.vector.tensor_tensor(pooled, pooled, p, ALU.subtract))
            link(nc.vector.tensor_tensor(spatial, spatial, mask.unsqueeze(1).to_broadcast([P, 4, P]), ALU.mult))
            dve.wait_ge(rooted.sem, rooted.at(1))
            link(nc.vector.reciprocal(root, root))
            link(nc.vector.tensor_tensor(centred, centred, root.unsqueeze(1).to_broadcast(wide), ALU.mult))
            step.used = link.n
    step.close(step.used)
    for s in (means, cent, vars_, rooted):
        s.close(1)
    loaded.close(n[0])
    token_major(core, [(centred, tokens)])
    mixed, pools = sig("spatial_mixed"), sig("pool_mixed")
    with nc.Block() as block:
        @block.tensor
        def _(pe):
            for t in range(TT):
                for g in range(4):
                    mm = nc.tensor.matmul(core.bank[t][:, g * P:(g + 1) * P], tokens[:, t, g * P:(g + 1) * P],
                                          spatial[:, g, :], start=True, stop=True)
                mm.then_inc(mixed.sem, 1)
            for g in range(4):
                mm = nc.tensor.matmul(core.bank[4 + g][:, 0:T], w_pool[:, g, :], pooled[:, g, :], start=True, stop=True)
                mm.then_inc(pools.sem, 1)

        @block.vector
        def _(dve):
            link = Chain(step, dve)
            for t in range(TT):
                dve.wait_ge(mixed.sem, mixed.at(t + 1))
                for g in range(4):
                    nc.vector.scalar_tensor_tensor(out=cat[:, g, t * P:(t + 1) * P], in0=core.bank[t][:, g * P:(g + 1) * P],
                                                   scalar=core.col("ev_g_v", g), in1=bias[:, g, :], op0=ALU.mult, op1=ALU.add)
            link(nc.vector.memset(core.work[:, 300:301], 0.0))
            nc.vector.tensor_tensor(cat[:, 0:4], cat[:, 0:4], u, ALU.mult)
            step.used = link.n

        @block.scalar
        def _(act):
            for g in range(4):
                act.wait_ge(pools.sem, pools.at(g + 1))
                nc.scalar.activation(cat[:, 4 + g, :], core.bank[4 + g][:, 0:T], ACT.Identity, scale=core.col("ev_pool_scale", g))
    step.close(step.used)
    mixed.close(TT)
    pools.close(4)
    core.linear(cat, "vector", [(0, 8, core.add_to_x(lambda n: core.mod[:, 0, bass.ds(n + 2 * KB, 1)]))])


def mixer_norm(core, layer):
    core.norm(core.x, core.h, core.gain[:, 2 * layer, :], core.mod[:, layer, 0:KB], view(core.arena, 0, 8, T))


def ffn_norm(core, layer):
    core.norm(core.x, core.h, core.gain[:, 2 * layer + 1, :], core.mod[:, layer, 3 * KB:4 * KB], view(core.arena, 0, 8, T))



def peer_queries(core, layer):
    nc, sig, A = core.nc, core.sig, core.arena
    queries, keys = view(A, 0, 16, T), view(A, 4096, 16, KEYS)
    core.linear(core.h, "scalar", [(0, 16, core.copy_to(queries))])
    scored, kept, loaded = sig("keys_scored"), sig("key_scores_kept"), sig("small_loaded")
    n = [0]
    with nc.Block() as block:
        @block.sync
        def _(sp):
            n[0] = core.load(sp, [(A[:, 4096:4096 + 16 * KEYS], f"peer_keys{layer}")])

        @block.tensor
        def _(pe):
            pe.wait_ge(loaded.sem, loaded.at(16))
            for g in range(TT * 4):
                t, first = g // 4, (g % 4) * 4
                if g >= 4:
                    pe.wait_ge(kept.sem, kept.at(g - 3))
                for q in range(4):
                    mm = nc.tensor.matmul(core.bank[g % 4][:, q * KEYS:(q + 1) * KEYS],
                                          queries[:, first + q, t * P:(t + 1) * P], keys[:, first + q, :],
                                          start=True, stop=True)
                mm.then_inc(scored.sem, 1)

        @block.scalar
        def _(act):
            for g in range(TT * 4):
                act.wait_ge(scored.sem, scored.at(g + 1))
                nc.scalar.activation(core.work[:, g * BANK:(g + 1) * BANK], core.bank[g % 4][:], ACT.Identity) \
                    .then_inc(kept.sem, 1)
    loaded.close(n[0])
    scored.close(8)
    kept.close(8)


def peer_scores(core, layer):
    nc, sig = core.nc, core.sig
    used, free, step = sig("tiles_used"), sig("bank_free"), sig("dve_step")
    seg, k = core.take_segment()
    acts = view(core.arena, 0, P, T)
    scores = core.work[:].rearrange("p (t h s n) -> p t h s n", t=TT, h=HEADS, s=2)
    b = core.pick
    sums = lambda t: b.sums[:, t].rearrange("p a b -> p (a b)")
    sums_rest = lambda t: b.sums_rest[:, t].rearrange("p a b -> p (a b)")
    with nc.Block() as block:
        @block.sync
        def _(sp):
            core.stream(sp, seg, k)

        @block.tensor
        def _(pe):
            with pe.Fori(0, P // RING) as turn:
                for slot in range(RING):
                    pe.wait_ge(free.sem, turn * RING + free.at(slot + 1 - RING))
                    core.wait_tile(pe, seg, turn * RING, slot)
                    for c in range(KB):
                        mm = nc.tensor.matmul(core.bank[slot][:, 0:T], core.ring[:, slot, c * P:(c + 1) * P],
                                              core.h[:, c, :], start=(c == 0), stop=(c == KB - 1))
                    mm.then_inc(used.sem, 1)

        @block.scalar
        def _(act):
            with act.Fori(0, P // RING) as turn:
                for slot in range(RING):
                    act.wait_ge(used.sem, turn * RING + (seg.first + RING + slot + 1))
                    nc.scalar.activation(acts[:, turn * RING + slot, :], core.bank[slot][:, 0:T], ACT.Gelu).then_inc(free.sem, 1)

        @block.vector
        def _(dve):
            link = Chain(step, dve)
            for h in range(HEADS):
                sets = [(t, s) for t in range(TT) for s in range(2)]
                link(nc.vector.tensor_copy(b.keys[:].rearrange("p t s n -> p (t s) n"),
                                           scores[:, :, h, :, :].rearrange("p t s n -> p t s n")))
                for t, s in sets:
                    i = nc.vector.max(b.top[:, t, s, 0:8], b.keys[:, t, s, :])
                link(i)
                for t, s in sets:
                    nc.vector.max_index(b.at[:, t, s, 0:8], b.top[:, t, s, 0:8], b.keys[:, t, s, :])
                    i = nc.vector.match_replace(b.rest[:, t, s, :], b.top[:, t, s, 0:8], b.keys[:, t, s, :], LOWEST)
                link(i)
                for t, s in sets:
                    i = nc.vector.max(b.top[:, t, s, 8:16], b.rest[:, t, s, :])
                link(i)
                for t, s in sets:
                    i = nc.vector.max_index(b.at[:, t, s, 8:16], b.top[:, t, s, 8:16], b.rest[:, t, s, :])
                link(i)
                nc.vector.tensor_copy(b.at_f[:], b.at[:])
                for t in range(TT):
                    i = nc.vector.tensor_tensor(b.sums[:, t], b.top[:, t, 0, :].unsqueeze(2).to_broadcast([P, 16, 16]),
                                                b.top[:, t, 1, :].unsqueeze(1).to_broadcast([P, 16, 16]), ALU.add)
                link(i)
                for t in range(TT):
                    i = nc.vector.max(b.best[:, t, 0:8], sums(t))
                link(i)
                for t in range(TT):
                    nc.vector.max_index(b.place[:, t, 0:8], b.best[:, t, 0:8], sums(t))
                    i = nc.vector.match_replace(sums_rest(t), b.best[:, t, 0:8], sums(t), LOWEST)
                link(i)
                for t in range(TT):
                    i = nc.vector.max(b.best[:, t, 8:16], sums_rest(t))
                link(i)
                for t in range(TT):
                    i = nc.vector.max_index(b.place[:, t, 8:16], b.best[:, t, 8:16], sums_rest(t))
                link(i)
                nc.vector.tensor_scalar(b.digit[:, 0], b.place[:], 4, None, ALU.logical_shift_right)
                link(nc.vector.tensor_scalar(b.digit[:, 1], b.place[:], 15, None, ALU.bitwise_and))
                link(nc.vector.tensor_copy(b.digit_f[:], b.digit[:]))
                iota = core.c("iota16").unsqueeze(1).to_broadcast([P, 16, 16])
                for s in range(2):
                    for t in range(TT):
                        i = nc.vector.tensor_tensor(b.onehot[:, t], b.digit_f[:, s, t, :].unsqueeze(2).to_broadcast([P, 16, 16]),
                                                    iota, ALU.is_equal)
                    link(i)
                    for t in range(TT):
                        i = nc.vector.tensor_tensor(b.onehot[:, t], b.onehot[:, t],
                                                    b.at_f[:, t, s, :].unsqueeze(1).to_broadcast([P, 16, 16]), ALU.mult)
                    link(i)
                    for t in range(TT):
                        i = nc.vector.tensor_reduce(b.chosen[:, s, t, h * TOPK:(h + 1) * TOPK], b.onehot[:, t], AX_X, ALU.add)
                    link(i)
                i = nc.vector.tensor_tensor(b.expo[:, :, h, :], b.best[:], b.best[:, :, 0:1].to_broadcast([P, TT, 16]), ALU.subtract)
                link(i)
            step.used = link.n
    step.close(step.used)
    free.close(P)


def peer_gates(core, layer):
    nc, sig, b = core.nc, core.sig, core.pick
    exped, gated, turned, step = sig("gates_exped"), sig("gates_ready"), sig("turned"), sig("dve_step")
    gates = b.expo[:].rearrange("p t h k -> p (t h) k")
    total = b.total[:]
    with nc.Block() as block:
        @block.scalar
        def _(act):
            nc.scalar.activation(b.expo[:], b.expo[:], ACT.Exp).then_inc(exped.sem, 1)

        @block.vector
        def _(dve):
            link = Chain(step, dve)
            dve.wait_ge(exped.sem, exped.at(1))
            link(nc.vector.tensor_reduce(total, gates, AX_X, ALU.add))
            link(nc.vector.reciprocal(total, total))
            nc.vector.tensor_tensor(gates, gates, total.unsqueeze(2).to_broadcast([P, TT * HEADS, TOPK]), ALU.mult) \
                .then_inc(gated.sem, 1)
            step.used = link.n
            for n in range(3):
                dve.wait_ge(turned.sem, turned.at(n + 1))
                nc.vector.tensor_copy(b.by_pick[:, n, :], core.bank[n][:, 0:T])

        @block.tensor
        def _(pe):
            for n in range(3):
                if n == 2:
                    pe.wait_ge(gated.sem, gated.at(1))
                    src = [b.expo[:, t].rearrange("p h k -> p (h k)") for t in range(TT)]
                else:
                    src = [b.chosen[:, n, t, :] for t in range(TT)]
                transposes(core, pe, src, [core.bank[n]], turned)
    step.close(step.used)
    turned.close(3)
    exped.close(1)
    gated.close(1)


def peer_weigh(core, layer):
    nc, sig, b = core.nc, core.sig, core.pick
    onehots, spread, taken = sig("onehots_ready"), sig("gates_spread"), sig("gates_taken")
    acts = view(core.arena, 0, P, T)
    first, second, gate = (b.by_pick[:, n, :] for n in range(3))
    hot = view(core.work, 0, 16, P)
    iota = core.c("iota")
    turns = T // 8
    with nc.Block() as block:
        @block.vector
        def _(dve):
            with dve.Fori(0, turns) as turn:
                for g in range(2):
                    dve.wait_ge(spread.sem, turn * 2 + spread.at(g + 1))
                    for u in range(4):
                        token = turn * 8 + 4 * g + u
                        nc.vector.tensor_scalar(hot[:, 4 * g + u, :], iota, first[:, bass.ds(token, 1)], None, ALU.is_equal)
                        i = nc.vector.tensor_scalar(hot[:, 8 + 4 * g + u, :], iota, second[:, bass.ds(token, 1)],
                                                    gate[:, bass.ds(token, 1)], ALU.is_equal, ALU.mult)
                    i.then_inc(onehots.sem, 1)
                for g in range(2):
                    dve.wait_ge(spread.sem, turn * 2 + spread.at(g + 3))
                    part = acts[:, :, bass.ds(turn * 8 + 4 * g, 4)]
                    nc.vector.tensor_tensor(part, part, core.bank[g][:].rearrange("p (u i) -> p i u", u=4), ALU.mult) \
                        .then_inc(taken.sem, 1)

        @block.tensor
        def _(pe):
            with pe.Fori(0, turns) as turn:
                for g in range(2):
                    pe.wait_ge(onehots.sem, turn * 2 + onehots.at(g + 1))
                    pe.wait_ge(taken.sem, turn * 2 + taken.at(g + 1))
                    for u in range(4):
                        mm = nc.tensor.matmul(core.bank[g][:, u * P:(u + 1) * P], hot[:, 8 + 4 * g + u, :],
                                              hot[:, 4 * g + u, :], start=True, stop=True)
                    mm.then_inc(spread.sem, 1)
    for s in (onehots, spread, taken):
        s.close(2 * turns)


def peer_output(core, layer):
    nc, sig = core.nc, core.sig
    used, summed, step = sig("tiles_used"), sig("experts_summed"), sig("dve_step")
    seg, k = core.take_segment()
    acts = view(core.arena, 0, P, T)
    out = [core.bank[4 + d // 2][:, (d % 2) * T:(d % 2 + 1) * T] for d in range(KB)]
    with nc.Block() as block:
        @block.sync
        def _(sp):
            core.stream(sp, seg, k)

        @block.tensor
        def _(pe):
            for d in range(4):
                nc.tensor.matmul(core.bank[4 + d][:], core.c("zeros"), core.h[:, 0:2, :], start=True, stop=False,
                                 skip_group_check=True)
            with pe.Fori(0, P // RING) as turn:
                for slot in range(RING):
                    core.wait_tile(pe, seg, turn * RING, slot)
                    for d in range(KB):
                        mm = nc.tensor.matmul(out[d], core.ring[:, slot, d * P:(d + 1) * P],
                                              acts[:, turn * RING + slot, :], start=False, stop=False, skip_group_check=True)
                    mm.then_inc(used.sem, 1)
            for d in range(4):
                mm = nc.tensor.matmul(core.bank[4 + d][:], core.c("zeros"), core.h[:, 0:2, :], start=False, stop=True,
                                      skip_group_check=True)
            mm.then_inc(summed.sem, 1)

        @block.vector
        def _(dve):
            dve.wait_ge(summed.sem, summed.at(1))
            for d in range(KB):
                core.add_to_x(lambda n: core.mod[:, layer, 5 * KB + n:5 * KB + n + 1])(d, out[d])
    summed.close(1)


def peer(core, layer):
    ffn_norm(core, layer)
    peer_queries(core, layer)
    peer_scores(core, layer)
    peer_gates(core, layer)
    peer_weigh(core, layer)
    peer_output(core, layer)


def rope(core, src, dst, pairs, cos, sin):
    nc, sig = core.nc, core.sig
    swapped, taken, straight = sig("halves_swapped"), sig("halves_taken"), sig("straight_ready")
    step = sig("dve_step")
    two = [P, 2, T]
    cosb, sinb = (a.unsqueeze(1).to_broadcast(two) for a in (cos, sin))
    side = core.work[:, 0:4 * BANK].rearrange("p (b n t) -> p b n t", b=4, n=2)
    with nc.Block() as block:
        @block.tensor
        def _(pe):
            for n in range(pairs):
                if n >= 4:
                    pe.wait_ge(taken.sem, taken.at(n - 3))
                nc.tensor.matmul(core.bank[n % 4][:], core.c("rot"), src[:, 2 * n:2 * n + 2, :], start=True, stop=True) \
                    .then_inc(swapped.sem, 1)

        @block.gpsimd
        def _(pool):
            for n in range(pairs):
                nc.gpsimd.tensor_tensor(dst[:, 2 * n:2 * n + 2, :], src[:, 2 * n:2 * n + 2, :], cosb, ALU.mult) \
                    .then_inc(straight.sem, 1)

        @block.vector
        def _(dve):
            link = Chain(step, dve)
            for n in range(pairs):
                dve.wait_ge(swapped.sem, swapped.at(n + 1))
                i = nc.vector.tensor_tensor(side[:, n % 4], core.bank[n % 4][:].rearrange("p (n t) -> p n t", n=2), sinb, ALU.mult)
                i.then_inc(taken.sem, 1)
                dve.wait_ge(taken.sem, taken.at(n + 1))
                dve.wait_ge(straight.sem, straight.at(n + 1))
                part = dst[:, 2 * n:2 * n + 2, :]
                nc.vector.tensor_tensor(part, part, side[:, n % 4], ALU.add)
            step.used = link.n
    step.close(step.used)
    for s in (swapped, taken, straight):
        s.close(pairs)


def block_rms(core, src, blocks, ones, count, eps, squares, root, centre=None):
    nc, sig = core.nc, core.sig
    step, meaned, squared, summed, rooted = (sig(n) for n in ("dve_step", "mean_ready", "squared", "square_sums", "rooted"))
    flat = lambda a: a.rearrange("p n t -> p (n t)")
    banks = blocks // 2
    src_f, squares_f, root_f = flat(src), flat(squares), flat(root)
    with nc.Block() as block:
        @block.tensor
        def _(pe):
            if centre is not None:
                for n in range(banks):
                    nc.tensor.matmul(core.bank[n][:], core.c(ones), src_f[:, n * BANK:(n + 1) * BANK], start=True, stop=True) \
                        .then_inc(meaned.sem, 1)
            for n in range(banks):
                pe.wait_ge(squared.sem, squared.at(n + 1))
                nc.tensor.matmul(core.bank[4 + n][:], core.c(ones), squares_f[:, n * BANK:(n + 1) * BANK], start=True, stop=True) \
                    .then_inc(summed.sem, 1)

        @block.scalar
        def _(act):
            for n in range(banks):
                act.wait_ge(summed.sem, summed.at(n + 1))
                nc.scalar.activation(root_f[:, n * BANK:(n + 1) * BANK], core.bank[4 + n][:], ACT.Sqrt, bias=eps,
                                     scale=1.0 / count).then_inc(rooted.sem, 1)

        @block.vector
        def _(dve):
            link = Chain(step, dve)
            for n in range(banks):
                part = slice(n * BANK, (n + 1) * BANK)
                if centre is not None:
                    dve.wait_ge(meaned.sem, meaned.at(n + 1))
                    link(nc.vector.scalar_tensor_tensor(out=flat(centre)[:, part], in0=core.bank[n][:], scalar=-1.0 / count,
                                                        in1=src_f[:, part], op0=ALU.mult, op1=ALU.add))
                    nc.vector.tensor_tensor(squares_f[:, part], flat(centre)[:, part], flat(centre)[:, part], ALU.mult) \
                        .then_inc(squared.sem, 1)
                else:
                    nc.vector.tensor_tensor(squares_f[:, part], src_f[:, part], src_f[:, part], ALU.mult).then_inc(squared.sem, 1)
            for n in range(banks):
                part = slice(n * BANK, (n + 1) * BANK)
                dve.wait_ge(rooted.sem, rooted.at(n + 1))
                nc.vector.reciprocal(root_f[:, part], root_f[:, part])
            step.used = link.n
    step.close(step.used)
    meaned.close(banks if centre is not None else 0)
    for s in (squared, summed, rooted):
        s.close(banks)


def odd_mixer(core):
    nc, sig, A = core.nc, core.sig, core.arena
    proj, turned, tokens, o = view(A, 0, 24, T), view(A, 6144, 16, T), view(A, 10240, 2, 8 * P), view(A, 12288, 8, T)
    squares, root = view(A, 14336, 8, T), view(A, 16384, 8, T)
    mask = A[:, 18432:18432 + 384]
    probs = A[:, 18816:18816 + 2 * 768].rearrange("p (b m k) -> p b m k", b=2, m=2)
    combined, combined_T = view(A, 20352, 2, 384), view(A, 21120, 2, 384)
    lam = A[:, 21888:21888 + 256].rearrange("p (n d) -> p n d", n=4)
    peak, total, minus_lam = A[:, 22144:22152], A[:, 22152:22160], A[:, 22160:22164]
    product, gain = A[:, 22164:22164 + 64], A[:, 22228:22229]
    core.linear(core.h, "scalar", [(0, 24, core.copy_to(proj))])
    rope(core, proj[:, 0:16], turned, 8, core.trig[:, 1, :], core.trig[:, 0, :])
    token_major(core, [(proj[:, 16:24], tokens)])

    step, loaded, act_step = sig("dve_step"), sig("small_loaded"), sig("lam_exped")
    n = [0]
    with nc.Block() as block:
        @block.sync
        def _(sp):
            n[0] = core.load(sp, [(mask, "attn_mask"), (lam, "od_lam")])

        @block.vector
        def _(dve):
            link = Chain(step, dve)
            dve.wait_ge(loaded.sem, loaded.at(32))
            for i in range(2):
                link(nc.vector.tensor_tensor(product, lam[:, 2 * i], lam[:, 2 * i + 1], ALU.mult))
                link(nc.vector.tensor_reduce(minus_lam[:, i:i + 1], product, AX_X, ALU.add))
            nc.vector.tensor_scalar(gain, core.col("od_g_sub"), 1.0 - LAM_INIT, None, ALU.mult).then_inc(sig("lam_summed").sem, 1)
            dve.wait_ge(act_step.sem, act_step.at(1))
            link(nc.vector.tensor_tensor(minus_lam[:, 3:4], minus_lam[:, 1:2], minus_lam[:, 0:1], ALU.subtract))
            link(nc.vector.tensor_scalar(minus_lam[:, 3:4], minus_lam[:, 3:4], LAM_INIT, None, ALU.subtract))
            step.used = link.n

        @block.scalar
        def _(act):
            act.wait_ge(sig("lam_summed").sem, sig("lam_summed").at(1))
            nc.scalar.activation(minus_lam[:, 0:2], minus_lam[:, 0:2], ACT.Exp).then_inc(act_step.sem, 1)
    step.close(step.used)
    loaded.close(n[0])
    act_step.close(1)
    sig("lam_summed").close(1)

    scored, peaked, exped, weighed, flipped, kept, mixed = (sig(x) for x in (
        "heads_scored", "heads_peaked", "heads_exped", "heads_weighed", "heads_flipped", "flips_kept", "heads_mixed"))
    scored_taken, mixed_taken = sig("scores_taken"), sig("mixed_taken")
    sums = lambda m, i: total[:, 2 * i + m:2 * i + m + 1]
    minus_peak = lambda m, i: peak[:, 2 * i + m:2 * i + m + 1]
    span = (slice(0, P), slice(P, 3 * P))
    with nc.Block() as block:
        @block.tensor
        def _(pe):
            def scores(h):
                if h >= 2:
                    pe.wait_ge(scored_taken.sem, scored_taken.at(h - 1))
                for m in range(2):
                    half = slice(64 * m, 64 * m + 64)
                    for i in range(2):
                        mm = nc.tensor.matmul(core.bank[2 * (h % 2) + m][:, span[i]], turned[half, h, i * P:(i + 1) * P],
                                              turned[half, 8 + h, 0:(i + 1) * P], start=True, stop=True)
                mm.then_inc(scored.sem, 1)

            scores(0)
            for h in range(HEADS):
                if h + 1 < HEADS:
                    scores(h + 1)
                pe.wait_ge(weighed.sem, weighed.at(h + 1))
                if h >= 2:
                    pe.wait_ge(kept.sem, kept.at(h - 1))
                w = combined[:, h % 2, :]
                flips = core.bank[4 + h % 2]
                for c, at in ((0, 0), (1, 1), (2, 2)):
                    mm = nc.tensor.transpose(flips[:, at * P:(at + 1) * P], w[:, c * P:(c + 1) * P], core.c("ident"))
                mm.then_inc(flipped.sem, 1)
                pe.wait_ge(kept.sem, kept.at(h + 1))
                if h >= 2:
                    pe.wait_ge(mixed_taken.sem, mixed_taken.at(h - 1))
                out = core.bank[6 + h % 2]
                v = tokens[:, :, h * P:(h + 1) * P]
                nc.tensor.matmul(out[:, 0:T], v[:, 0, :], combined_T[:, h % 2, 0:T], start=True, stop=False)
                nc.tensor.matmul(out[:, P:T], v[:, 1, :], combined_T[:, h % 2, T:3 * P], start=False, stop=True) \
                    .then_inc(mixed.sem, 1)

        @block.vector
        def _(dve):
            link = Chain(step, dve)

            def peaks(h):
                dve.wait_ge(scored.sem, scored.at(h + 1))
                s = probs[:, h % 2]
                for m in range(2):
                    i = nc.vector.scalar_tensor_tensor(out=s[:, m], in0=core.bank[2 * (h % 2) + m][:, 0:384], scalar=0.125,
                                                       in1=mask, op0=ALU.mult, op1=ALU.add)
                i.then_inc(scored_taken.sem, 1)
                dve.wait_ge(scored_taken.sem, scored_taken.at(h + 1))
                nc.vector.tensor_reduce(peak[:, 0:2], s[:, :, 0:P], AX_X, ALU.max)
                link(nc.vector.tensor_reduce(peak[:, 2:4], s[:, :, P:3 * P], AX_X, ALU.max))
                nc.vector.tensor_scalar(peak[:, 0:4], peak[:, 0:4], -1.0, None, ALU.mult).then_inc(peaked.sem, 1)

            for h in range(HEADS):
                peaks(h)
                dve.wait_ge(exped.sem, exped.at(h + 1))
                s = probs[:, h % 2]
                link(nc.vector.reciprocal(total[:, 0:4], total[:, 0:4]))
                for i in range(2):
                    j = nc.vector.tensor_tensor(sums(1, i), sums(1, i), minus_lam[:, 3:4], ALU.mult)
                link(j)
                for i in range(2):
                    j = nc.vector.tensor_scalar(s[:, 1, span[i]], s[:, 1, span[i]], sums(1, i), None, ALU.mult)
                link(j)
                if h >= 2:
                    dve.wait_ge(flipped.sem, flipped.at(h - 1))
                for i in range(2):
                    j = nc.vector.scalar_tensor_tensor(out=combined[:, h % 2, span[i]], in0=s[:, 0, span[i]], scalar=sums(0, i),
                                                       in1=s[:, 1, span[i]], op0=ALU.mult, op1=ALU.add)
                j.then_inc(weighed.sem, 1)
            step.used = link.n

        @block.scalar
        def _(act):
            for h in range(HEADS + 1):
                if h < HEADS:
                    act.wait_ge(peaked.sem, peaked.at(h + 1))
                    s = probs[:, h % 2]
                    for m in range(2):
                        for i in range(2):
                            j = nc.scalar.activation(s[:, m, span[i]], s[:, m, span[i]], ACT.Exp, bias=minus_peak(m, i),
                                                     accum_out=sums(m, i))
                    j.then_inc(exped.sem, 1)
                if h >= 1:
                    act.wait_ge(mixed.sem, mixed.at(h))
                    nc.scalar.activation(o[:, h - 1, :], core.bank[6 + (h - 1) % 2][:, 0:T], ACT.Identity).then_inc(mixed_taken.sem, 1)
                if h < HEADS:
                    act.wait_ge(flipped.sem, flipped.at(h + 1))
                    src, dst = core.bank[4 + h % 2], combined_T[:, h % 2]
                    nc.scalar.activation(dst, src[:, 0:384], ACT.Identity).then_inc(kept.sem, 1)
    step.close(step.used)
    for s in (scored, peaked, exped, weighed, flipped, kept, mixed, scored_taken, mixed_taken):
        s.close(HEADS)

    block_rms(core, o, 8, "ones", P, core.c("eps"), squares, root)
    with nc.Block() as block:
        @block.vector
        def _(dve):
            nc.vector.scalar_tensor_tensor(out=o, in0=o, scalar=gain, in1=root, op0=ALU.mult, op1=ALU.mult)
    core.linear(o, "vector", [(0, 8, core.add_to_x(lambda n: core.mod[:, 1, bass.ds(n + 2 * KB, 1)]))])


def norm_in_place(core, gain):
    core.norm(core.x, core.x, core.col(gain), None, view(core.arena, 0, 8, T))



def second_projection(core):
    nc, sig, A = core.nc, core.sig, core.arena
    proj, tail = view(A, 0, 31, T), view(A, 8192, KB, 288)
    core.linear(core.h, "scalar", [(0, 28, core.copy_to(proj))])
    loaded, done = sig("small_loaded"), sig("tail_projected")
    n = [0]
    with nc.Block() as block:
        @block.sync
        def _(sp):
            n[0] = core.load(sp, [(tail, "w_in_tail")])

        @block.tensor
        def _(pe):
            pe.wait_ge(loaded.sem, loaded.at(16))
            for b, width in enumerate((P, P, 32)):
                for c in range(KB):
                    mm = nc.tensor.matmul(core.bank[b][0:width, 0:T], tail[:, c, b * P:b * P + width], core.h[:, c, :],
                                          start=(c == 0), stop=(c == KB - 1))
                mm.then_inc(done.sem, 1)

        @block.scalar
        def _(act):
            for b, width in enumerate((P, P, 32)):
                act.wait_ge(done.sem, done.at(b + 1))
                nc.scalar.activation(proj[0:width, 28 + b, :], core.bank[b][0:width, 0:T], ACT.Identity)
    loaded.close(n[0])
    done.close(3)


def scaled_and_shifted(core, dst, src, gain, bias):
    for b in range(4):
        i = core.nc.vector.tensor_scalar(dst[:, b, :], src[:, b, :], core.col(gain, b), core.col(bias, b), ALU.mult, ALU.add)
    return i


def retention(core):
    nc, sig, A = core.nc, core.sig, core.arena
    proj, turned, tokens = view(A, 0, 31, T), view(A, 10496, 8, T), view(A, 12544, 2, 4 * P)
    decay, scores = view(A, 13568, 8, 3 * P), view(A, 16640, 8, 3 * P)
    y, cat = view(A, 19712, 4, T), view(A, 20736, 8, T)
    rope(core, proj[:, 0:8], turned, 4, core.trig[:, 3, :], core.trig[:, 2, :])
    token_major(core, [(proj[:, 8:12], tokens)])
    scored, decayed, mixed, loaded = sig("heads_scored"), sig("heads_weighed"), sig("heads_mixed"), sig("small_loaded")
    n = [0]
    with nc.Block() as block:
        @block.sync
        def _(sp):
            n[0] = core.load(sp, [(A[:, 13568:13568 + 8 * 384], "decay")])

        @block.tensor
        def _(pe):
            for h in range(8):
                half = slice(64 * (h % 2), 64 * (h % 2) + 64)
                if h >= 4:
                    pe.wait_ge(decayed.sem, decayed.at(h - 3))
                q, k = turned[half, h // 2, :], turned[half, 4 + h // 2, :]
                nc.tensor.matmul(core.bank[h % 4][:, 0:T], k[:, 0:P], q, start=True, stop=True)
                nc.tensor.matmul(core.bank[h % 4][:, T:3 * P], k[:, P:T], q[:, P:T], start=True, stop=True).then_inc(scored.sem, 1)
            for h in range(8):
                half = slice(64 * (h % 2), 64 * (h % 2) + 64)
                pe.wait_ge(decayed.sem, decayed.at(h + 1))
                out = core.bank[4 + h // 2][half]
                nc.tensor.matmul(out[:, 0:T], tokens[:, 0, h * 64:(h + 1) * 64], scores[:, h, 0:T], start=True, stop=False,
                                 skip_group_check=True)
                nc.tensor.matmul(out[:, P:T], tokens[:, 1, h * 64:(h + 1) * 64], scores[:, h, T:3 * P], start=False, stop=True,
                                 skip_group_check=True).then_inc(mixed.sem, 1)

        @block.vector
        def _(dve):
            dve.wait_ge(loaded.sem, loaded.at(16))
            for h in range(8):
                dve.wait_ge(scored.sem, scored.at(h + 1))
                nc.vector.tensor_tensor(scores[:, h, :], core.bank[h % 4][:, 0:3 * P], decay[:, h, :], ALU.mult) \
                    .then_inc(decayed.sem, 1)

        @block.scalar
        def _(act):
            for b in range(4):
                act.wait_ge(mixed.sem, mixed.at(2 * b + 2))
                nc.scalar.activation(y[:, b, :], core.bank[4 + b][:, 0:T], ACT.Identity)
    loaded.close(n[0])
    for s in (scored, decayed, mixed):
        s.close(8)
    centred, squares, root = view(A, 13568, 4, T), view(A, 14592, 4, T), view(A, 15616, 4, T)
    block_rms(core, y, 4, "half_ones", 64, core.c("eps_ret"), squares, root, centre=centred)
    gated, step = sig("gate_activated"), sig("dve_step")
    with nc.Block() as block:
        @block.scalar
        def _(act):
            nc.scalar.activation(squares, proj[:, 12:16], ACT.Silu).then_inc(gated.sem, 1)

        @block.vector
        def _(dve):
            link = Chain(step, dve)
            link(nc.vector.tensor_tensor(centred, centred, root, ALU.mult))
            link(scaled_and_shifted(core, centred, centred, "ret_gn_w_2", "ret_gn_b_2"))
            dve.wait_ge(gated.sem, gated.at(1))
            nc.vector.tensor_tensor(cat[:, 0:4], centred, squares, ALU.mult)
            step.used = link.n
    step.close(step.used)
    gated.close(1)


def rwkv(core):
    nc, sig, A = core.nc, core.sig, core.arena
    proj, cat = view(A, 0, 31, T), view(A, 20736, 8, T)
    step, act_step = sig("dve_step"), sig("act_step")
    spots = [8192 + 1024 * i for i in range(12)] + [22784 + 1024 * i for i in range(9)]
    area = lambda i, n=1: view(A, spots[i], 4 * n, T)
    shifted = view(A, 8192, 15, T)
    r, k, v = proj[:, 16:20], proj[:, 20:24], proj[:, 24:28]
    low = proj[:, 28]
    up, g_up, g_up_tail = A[:, 31744:31744 + 512], A[:, 32256:32768], core.work[0:32, 3584:4096]
    loaded = sig("small_loaded")
    n = [0]

    with nc.Block() as block:
        @block.sync
        def _(sp):
            n[0] = core.load(sp, [(up, "rwkv_up"), (g_up, "rwkv_g_up"), (g_up_tail, "rwkv_g_up_tail")])

        @block.vector
        def _(dve):
            link = Chain(step, dve)
            for blocks, rows in ((slice(0, 14), slice(0, P)), (slice(14, 15), slice(0, 32))):
                p = proj[rows, 16:31][:, blocks]
                d = shifted[rows, blocks]
                nc.vector.tensor_tensor(d[:, :, 1:T], p[:, :, 0:T - 1], p[:, :, 1:T], ALU.subtract)
                link(nc.vector.tensor_scalar(d[:, :, 0:1], p[:, :, 0:1], -1.0, None, ALU.mult))
            for b in range(15):
                rows = slice(0, P) if b < 14 else slice(0, 32)
                mu = core.col("rwkv_mu_2", b) if b < 14 else core.col("rwkv_mu_tail")
                link(nc.vector.scalar_tensor_tensor(out=proj[rows, 16 + b, :], in0=shifted[rows, b, :], scalar=mu[rows],
                                                    in1=proj[rows, 16 + b, :], op0=ALU.mult, op1=ALU.add))
            step.used = link.n
    step.close(step.used)
    loaded.close(n[0])

    sig_w, a, gate, kk, squares, norm = area(0), area(2), area(3), area(4), area(5), area(6)
    hidden, sums = sig("hidden_ready"), sig("low_rank_ready")
    with nc.Block() as block:
        @block.scalar
        def _(act):
            nc.scalar.activation(low[0:64], low[0:64], ACT.Tanh)
            nc.scalar.activation(proj[:, 29], proj[:, 29], ACT.Sigmoid)
            nc.scalar.activation(proj[0:32, 30], proj[0:32, 30], ACT.Sigmoid).then_inc(hidden.sem, 1)
            for b in range(4):
                act.wait_ge(sums.sem, sums.at(b + 1))
                nc.scalar.activation(sig_w[:, b, :], core.bank[b][:, 0:T], ACT.Sigmoid, bias=core.col("rwkv_w0_2", b))
                nc.scalar.activation(a[:, b, :], core.bank[4 + b][:, 0:T], ACT.Sigmoid, bias=core.col("rwkv_a0_2", b))
                nc.scalar.activation(gate[:, b, :], core.bank[b][:, T:2 * T], ACT.Identity)

        @block.tensor
        def _(pe):
            pe.wait_ge(hidden.sem, hidden.at(1))
            for b in range(4):
                c = slice(b * P, (b + 1) * P)
                nc.tensor.matmul(core.bank[b][:, 0:T], up[0:64, c], low[0:64], start=True, stop=True)
                nc.tensor.matmul(core.bank[4 + b][:, 0:T], up[64:P, c], low[64:P], start=True, stop=True)
                nc.tensor.matmul(core.bank[b][:, T:2 * T], g_up[:, c], proj[:, 29], start=True, stop=False)
                nc.tensor.matmul(core.bank[b][:, T:2 * T], g_up_tail[:, c], proj[0:32, 30], start=False, stop=True) \
                    .then_inc(sums.sem, 1)

        @block.vector
        def _(dve):
            for b in range(4):
                nc.vector.tensor_scalar(kk[:, b, :], k[:, b, :], core.col("rwkv_k_k_2", b), None, ALU.mult)
    hidden.close(1)
    sums.close(4)
    squared, summed, rooted = sig("squared"), sig("square_sums"), sig("rooted")
    flat = lambda x: x.rearrange("p n t -> p (n t)")
    decay_sum, decay_log = area(1), area(0)
    reset = flat(area(7))
    cols = [0]
    with nc.Block() as block:
        @block.sync
        def _(sp):
            cols[0] = core.load(sp, [(reset, "reset")])

        @block.vector
        def _(dve):
            link = Chain(step, dve)
            nc.vector.tensor_tensor(squares, kk, kk, ALU.mult).then_inc(squared.sem, 1)
            link(nc.vector.tensor_scalar(decay_log, sig_w, -math.exp(-0.5), None, ALU.mult))
            dve.wait_ge(loaded.sem, loaded.at(16))
            link(nc.vector.tensor_tensor_scan(flat(decay_sum), reset, flat(decay_log), 0.0, ALU.mult, ALU.add))
            dve.wait_ge(rooted.sem, rooted.at(1))
            link(nc.vector.tensor_scalar(norm, norm, 1e-12, None, ALU.max))
            link(nc.vector.reciprocal(norm, norm))
            link(nc.vector.tensor_tensor(kk, kk, norm, ALU.mult))
            for b in range(4):
                i = nc.vector.tensor_scalar(squares[:, b, :], a[:, b, :], 1.0, core.col("rwkv_k_a_2", b), ALU.subtract, ALU.mult)
            link(i)
            link(nc.vector.scalar_tensor_tensor(out=k, in0=squares, scalar=1.0, in1=k, op0=ALU.add, op1=ALU.mult))
            link(nc.vector.tensor_tensor(a, kk, a, ALU.mult))
            step.used = link.n

        @block.tensor
        def _(pe):
            pe.wait_ge(squared.sem, squared.at(1))
            for i in range(2):
                mm = nc.tensor.matmul(core.bank[i][:], core.c("half_ones"), flat(squares)[:, i * BANK:(i + 1) * BANK], start=True, stop=True)
            mm.then_inc(summed.sem, 1)

        @block.scalar
        def _(act):
            act.wait_ge(summed.sem, summed.at(1))
            for i in range(2):
                j = nc.scalar.activation(flat(norm)[:, i * BANK:(i + 1) * BANK], core.bank[i][:], ACT.Sqrt)
            j.then_inc(rooted.sem, 1)
    step.close(step.used)
    loaded.close(cols[0])
    for s in (squared, summed, rooted):
        s.close(1)
    b_vec = a

    upto, before, inverse, rest = area(7), area(8), area(9), area(10)
    a_in, b_out, k_out, r_in, b_end, k_end = area(5), area(6), area(9), area(7), area(11), area(12)
    logs = area(13)
    chunks = lambda x: x.rearrange("p n (c t) -> p (n c) t", t=CHUNK)
    exped = sig("decays_exped")
    with nc.Block() as block:
        @block.vector
        def _(dve):
            link = Chain(step, dve)
            link(nc.vector.tensor_tensor(before, decay_sum, decay_log, ALU.subtract))
            last = chunks(decay_sum)[:, :, CHUNK - 1:CHUNK].to_broadcast([P, 16, CHUNK])
            nc.vector.tensor_tensor(chunks(rest), last, chunks(decay_sum), ALU.subtract).then_inc(exped.sem, 1)
            dve.wait_ge(exped.sem, exped.at(5))
            link(nc.vector.scalar_tensor_tensor(out=a_in, in0=kk, scalar=-1.0, in1=before, op0=ALU.mult, op1=ALU.mult))
            link(nc.vector.tensor_tensor(b_out, b_vec, inverse, ALU.mult))
            link(nc.vector.tensor_tensor(k_out, k, inverse, ALU.mult))
            link(nc.vector.tensor_tensor(b_end, b_vec, rest, ALU.mult))
            link(nc.vector.tensor_tensor(k_end, k, rest, ALU.mult))
            link(nc.vector.tensor_copy(core.work[:, 0:16], chunks(upto)[:, :, CHUNK - 1]))
            for b in range(4):
                i = nc.vector.scalar_tensor_tensor(out=logs[:, b, :], in0=r[:, b, :], scalar=core.col("rwkv_r_k_2", b),
                                                   in1=k[:, b, :], op0=ALU.mult, op1=ALU.mult)
            link(i)
            link(nc.vector.tensor_tensor(r_in, r, upto, ALU.mult))
            step.used = link.n

        @block.scalar
        def _(act):
            act.wait_ge(exped.sem, exped.at(1))
            for dst, src, scale in ((upto, decay_sum, 1.0), (before, before, 1.0), (inverse, decay_sum, -1.0), (rest, rest, 1.0)):
                nc.scalar.activation(dst, src, ACT.Exp, scale=scale).then_inc(exped.sem, 1)
    step.close(step.used)
    exped.close(5)
    bonus_terms = logs

    a_tok, b_tok, k_tok, v_tok = (view(A, spots[i], 2, 4 * P) for i in (0, 1, 2, 14))
    token_major(core, [(a_in, a_tok), (b_end, b_tok), (k_end, k_tok), (v, v_tok)])

    wide = lambda at: view(A, at, 8, P)
    masks = view(core.work, 16, 8, P)
    NT, inv, inv_T = wide(spots[8]), wide(spots[10]), wide(spots[11])
    M1, LT = wide(spots[12]), wide(spots[15])
    RB, RK = wide(spots[16]), wide(spots[17])
    LV, both = view(core.h_flat, 0, 8, 64), wide(spots[18])
    M_T, Q, R2, y = area(19), area(4), area(20), view(core.h_flat, 1024, 4, T)
    M_T_c = M_T.rearrange("p n (c k) -> p n c k", c=CHUNKS)
    Q_c = Q.rearrange("p n (c k) -> p n c k", c=CHUNKS)
    with nc.Block() as block:
        @block.sync
        def _(sp):
            n[0] = core.load(sp, [(core.work[:, 16:16 + 8 * P], "rwkv_masks")])
    loaded.close(n[0])
    eye2 = core.c("eye2")
    full, out_ready = sig("products_ready"), sig("products_kept")

    def tile(t):
        tk = slice(t * P, (t + 1) * P)
        half = lambda h: slice(64 * (h % 2), 64 * (h % 2) + 64)
        hc = lambda h: slice(h * 64, (h + 1) * 64)
        mask = lambda i: masks[:, i, :].unsqueeze(1).to_broadcast([P, 4, P])
        kinds = [(b_out, a_in, NT, 6), (k_out, a_in, LT, 6), (b_out, r_in, RB, 7), (k_out, r_in, RK, 7)]
        bank4 = lambda i: core.bank[i][:].rearrange("p (h k) -> p h k", h=4)
        with nc.Block() as block:
            @block.tensor
            def _(pe):
                for n, (left, right, _, _) in enumerate(kinds):
                    for g in range(2):
                        for h in range(g, 8, 2):
                            mm = nc.tensor.matmul(core.bank[2 * n + g][:, (h // 2) * P:(h // 2 + 1) * P], left[half(h), h // 2, tk],
                                                  right[half(h), h // 2, tk], start=True, stop=True)
                        mm.then_inc(full.sem, 1)

            @block.vector
            def _(dve):
                for n, (_, _, dst, which) in enumerate(kinds):
                    for g in range(2):
                        dve.wait_ge(full.sem, full.at(2 * n + g + 1))
                        nc.vector.tensor_tensor(dst[:, g:8:2, :], bank4(2 * n + g), mask(which), ALU.mult)

            @block.gpsimd
            def _(pool):
                for g in range(8):
                    nc.gpsimd.tensor_copy(inv[:, g, :], core.c("ident"))
                    nc.gpsimd.tensor_copy(inv_T[:, g, :], core.c("ident"))
        full.close(8)

        with nc.Block() as block:
            @block.tensor
            def _(pe):
                for level in range(6):
                    for g in range(2):
                        if level:
                            pe.wait_ge(out_ready.sem, out_ready.at(4 * (level - 1) + 2 + g + 1))
                        for h in range(4 * g, 4 * g + 4):
                            mm = nc.tensor.matmul(core.bank[g][:, (h % 4) * P:(h % 4 + 1) * P], NT[:, h, :], inv[:, h, :],
                                                  start=True, stop=True)
                        mm.then_inc(full.sem, 1)
                    for g in range(2):
                        pe.wait_ge(out_ready.sem, out_ready.at(4 * level + g + 1))
                        for h in range(4 * g, 4 * g + 4):
                            c = slice((h % 4) * P, (h % 4 + 1) * P)
                            nc.tensor.matmul(core.bank[2 + g][:, c], inv_T[:, h, :], M1[:, h, :], start=True, stop=True)
                            mm = nc.tensor.matmul(core.bank[4 + g][:, c], M1[:, h, :], inv_T[:, h, :], start=True, stop=True)
                        mm.then_inc(full.sem, 1)

            @block.vector
            def _(dve):
                for level in range(6):
                    for g in range(2):
                        dve.wait_ge(full.sem, full.at(4 * level + g + 1))
                        nc.vector.tensor_tensor(M1[:, 4 * g:4 * g + 4, :], bank4(g), mask(level), ALU.mult).then_inc(out_ready.sem, 1)
                    for g in range(2):
                        dve.wait_ge(full.sem, full.at(4 * level + 2 + g + 1))
                        s = slice(4 * g, 4 * g + 4)
                        nc.vector.tensor_tensor(inv[:, s, :], inv[:, s, :], bank4(2 + g), ALU.add)
                        nc.vector.tensor_tensor(inv_T[:, s, :], inv_T[:, s, :], bank4(4 + g), ALU.add).then_inc(out_ready.sem, 1)
        full.close(24)
        out_ready.close(24)

        with nc.Block() as block:
            @block.tensor
            def _(pe):
                for h in range(8):
                    mm = nc.tensor.matmul(core.bank[0][:, hc(h)], LT[:, h, :], v_tok[:, t, hc(h)], start=True, stop=True)
                mm.then_inc(full.sem, 1)
                for g in range(2):
                    for h in range(4 * g, 4 * g + 4):
                        at = (h % 4) * P
                        mm = nc.tensor.matmul(core.bank[1 + g][:, at + 64:at + P], inv_T[:, h, :], a_tok[:, t, hc(h)], start=True, stop=True)
                pe.wait_ge(out_ready.sem, out_ready.at(1))
                for g in range(2):
                    for h in range(4 * g, 4 * g + 4):
                        at = (h % 4) * P
                        mm = nc.tensor.matmul(core.bank[1 + g][:, at:at + 64], inv_T[:, h, :], LV[:, h, :], start=True, stop=True)
                    mm.then_inc(full.sem, 1)
                pe.wait_ge(out_ready.sem, out_ready.at(3))
                for c in range(2):
                    rows = slice(64 * c, 64 * c + 64)
                    for h in range(8):
                        at = slice((h // 2) * 64, (h // 2) * 64 + 64)
                        nc.tensor.matmul(core.bank[3 + c][half(h), at], both[rows, h, 64:P], b_tok[rows, t, hc(h)],
                                         start=True, stop=True, skip_group_check=True)
                    for h in range(8):
                        at = slice(T + (h // 2) * 64, T + (h // 2) * 64 + 64)
                        nc.tensor.matmul(core.bank[3 + c][half(h), at], b_tok[rows, t, hc(h)], both[rows, h, 0:64],
                                         start=True, stop=False, skip_group_check=True)
                        mm = nc.tensor.matmul(core.bank[3 + c][half(h), at], k_tok[rows, t, hc(h)], v_tok[rows, t, hc(h)],
                                              start=False, stop=True, skip_group_check=True)
                    mm.then_inc(full.sem, 1)
                for h in range(8):
                    at = slice((h // 2) * P, (h // 2 + 1) * P)
                    nc.tensor.matmul(core.bank[5][half(h), at], both[:, h, 64:P], RB[:, h, :], start=True, stop=True,
                                     skip_group_check=True)
                    nc.tensor.matmul(core.bank[6][half(h), at], both[:, h, 0:64], RB[:, h, :], start=True, stop=False,
                                     skip_group_check=True)
                    mm = nc.tensor.matmul(core.bank[6][half(h), at], v_tok[:, t, hc(h)], RK[:, h, :], start=False, stop=True,
                                          skip_group_check=True)
                mm.then_inc(full.sem, 1)

            @block.vector
            def _(dve):
                dve.wait_ge(full.sem, full.at(1))
                nc.vector.tensor_copy(LV, core.bank[0][:].rearrange("p (h k) -> p h k", h=8)).then_inc(out_ready.sem, 1)
                for g in range(2):
                    dve.wait_ge(full.sem, full.at(2 + g))
                    nc.vector.tensor_copy(both[:, 4 * g:4 * g + 4, :], bank4(1 + g)).then_inc(out_ready.sem, 1)
                for c in range(2):
                    dve.wait_ge(full.sem, full.at(4 + c))
                    chunk = 2 * t + c
                    for b in range(4):
                        nc.vector.scalar_tensor_tensor(out=M_T_c[:, b, chunk, :], in0=eye2,
                                                       scalar=core.work[:, b * CHUNKS + chunk:b * CHUNKS + chunk + 1],
                                                       in1=core.bank[3 + c][:, b * 64:(b + 1) * 64], op0=ALU.mult, op1=ALU.add)
                    nc.vector.tensor_copy(Q_c[:, :, chunk, :], core.bank[3 + c][:, T:2 * T].rearrange("p (n k) -> p n k", n=4))
                dve.wait_ge(full.sem, full.at(6))
                nc.vector.tensor_tensor(R2[:, :, tk], r_in[:, :, tk], bank4(5), ALU.add)
                nc.vector.tensor_copy(y[:, :, tk], bank4(6))
        full.close(6)
        out_ready.close(3)

    for t in range(TT):
        tile(t)

    states = view(A, spots[8], 12, 64)
    state = lambda c: states[:, 4 * (c - 1):4 * c, :]
    part = lambda h: slice(64 * (h % 2), 64 * (h % 2) + 64)
    with nc.Block() as block:
        @block.tensor
        def _(pe):
            for c in range(1, CHUNKS):
                pe.wait_ge(out_ready.sem, out_ready.at(c))
                if c < CHUNKS - 1:
                    for h in range(8):
                        mm = nc.tensor.matmul(core.bank[c][part(h), (h // 2) * 64:(h // 2) * 64 + 64], M_T_c[part(h), h // 2, c, :],
                                              state(c)[part(h), h // 2, :], start=True, stop=True, skip_group_check=True)
                    mm.then_inc(full.sem, 1)
                for h in range(8):
                    mm = nc.tensor.matmul(core.bank[3 + c][part(h), (h // 2) * 64:(h // 2) * 64 + 64], state(c)[part(h), h // 2, :],
                                          R2[part(h), h // 2, c * CHUNK:(c + 1) * CHUNK], start=True, stop=True, skip_group_check=True)
                mm.then_inc(full.sem, 1)

        @block.vector
        def _(dve):
            bank64 = lambda i: core.bank[i][:, 0:T].rearrange("p (n k) -> p n k", n=4)
            nc.vector.tensor_copy(state(1), Q_c[:, :, 0, :]).then_inc(out_ready.sem, 1)
            count = 0
            for c in range(1, CHUNKS):
                if c < CHUNKS - 1:
                    count += 1
                    dve.wait_ge(full.sem, full.at(count))
                    nc.vector.tensor_tensor(state(c + 1), bank64(c), Q_c[:, :, c, :], ALU.add).then_inc(out_ready.sem, 1)
                count += 1
                dve.wait_ge(full.sem, full.at(count))
                out = y[:, :, c * CHUNK:(c + 1) * CHUNK]
                nc.vector.tensor_tensor(out, out, bank64(3 + c), ALU.add)
    full.close(5)
    out_ready.close(3)

    centred, squares, root = area(0), area(1), area(2)
    block_rms(core, y, 4, "half_ones", 64, core.c("eps_rwkv"), squares, root, centre=centred)
    with nc.Block() as block:
        @block.tensor
        def _(pe):
            for i in range(2):
                mm = nc.tensor.matmul(core.bank[i][:], core.c("half_ones"), flat(bonus_terms)[:, i * BANK:(i + 1) * BANK],
                                      start=True, stop=True)
            mm.then_inc(full.sem, 1)

        @block.vector
        def _(dve):
            link = Chain(step, dve)
            link(nc.vector.tensor_tensor(centred, centred, root, ALU.mult))
            link(scaled_and_shifted(core, centred, centred, "rwkv_gn_w_2", "rwkv_gn_b_2"))
            dve.wait_ge(full.sem, full.at(1))
            for i in range(2):
                j = nc.vector.tensor_tensor(flat(squares)[:, i * BANK:(i + 1) * BANK], core.bank[i][:],
                                            flat(v)[:, i * BANK:(i + 1) * BANK], ALU.mult)
            link(j)
            link(nc.vector.tensor_tensor(centred, centred, squares, ALU.add))
            nc.vector.tensor_tensor(cat[:, 4:8], centred, gate, ALU.mult)
            step.used = link.n
    step.close(step.used)
    full.close(1)


def second_mixer(core):
    second_projection(core)
    retention(core)
    rwkv(core)
    core.linear(view(core.arena, 20736, 8, T), "vector", [(0, 8, core.add_to_x())])



def cross_attention(core):
    nc, sig, A = core.nc, core.sig, core.arena
    scratch, mem, q, kv = view(A, 0, 8, T), view(A, 2048, 8, T), view(A, 4096, 8, T), view(A, 6144, 16, T)
    tokens, o = view(A, 10240, 2, D), view(A, 12288, 8, T)
    probs, probs_T = view(A, 14336, 4, T), view(A, 15360, 4, T)
    small = A[:, 16384:16384 + 16]
    loaded, step = sig("small_loaded"), sig("dve_step")
    core.norm(core.x, core.h, core.col("norm_xattn_2"), None, scratch)
    core.linear(core.h, "scalar", [(0, 8, core.copy_to(q))])
    n = [0]
    with nc.Block() as block:
        @block.sync
        def _(sp):
            n[0] = core.load(sp, [(mem, "mem")])
    loaded.close(n[0])
    core.norm(mem, core.h, core.col("norm_mem_2"), None, scratch)
    core.linear(core.h, "scalar", [(0, 16, core.copy_to(kv))])
    token_major(core, [(kv[:, 8:16], tokens)])
    scored, peaked, exped, weighed, flipped, kept, mixed, mixed_taken = (sig(x) for x in (
        "heads_scored", "heads_peaked", "heads_exped", "heads_weighed", "heads_flipped", "flips_kept", "heads_mixed", "mixed_taken"))
    scale = 1.0 / 16
    with nc.Block() as block:
        @block.tensor
        def _(pe):
            def scores(h):
                if h >= 2:
                    pe.wait_ge(exped.sem, exped.at(h - 1))
                for i in range(2):
                    for b in range(2):
                        mm = nc.tensor.matmul(core.bank[h % 2][:, i * T:(i + 1) * T], q[:, 2 * h + b, i * P:(i + 1) * P],
                                              kv[:, 2 * h + b, :], start=(b == 0), stop=(b == 1))
                mm.then_inc(scored.sem, 1)

            scores(0)
            for h in range(4):
                if h + 1 < 4:
                    scores(h + 1)
                pe.wait_ge(weighed.sem, weighed.at(h + 1))
                if h >= 2:
                    pe.wait_ge(kept.sem, kept.at(h - 1))
                for m in range(2):
                    for i in range(2):
                        mm = nc.tensor.transpose(core.bank[2 + h % 2][:, m * T + i * P:m * T + (i + 1) * P],
                                                 probs[:, 2 * (h % 2) + i, m * P:(m + 1) * P], core.c("ident"))
                mm.then_inc(flipped.sem, 1)
                pe.wait_ge(kept.sem, kept.at(h + 1))
                if h >= 2:
                    pe.wait_ge(mixed_taken.sem, mixed_taken.at(h - 1))
                for b in range(2):
                    for m in range(2):
                        mm = nc.tensor.matmul(core.bank[4 + h % 2][:, b * T:(b + 1) * T],
                                              tokens[:, m, (2 * h + b) * P:(2 * h + b + 1) * P], probs_T[:, 2 * (h % 2) + m, :],
                                              start=(m == 0), stop=(m == 1))
                mm.then_inc(mixed.sem, 1)

        @block.vector
        def _(dve):
            link = Chain(step, dve)
            for h in range(4):
                dve.wait_ge(scored.sem, scored.at(h + 1))
                link(nc.vector.tensor_reduce(small[:, 0:2], core.bank[h % 2][:].rearrange("p (i m) -> p i m", i=2), AX_X, ALU.max))
                nc.vector.tensor_scalar(small[:, 2:4], small[:, 0:2], -scale, None, ALU.mult).then_inc(peaked.sem, 1)
                dve.wait_ge(exped.sem, exped.at(h + 1))
                link(nc.vector.reciprocal(small[:, 4:6], small[:, 4:6]))
                for i in range(2):
                    p = probs[:, 2 * (h % 2) + i, :]
                    j = nc.vector.tensor_scalar(p, p, small[:, 4 + i:5 + i], None, ALU.mult)
                j.then_inc(weighed.sem, 1)
            step.used = link.n

        @block.scalar
        def _(act):
            for h in range(5):
                if h < 4:
                    act.wait_ge(peaked.sem, peaked.at(h + 1))
                    if h >= 2:
                        act.wait_ge(flipped.sem, flipped.at(h - 1))
                    for i in range(2):
                        j = nc.scalar.activation(probs[:, 2 * (h % 2) + i, :], core.bank[h % 2][:, i * T:(i + 1) * T], ACT.Exp,
                                                 bias=small[:, 2 + i:3 + i], scale=scale, accum_out=small[:, 4 + i:5 + i])
                    j.then_inc(exped.sem, 1)
                if h >= 1:
                    act.wait_ge(mixed.sem, mixed.at(h))
                    nc.scalar.activation(o[:, 2 * h - 2:2 * h, :], core.bank[4 + (h - 1) % 2][:].rearrange("p (b t) -> p b t", b=2),
                                         ACT.Identity).then_inc(mixed_taken.sem, 1)
                if h < 4:
                    act.wait_ge(flipped.sem, flipped.at(h + 1))
                    s = slice(2 * (h % 2), 2 * (h % 2) + 2)
                    nc.scalar.activation(probs_T[:, s, :], core.bank[2 + h % 2][:].rearrange("p (m t) -> p m t", m=2),
                                         ACT.Identity).then_inc(kept.sem, 1)
    step.close(step.used)
    for s in (scored, peaked, exped, weighed, flipped, kept, mixed, mixed_taken):
        s.close(4)
    core.linear(o, "vector", [(0, 8, core.add_to_x())])


def mlp(core):
    nc = core.nc
    hidden = view(core.arena, 2048, 32, T)
    core.norm(core.x, core.h, core.col("norm_mlp_2"), None, view(core.arena, 0, 8, T))
    positive = core.sig("positive_part")

    def squared_relu(n, bank):
        part = hidden[:, n, :]
        nc.vector.tensor_scalar(part, bank, 0.0, None, ALU.max).then_inc(positive.sem, 1)
        nc.vector.wait_ge(positive.sem, n + positive.at(1))
        return nc.vector.tensor_tensor(part, part, bank, ALU.mult)

    core.linear(core.h, "vector", [(0, 32, squared_relu)])
    positive.close(32)
    core.linear(hidden, "vector", [(0, 8, core.add_to_x())], groups=4)
    core.norm(core.x, core.h, core.col("norm_final_2"), None, view(core.arena, 0, 8, T))


def column_blocks(w):

    k, n = w.shape
    w = w.reshape(k // D, KB, P, n // P, P).transpose(3, 0, 2, 1, 4)
    return np.ascontiguousarray(w.reshape(-1, P, KB * P))


def columns(*vectors):
    return np.concatenate([np.asarray(v).reshape(-1, P).T for v in vectors], axis=1)


def tokens_last(a):
    return np.ascontiguousarray(a.reshape(T, KB, P).transpose(2, 1, 0))


def layouts(i):
    out = dict(shape_constants())
    names = []

    def add(name, v):
        v = np.asarray(v).reshape(-1, P).T
        at = COLS_AT[0]
        COLS[name] = (at, at + v.shape[1])
        COLS_AT[0] += v.shape[1]
        names.append(v)

    COLS_AT = [0]
    add("c", i["c"])
    for layer in range(2):
        add(f"ada_b{layer}", i["ada_b"][layer])
        add(f"norm_mix{layer}", i["norm_mix"][layer])
        add(f"norm_ffn{layer}", i["norm_ffn"][layer])
    add("ev_g_v", i["ev_g_v"])
    add("ev_pool_scale", i["ev_pool_scale"])
    add("od_g_sub", i["od_g_sub"])
    for name in ("final_norm", "norm_mix_2", "ret_gn_w_2", "ret_gn_b_2", "rwkv_w0_2", "rwkv_a0_2", "rwkv_k_k_2",
                 "rwkv_k_a_2", "rwkv_r_k_2", "rwkv_gn_w_2", "rwkv_gn_b_2", "norm_xattn_2", "norm_mem_2", "norm_mlp_2",
                 "norm_final_2"):
        add(name, i[name])
    mu = np.asarray(i["rwkv_mu_2"]).reshape(-1)
    add("rwkv_mu_2", mu[:14 * P])
    add("rwkv_mu_tail", np.concatenate([mu[14 * P:]] * 4))
    out["cols"] = np.ascontiguousarray(np.concatenate(names, axis=1))
    out["x"] = tokens_last(i["x"])
    out["mem"] = tokens_last(i["mem_2"])
    out["positions"] = np.ascontiguousarray(np.tile(np.concatenate(
        [i["positions"].reshape(1, T), i["positions_2"].reshape(1, T)], axis=1), (P, 1)))
    for layer in range(2):
        out[f"ada_w{layer}"] = column_blocks(i["ada_w"][layer])
        out[f"peer_w_q{layer}"] = column_blocks(i["peer_w_q"][layer].reshape(D, -1))
        out[f"peer_keys{layer}"] = np.ascontiguousarray(i["peer_sub_keys"][layer].transpose(3, 0, 1, 2)).reshape(P, -1)
        out[f"peer_u{layer}"] = column_blocks(i["peer_u"][layer].T)
        out[f"peer_v{layer}"] = np.ascontiguousarray(i["peer_v"][layer].reshape(P, P, D))
    out["ev_w_in"] = column_blocks(i["ev_w_in"][0])
    out["ev_w_s"] = np.ascontiguousarray(i["ev_w_s"][0].transpose(2, 0, 1))
    out["ev_b_s"] = np.ascontiguousarray(np.tile(i["ev_b_s"].reshape(1, 4, P), (P, 1, 1)))
    out["ev_w_pool"] = np.ascontiguousarray(i["ev_w_pool"][0].transpose(1, 0, 2))
    out["ev_w_out"] = column_blocks(i["ev_w_out"][0])
    out["od_w_in"] = column_blocks(i["od_w_in"][0])
    out["od_w_out"] = column_blocks(i["od_w_out"][0])
    out["od_lam"] = np.ascontiguousarray(np.tile(np.stack(
        [i[f"od_lam_{n}"].reshape(64) for n in ("q1", "k1", "q2", "k2")])[None], (P, 1, 1)))
    w_in = np.asarray(i["w_in_2"][0])
    out["w_in_2"] = column_blocks(w_in[:, :28 * P])
    out["w_in_tail"] = np.ascontiguousarray(w_in[:, 28 * P:].reshape(KB, P, -1).transpose(1, 0, 2))
    out["rwkv_up"] = np.ascontiguousarray(np.concatenate([i["rwkv_w_up_2"][0], i["rwkv_a_up_2"][0]]))
    out["rwkv_g_up"] = np.ascontiguousarray(i["rwkv_g_up_2"][0][:P])
    out["rwkv_g_up_tail"] = np.ascontiguousarray(i["rwkv_g_up_2"][0][P:])
    out["w_out_2"] = column_blocks(i["w_out_2"][0])
    out["xattn_w_q"] = column_blocks(i["xattn_w_q_2"][0])
    out["xattn_w_kv"] = column_blocks(i["xattn_w_kv_2"][0])
    out["xattn_w_o"] = column_blocks(i["xattn_w_o_2"][0])
    out["mlp_w_up"] = column_blocks(i["mlp_w_up_2"][0])
    out["mlp_w_down"] = column_blocks(i["mlp_w_down_2"][0])
    return out


SEGMENTS = ["ada_w0", "ada_w1", "ev_w_in", "ev_w_out", "peer_w_q0", "peer_u0", "peer_v0", "od_w_in", "od_w_out",
            "peer_w_q1", "peer_u1", "peer_v1", "w_in_2", "w_out_2", "xattn_w_q", "xattn_w_kv", "xattn_w_o",
            "mlp_w_up", "mlp_w_down"]

STEPS = [
    ("setup", setup),
    ("ada0", lambda core: modulation(core, 0)),
    ("ada1", lambda core: modulation(core, 1)),
    ("norm0", lambda core: mixer_norm(core, 0)),
    ("even", even_mixer),
    ("peer0", lambda core: peer(core, 0)),
    ("norm1", lambda core: mixer_norm(core, 1)),
    ("odd", odd_mixer),
    ("peer1", lambda core: peer(core, 1)),
    ("first_end", lambda core: norm_in_place(core, "final_norm")),
    ("norm2", lambda core: core.norm(core.x, core.h, core.col("norm_mix_2"), None, view(core.arena, 0, 8, T))),
    ("second_mixer", second_mixer),
    ("cross", cross_attention),
    ("mlp", mlp),
]


def store(core, out):
    nc = core.nc
    stored = core.sig("stored")
    with nc.Block() as block:
        @block.sync
        def _(sp):
            sp.dma_start(out, core.h[:]).then_inc(stored.sem, 16)
            sp.wait_ge(stored.sem, 16)


def program(nc, dram, out, steps=STEPS, source=None):
    core = Core(nc, dram)
    for name in SEGMENTS:
        core.add_segment(name)
    for _, step in steps:
        step(core)
    if source is not None:
        source(core)
    store(core, out)
    return core


def kernel(**inputs):
    import numpy as _np
    import concourse.bacc as _bacc
    from concourse import mybir as _mybir
    from concourse.bass_utils import run_bass_kernel_spmd as _run

    nc = _bacc.Bacc("TRN2", target_bir_lowering=False, num_devices=1)
    arrays, dram = {}, {}
    for name, a in layouts({k: _np.asarray(v) for k, v in inputs.items()}).items():
        arrays[f"{name}_dram"] = a
        dram[name] = nc.dram_tensor(f"{name}_dram", a.shape, _mybir.dt.from_np(a.dtype), kind="ExternalInput").ap()
    out = nc.dram_tensor("out_dram", (P, KB, T), F32, kind="ExternalOutput").ap()
    program(nc, dram, out)
    r = _run(nc, [arrays], core_ids=[0])
    return _np.ascontiguousarray(r.results[0]["out_dram"].transpose(2, 1, 0)).reshape(1, T, D)
```

```python
import math

import numpy as np

import concourse.bass as bass
from concourse import mybir

F32 = mybir.dt.float32
F32R = mybir.dt.float32r
I32 = mybir.dt.int32
U32 = mybir.dt.uint32
ALU = mybir.AluOpType
ACT = mybir.ActivationFunctionType
AX_X = mybir.AxisListType.X

P = 128
D = 1024
KB = D // P
T = 256
TT = T // P
BANK = 512
RING = 4
HEADS, TOPK, KEYS = 8, 16, 128
CHUNK = 64
CHUNKS = T // CHUNK
EPS = 1e-6
LAM_INIT = 0.8 - 0.6 * math.exp(-0.3)
LOWEST = -3.0e38
ROUND = 1.5 * 2.0 ** 23

CONST = {}
COLS = {}


def shape_constants():
    eye = np.eye(P, dtype=np.float32)
    p = np.arange(P)
    same_half = (p[:, None] // 64 == p[None, :] // 64)
    rot = np.zeros((P, P), np.float32)
    for m in range(P):
        if m % 64 < 32:
            rot[m + 32, m] = -1.0
        else:
            rot[m - 32, m] = 1.0
    half = (p % 32).astype(np.float32)
    inv_a = (np.float32(1.0) / (np.float32(10000.0) ** ((2 * half).astype(np.float32) / np.float32(64)))).astype(np.float32)
    inv_b = (np.float32(10000.0) ** (-(half / np.float32(32)))).astype(np.float32)
    parts = [
        ("ident", eye), ("ones", np.ones((P, P))), ("half_ones", same_half), ("rot", rot),
        ("iota", np.tile(p, (P, 1))), ("iota16", np.tile(np.arange(16), (P, 1))),
        ("eye2", np.concatenate([np.eye(64), np.eye(64)])),
        ("inv_freq_a", inv_a[:, None]), ("inv_freq_b", inv_b[:, None]),
        ("eps", np.full((P, 1), EPS)), ("eps_ret", np.full((P, 1), 1e-5)), ("eps_rwkv", np.full((P, 1), 64e-5)),
        ("zeros", np.zeros((P, P))),
    ]
    at = 0
    for name, a in parts:
        CONST[name] = (at, at + a.shape[1])
        at += a.shape[1]
    resident = np.concatenate([np.asarray(a, np.float32) for _, a in parts], axis=1)

    s, t = p[:, None], p[None, :]
    even_mask = (s <= t).astype(np.float32)
    inv_count = np.zeros((P, 4, T), np.float32)
    for g, w in enumerate((2, 4, 8, 16)):
        inv_count[:, g, :] = 1.0 / np.minimum(np.arange(T) + 1, w)
    diag = np.where(t <= s, 0.0, LOWEST).astype(np.float32)
    attn_mask = np.concatenate([diag, np.zeros((P, P), np.float32), diag], axis=1)
    decay = np.zeros((P, 8, 3 * P), np.float64)
    j = p[:, None]
    for h in range(8):
        lg = np.log(1.0 - 2.0 ** (-5.0 - h))
        i0 = np.arange(T)[None, :]
        decay[:, h, 0:T] = np.where(i0 >= j, np.exp(lg * np.maximum(i0 - j, 0)), 0.0) / 8.0
        i1 = np.arange(P)[None, :]
        decay[:, h, T:] = np.where(i1 >= j, np.exp(lg * np.maximum(i1 - j, 0)), 0.0) / 8.0
    levels = []
    for lv in range(6):
        b = 2 ** lv
        levels.append((t // (2 * b) == s // (2 * b)) & (s // b == t // b + 1) & (s // CHUNK == t // CHUNK))
    chunk_same = s // CHUNK == t // CHUNK
    before = (s < t) & chunk_same
    upto = (s <= t) & chunk_same
    rwkv_masks = np.concatenate([np.concatenate(levels, 1), before, upto], 1).astype(np.float32)
    reset = np.ones((P, 4 * T), np.float32)
    reset[:, ::CHUNK] = 0.0
    return {
        "resident": resident, "even_mask": even_mask, "inv_count": inv_count.reshape(P, -1),
        "attn_mask": attn_mask, "decay": decay.reshape(P, -1).astype(np.float32),
        "rwkv_masks": rwkv_masks, "reset": reset,
    }


class Signal:

    def __init__(self, nc, name):
        self.sem = nc.alloc_semaphore(name)
        self.base = 0

    def at(self, n):
        return n + self.base

    def close(self, raised):
        self.base += raised


class Chain:

    def __init__(self, signal, engine):
        self.steps, self.engine, self.n = signal, engine, 0

    def __call__(self, instruction):
        self.n += 1
        instruction.then_inc(self.steps.sem, 1)
        self.engine.wait_ge(self.steps.sem, self.steps.at(self.n))


class Segment:

    def __init__(self, tiles, count, first):
        self.tiles, self.count, self.first = tiles, count, first


def view(t, at, n, w):
    return t[:, at:at + n * w].rearrange("p (n w) -> p n w", w=w)


class Picks:

    def __init__(self, sb):
        self.top = sb("pick_top", [P, TT, 2, TOPK])
        self.at = sb("pick_at", [P, TT, 2, TOPK], U32)
        self.at_f = sb("pick_at_f", [P, TT, 2, TOPK])
        self.sums = sb("pick_sums", [P, TT, TOPK, TOPK])
        self.best = sb("pick_best", [P, TT, TOPK])
        self.place = sb("pick_place", [P, TT, TOPK], U32)
        self.digit = sb("pick_digit", [P, 2, TT, TOPK], U32)
        self.digit_f = sb("pick_digit_f", [P, 2, TT, TOPK])
        self.chosen = sb("pick_chosen", [P, 2, TT, HEADS * TOPK])
        self.expo = sb("pick_expo", [P, TT, HEADS, TOPK])
        self.total = sb("pick_total", [P, TT * HEADS])
        self.by_pick = sb("by_pick", [P, 3, T])


SCORES_AT = 112 * T


class Core:

    def __init__(self, nc, dram):
        self.nc, self.dram = nc, dram
        sb = lambda name, shape, dt=F32: nc.alloc_sbuf_tensor(name, shape, dt)
        aligned = lambda: (nc.sbuf_base + 31) // 32 * 32

        def over(name, shape, dt, start):
            return nc.alloc_sbuf_tensor_at(name, shape, dt, offset=start)

        arena_at = aligned()
        self.arena = sb("arena", [P, P * T])
        self.x = sb("x_T", [P, KB, T])
        h_at = aligned()
        self.h_high = sb("h_high", [P, KB, T], F32R)
        self.h_low = sb("h_low", [P, KB, T], F32R)
        self.scratch = over("scratch", [P, 2 * KB * T], F32, h_at)
        self.act_high = over("act_high", [P, RING, T], F32R, h_at)
        self.act_low = over("act_low", [P, RING, T], F32R, h_at + RING * T * 4)
        self.hidden_high = over("hidden_high", [P, 32, T], F32R, arena_at + 4 * 10240)
        self.hidden_low = over("hidden_low", [P, 32, T], F32R, arena_at + 4 * 18432)
        raw_at = aligned()
        self.raw = sb("weight_raw", [P, RING, KB * P])
        self.low = over("weight_low", [P, RING, KB * P], F32R, raw_at)
        high_at = aligned()
        self.high = sb("weight_high", [P, RING, KB * P], F32R)
        self.spare = over("spare", [P, RING, KB * P], F32, high_at)
        self.work = sb("work", [P, 512])
        self.silu = sb("silu", [P, KB])
        self.const = sb("const", [P, dram["resident"].shape[1]])
        self.cols = sb("cols", [P, dram["cols"].shape[1]])
        self.mod = sb("mod", [P, 2, 48])
        self.gain = sb("gain", [P, 4, KB])
        self.trig = sb("trig", [P, 4, T])
        self.pick = Picks(sb)
        self.bank = [nc.alloc_psum_tensor(f"bank{i}", [P, BANK], F32) for i in range(8)]
        self.flags = {}
        self.segments = []
        self.next_segment = 0

    def sig(self, name):
        if name not in self.flags:
            self.flags[name] = Signal(self.nc, name)
        return self.flags[name]

    def c(self, name):
        a, b = CONST[name]
        return self.const[:, a:b]

    def col(self, name, n=None):
        a, b = COLS[name]
        return self.cols[:, a:b] if n is None else self.cols[:, a + n:a + n + 1]

    def add_segment(self, name):
        tiles = self.dram[name]
        first = self.segments[-1].first + self.segments[-1].count if self.segments else 0
        self.segments.append(Segment(tiles, tiles.shape[0], first))

    def load_tile(self, sp, seg, n, slot):
        sp.wait_ge(self.sig("tiles_used").sem, n + (seg.first + 1))
        sp.dma_start(self.raw[:, slot, :], seg.tiles[n]).then_inc(self.sig(f"slot{slot}_loaded").sem, 16)

    def first_tiles(self, sp, k):
        if k < len(self.segments):
            for slot in range(RING):
                self.load_tile(sp, self.segments[k], slot, slot)

    def stream(self, sp, seg, k):
        if seg.count > RING:
            with sp.Fori(1, seg.count // RING) as g:
                for slot in range(RING):
                    self.load_tile(sp, seg, g * RING + slot, slot)
        self.first_tiles(sp, k + 1)

    def take_segment(self):
        k = self.next_segment
        self.next_segment += 1
        return self.segments[k], k

    def make_high(self, act, seg, n, slot):
        act.wait_ge(self.sig(f"slot{slot}_loaded").sem, n * (16 // RING) + 16 * (seg.first // RING + 1))
        self.nc.scalar.activation(self.high[:, slot, :], self.raw[:, slot, :], ACT.Identity) \
            .then_inc(self.sig("high_ready").sem, 1)

    def make_low(self, eng, seg, n, slot):
        eng.wait_ge(self.sig("high_ready").sem, n + (seg.first + slot + 1))
        eng.tensor_tensor(self.low[:, slot, :], self.raw[:, slot, :], self.high[:, slot, :].bitcast(F32), ALU.subtract) \
            .then_inc(self.sig(f"low{slot}_ready").sem, 1)

    def wait_turn(self, pe, seg, turn, slot):
        pe.wait_ge(self.sig(f"low{slot}_ready").sem, turn + (seg.first // RING + 1))

    def paced(self, eng, seg, per_turn, ahead, make, finish, every=1):
        turns = seg.count // per_turn
        for n in range(ahead):
            make(0, n)

        def turn(i, last):
            for t in range(per_turn):
                if (t + 1) % every == 0:
                    finish(i, t)
                if not (last and t + ahead >= per_turn):
                    make(i, t + ahead)

        if turns > 1:
            with eng.Fori(0, turns - 1) as i:
                turn(i, False)
        turn(turns - 1, True)

    def norm(self, src, gain, shift, scaled, dst=None):
        nc, sig = self.nc, self.sig
        squared, summed, rooted, step = (sig(n) for n in ("squared", "square_sums", "rooted", "dve_step"))
        multiplied, moved, rounded = sig("norm_scaled"), sig("norm_shifted"), sig("norm_rounded")
        sums = self.bank[4][:, 0:T]
        root = self.work[:, 0:T]
        with nc.Block() as block:
            @block.vector
            def _(dve):
                link = Chain(step, dve)
                for half in range(2):
                    s = slice(half * KB // 2, (half + 1) * KB // 2)
                    nc.vector.tensor_tensor(scaled[:, s], src[:, s], src[:, s], ALU.mult).then_inc(squared.sem, 1)
                dve.wait_ge(rooted.sem, rooted.at(1))
                link(nc.vector.reciprocal(root, root))
                out = scaled if dst is None else dst
                for k in range(KB):
                    nc.vector.scalar_tensor_tensor(out=out[:, k, :], in0=src[:, k, :], scalar=gain[:, k:k + 1], in1=root,
                                                   op0=ALU.mult, op1=ALU.mult).then_inc(multiplied.sem, 1)
                    if dst is None and k >= 1:
                        dve.wait_ge(rounded.sem, rounded.at(k))
                        nc.vector.tensor_tensor(self.h_low[:, k - 1, :], scaled[:, k - 1, :],
                                                self.h_high[:, k - 1, :].bitcast(F32), ALU.subtract)
                if dst is None:
                    dve.wait_ge(rounded.sem, rounded.at(KB))
                    nc.vector.tensor_tensor(self.h_low[:, KB - 1, :], scaled[:, KB - 1, :],
                                            self.h_high[:, KB - 1, :].bitcast(F32), ALU.subtract)
                step.used = link.n

            @block.tensor
            def _(pe):
                for k in range(KB):
                    if k % (KB // 2) == 0:
                        pe.wait_ge(squared.sem, squared.at(k // (KB // 2) + 1))
                    mm = nc.tensor.matmul(sums, self.c("ones"), scaled[:, k, :], start=(k == 0), stop=(k == KB - 1))
                mm.then_inc(summed.sem, 1)

            @block.scalar
            def _(act):
                act.wait_ge(summed.sem, summed.at(1))
                nc.scalar.activation(root, sums, ACT.Sqrt, bias=self.c("eps"), scale=1.0 / D).then_inc(rooted.sem, 1)
                if dst is None:
                    for k in range(KB):
                        act.wait_ge(multiplied.sem, multiplied.at(k + 1))
                        if shift is not None:
                            nc.scalar.activation(scaled[:, k, :], scaled[:, k, :], ACT.Identity, bias=shift[:, k:k + 1]) \
                                .then_inc(moved.sem, 1)
                            act.wait_ge(moved.sem, moved.at(k + 1))
                        nc.scalar.activation(self.h_high[:, k, :], scaled[:, k, :], ACT.Identity).then_inc(rounded.sem, 1)
        step.close(step.used)
        for s, n in ((squared, 2), (summed, 1), (rooted, 1), (multiplied, KB)):
            s.close(n)
        if dst is None:
            rounded.close(KB)
            if shift is not None:
                moved.close(KB)

    def split(self, src, high, low):
        nc, rounded = self.nc, self.sig("norm_rounded")
        pairs = src.shape[1] // 2
        with nc.Block() as block:
            @block.scalar
            def _(act):
                for n in range(pairs):
                    nc.scalar.activation(high[:, 2 * n:2 * n + 2, :], src[:, 2 * n:2 * n + 2, :], ACT.Identity).then_inc(rounded.sem, 1)

            @block.vector
            def _(dve):
                for n in range(pairs):
                    dve.wait_ge(rounded.sem, rounded.at(n + 1))
                    nc.vector.tensor_tensor(low[:, 2 * n:2 * n + 2, :], src[:, 2 * n:2 * n + 2, :],
                                            high[:, 2 * n:2 * n + 2, :].bitcast(F32), ALU.subtract)
        rounded.close(pairs)

    def product(self, out, slot, rhs, k, start, stop):
        high, low = self.high[:, slot, k * P:(k + 1) * P], self.low[:, slot, k * P:(k + 1) * P]
        skip = not (start or stop)
        mm = None
        for i, (w, x) in enumerate(((high, rhs[0]), (high, rhs[1]), (low, rhs[0]))):
            mm = self.nc.tensor.matmul(out, w, x, start=(start and i == 0), stop=(stop and i == 2), skip_group_check=skip)
        return mm

    def linear(self, engine, take, groups=1, rhs=None):
        nc, sig = self.nc, self.sig
        free, used = sig("bank_free"), sig("tiles_used")
        rhs_high, rhs_low = rhs or (self.h_high, self.h_low)
        seg, k = self.take_segment()
        blocks = seg.count // groups
        per_turn = RING * groups
        with nc.Block() as block:
            @block.sync
            def _(sp):
                self.stream(sp, seg, k)

            @block.tensor
            def _(pe):
                with pe.Fori(0, blocks // RING) as turn:
                    for b in range(RING):
                        pe.wait_ge(free.sem, turn * RING + free.at(b + 1 - RING))
                        for g in range(groups):
                            slot = (b * groups + g) % RING
                            pe.wait_ge(sig(f"low{slot}_ready").sem,
                                       turn * groups + ((b * groups + g) // RING + seg.first // RING + 1))
                            for c in range(KB):
                                x = (rhs_high[:, g * KB + c, :], rhs_low[:, g * KB + c, :])
                                mm = self.product(self.bank[b][:, 0:T], slot, x, c, g + c == 0, g == groups - 1 and c == KB - 1)
                            mm.then_inc(used.sem, 1)

            def take_out(eng):
                def finish(i, t):
                    b = t // groups
                    eng.wait_ge(used.sem, i * per_turn + (seg.first + RING + t + 1))
                    take(i * RING + b, self.bank[b][:, 0:T]).then_inc(free.sem, 1)
                return finish

            def make_high(act):
                return lambda i, t: self.make_high(act, seg, i * per_turn + (t - t % RING), t % RING)

            def make_low(eng, slots):
                def make(i, t):
                    if t % RING in slots:
                        self.make_low(eng, seg, i * per_turn + (t - t % RING), t % RING)
                return make

            nothing = lambda i, t: None

            @block.scalar
            def _(act):
                self.paced(act, seg, per_turn, RING - 1, make_high(act), take_out(act) if engine == "scalar" else nothing, groups)

            @block.vector
            def _(dve):
                self.paced(dve, seg, per_turn, RING - 1, make_low(dve, (0, 2)), take_out(dve) if engine == "vector" else nothing, groups)

            @block.gpsimd
            def _(pool):
                self.paced(pool, seg, per_turn, RING - 1, make_low(pool, (1, 3)), nothing)
        free.close(blocks)

    def copy_to(self, dst, func=ACT.Identity, offset=0):
        return lambda n, bank: self.nc.scalar.activation(dst[:, n + offset, :], bank, func)

    def add_to_x(self, gate=None):
        def fn(n, bank):
            x = self.x[:, n, :]
            if gate is None:
                return self.nc.vector.tensor_tensor(x, bank, x, ALU.add)
            return self.nc.vector.scalar_tensor_tensor(out=x, in0=bank, scalar=gate(n), in1=x, op0=ALU.mult, op1=ALU.add)
        return fn

    def load(self, eng, pairs):
        loaded = self.sig("small_loaded")
        for dst, name in pairs:
            eng.dma_start(dst, self.dram[name]).then_inc(loaded.sem, 16)
        eng.wait_ge(loaded.sem, loaded.at(16 * len(pairs)))
        return 16 * len(pairs)


def setup(core):
    nc, sig = core.nc, core.sig
    loaded, step, sined = sig("small_loaded"), sig("dve_step"), sig("angles_ready")
    pos = core.scratch[:, 0:2 * T].bitcast(I32)
    pos_f = view(core.scratch, 2 * T, 2, T)
    turns = core.scratch[:, 4 * T:5 * T]
    angle = view(core.scratch, 5 * T, 4, T)
    n = [0]
    with nc.Block() as block:
        @block.sync
        def _(sp):
            core.first_tiles(sp, 0)

        @block.scalar
        def _(act):
            n[0] = core.load(act, [(core.const[:], "resident"), (core.cols[:], "cols"), (pos, "positions")] +
                             [(core.x[:], "x")])
            nc.scalar.activation(core.gain[:, 0, :], core.col("c"), ACT.Silu)
            act.wait_ge(sined.sem, sined.at(1))
            nc.scalar.activation(core.trig[:], angle, ACT.Sin)

        @block.vector
        def _(dve):
            link = Chain(step, dve)
            nc.vector.memset(core.scratch[:, 9 * T:9 * T + 1], 0.0).then_inc(sig("bank_free").sem, RING)
            for i, name in enumerate(("next_row_kept", "next_row_turned", "next_block_used")):
                nc.vector.memset(core.scratch[:, 15 * T + i:15 * T + i + 1], 0.0).then_inc(sig(name).sem, 1)
            for i, name in enumerate(("chunk_used", "row_kept", "row_turned")):
                nc.vector.memset(core.scratch[:, 14 * T + i:14 * T + i + 1], 0.0).then_inc(sig(name).sem, 4)
            nc.vector.memset(core.scratch[:, 12 * T:12 * T + 1], 0.0).then_inc(sig("gates_taken").sem, 4)
            nc.vector.memset(core.scratch[:, 13 * T:13 * T + 1], 0.0).then_inc(sig("gates_spread").sem, 2)
            nc.vector.memset(core.scratch[:, 10 * T:10 * T + 1], 0.0).then_inc(sig("tiles_used").sem, RING)
            dve.wait_ge(loaded.sem, loaded.at(16 * 4))
            link(nc.vector.tensor_copy(pos_f, pos.rearrange("p (n t) -> p n t", n=2)))
            for which, freq in enumerate(("inv_freq_a", "inv_freq_b")):
                for quarter in range(2):
                    out = angle[:, 2 * which + quarter, :]
                    link(nc.vector.tensor_scalar(out, pos_f[:, which, :], core.c(freq), None, ALU.mult))
                    link(nc.vector.tensor_scalar(turns, out, 1.0 / (2 * math.pi), 0.25 * quarter, ALU.mult, ALU.add))
                    link(nc.vector.tensor_scalar(turns, turns, ROUND, None, ALU.add))
                    link(nc.vector.tensor_scalar(turns, turns, ROUND, None, ALU.subtract))
                    high = 6.28125
                    mid = float(np.float32(np.round((2 * math.pi - high) * 2 ** 20) / 2 ** 20))
                    low = 2 * math.pi - high - mid
                    for part in (high, mid, low):
                        link(nc.vector.scalar_tensor_tensor(out=out, in0=turns, scalar=-part, in1=out,
                                                            op0=ALU.mult, op1=ALU.add))
                    if quarter:
                        link(nc.vector.tensor_scalar(out, out, math.pi / 2, None, ALU.add))
                    link(nc.vector.tensor_scalar(out, out, 3.1415925, -3.1415925, ALU.min, ALU.max))
            nc.vector.memset(core.scratch[:, 11 * T:11 * T + 1], 0.0).then_inc(sined.sem, 1)
            step.used = link.n
    step.close(step.used)
    sined.close(1)
    loaded.close(n[0])
    sig("bank_free").close(RING)


def modulation_blocks(core, pe, tiles, row):
    mm = None
    for n, tile in enumerate(tiles):
        for c in range(KB):
            mm = core.nc.tensor.matmul(row[0:1, n * P:(n + 1) * P], core.silu[:, c:c + 1], tile[:, c * P:(c + 1) * P],
                                       start=(c == 0), stop=(c == KB - 1))
    return mm


def row_to_columns(core, link, row, turned, mod, first, blocks):
    nc = core.nc
    link(nc.vector.transpose(turned[0:32, 0:blocks * P], row[0:32, 0:blocks * P]))
    parts = turned[0:32, 0:blocks * P].rearrange("p (n g i) -> p n g i", n=blocks, g=4)
    for g in range(4):
        i = nc.vector.tensor_copy(mod[32 * g:32 * g + 32, bass.ds(first, blocks)], parts[:, :, g, 0])
    return i


def modulation_gains(core, dve, link, layer):
    nc = core.nc
    mod = core.mod[:, layer, :]
    link(nc.vector.tensor_tensor(mod, mod, core.col(f"ada_b{layer}"), ALU.add))
    for which, name in enumerate(("norm_mix", "norm_ffn")):
        scale = mod[:, (3 * which + 1) * KB:(3 * which + 2) * KB]
        link(nc.vector.scalar_tensor_tensor(out=core.gain[:, 2 * layer + which, :], in0=scale, scalar=1.0,
                                            in1=core.col(f"{name}{layer}"), op0=ALU.add, op1=ALU.mult))


def modulation(core):
    nc, sig = core.nc, core.sig
    step, silu_kept, used, summed, kept, turned_ = (sig(n) for n in (
        "dve_step", "silu_kept", "chunk_used", "row_ready", "row_kept", "row_turned"))
    chunks = 48 // 4
    tiles = core.dram["ada_w0"].rearrange("(q n) p c -> q p n c", n=4)
    buffers = [core.arena[:, 4096 * b:4096 * (b + 1)].rearrange("p (n c) -> p n c", n=4) for b in range(4)]
    rows = core.scratch[0:32, 0:4 * BANK].rearrange("p (b n) -> p b n", b=4)
    turned = core.scratch[0:32, 4 * BANK:5 * BANK]
    with nc.Block() as block:
        @block.sync
        def _(sp):
            with sp.Fori(0, chunks // 4) as turn:
                for b in range(4):
                    sp.wait_ge(used.sem, turn * 4 + used.at(b + 1))
                    sp.dma_start(buffers[b], tiles[turn * 4 + b]).then_inc(sig(f"chunk{b}_loaded").sem, 16)

        @block.scalar
        def _(act):
            nc.scalar.activation(core.silu[:], core.col("c"), ACT.Silu).then_inc(silu_kept.sem, 1)
            act.wait_ge(sig("rows_cleared").sem, 1)
            with act.Fori(0, chunks // 4) as turn:
                for b in range(4):
                    act.wait_ge(summed.sem, turn * 4 + summed.at(b + 1))
                    act.wait_ge(turned_.sem, turn * 4 + turned_.at(b + 1))
                    nc.scalar.activation(rows[0:1, b, :], core.bank[b][0:1, :], ACT.Identity).then_inc(kept.sem, 1)

        @block.tensor
        def _(pe):
            pe.wait_ge(silu_kept.sem, silu_kept.at(1))
            with pe.Fori(0, chunks // 4) as turn:
                for b in range(4):
                    pe.wait_ge(sig(f"chunk{b}_loaded").sem, turn * 16 + 16)
                    pe.wait_ge(kept.sem, turn * 4 + kept.at(b + 1))
                    modulation_blocks(core, pe, [buffers[b][:, n] for n in range(4)], core.bank[b]).then_inc(summed.sem, 1)
                    nc.tensor.matmul(core.bank[7][0:1, 0:1], core.silu[:, 0:1], core.silu[:, 0:1], start=True, stop=True) \
                        .then_inc(used.sem, 1)

        @block.vector
        def _(dve):
            link = Chain(step, dve)
            nc.vector.memset(rows, 0.0).then_inc(sig("rows_cleared").sem, 1)
            for n in range(chunks):
                dve.wait_ge(kept.sem, kept.at(4 + n + 1))
                link(row_to_columns(core, link, rows[:, n % 4, :], turned, core.mod[:, 0, :], 4 * n, 4))
                nc.vector.memset(core.work[:, 500:501], 0.0).then_inc(turned_.sem, 1)
            modulation_gains(core, dve, link, 0)
            step.used = link.n

    step.close(step.used)
    silu_kept.close(1)
    for s in (used, summed, kept, turned_):
        s.close(chunks)


def transposes(core, pe, src, dst_banks, raised):
    for n, block in enumerate(src):
        mm = core.nc.tensor.transpose(dst_banks[n // 4][:, (n % 4) * P:(n % 4 + 1) * P], block, core.c("ident"))
        if n % 4 == 3 or n == len(src) - 1:
            mm.then_inc(raised.sem, 1)


def token_major(core, jobs):
    nc, sig = core.nc, core.sig
    turned, kept = sig("turned"), sig("turned_kept")
    groups = []
    for src, dst in jobs:
        blocks = src.shape[1]
        for t in range(TT):
            for b in range(0, blocks, 4):
                groups.append((src, dst, t, b))
    with nc.Block() as block:
        @block.tensor
        def _(pe):
            for n, (src, dst, t, b) in enumerate(groups):
                if n >= 4:
                    pe.wait_ge(kept.sem, kept.at(n - 3))
                transposes(core, pe, [src[:, b + i, t * P:(t + 1) * P] for i in range(4)], [core.bank[n % 4]], turned)

        @block.scalar
        def _(act):
            for n, (src, dst, t, b) in enumerate(groups):
                act.wait_ge(turned.sem, turned.at(n + 1))
                nc.scalar.activation(dst[:, t, b * P:(b + 4) * P], core.bank[n % 4][:], ACT.Identity).then_inc(kept.sem, 1)
    turned.close(len(groups))
    kept.close(len(groups))


def even_mixer(core):
    nc, sig, A = core.nc, core.sig, core.arena
    proj = view(A, 2048, 12, T)
    core.linear("scalar", core.copy_to(proj))
    u, v, p = proj[:, 0:4], proj[:, 4:8], proj[:, 8:12]
    gelus = sig("gelus_ready")
    centred, squares, tokens = view(A, 5120, 4, T), view(A, 6144, 4, T), view(A, 7168, 2, 4 * P)
    spatial, bias = view(A, 8192, 4, P), view(A, 8704, 4, P)
    ping, pong = view(A, 9216, 4, T + 16), view(A, 10304, 4, T + 16)
    pooled, inv_count, w_pool = view(A, 11392, 4, T), A[:, 12416:13440], view(A, 13440, 4, P)
    mask, cat = A[:, 13952:14080], view(A, 14336, 8, T)
    step, loaded = sig("dve_step"), sig("small_loaded")
    n = [0]
    mean, var = core.bank[4][:, 0:T], core.bank[5][:, 0:T]
    means, cent, vars_, rooted = sig("mean_ready"), sig("centred_squared"), sig("variance_ready"), sig("rooted")
    wide = [P, 4, T]
    root = core.work[:, 0:T]
    with nc.Block() as block:
        @block.sync
        def _(sp):
            n[0] = core.load(sp, [(spatial, "ev_w_s"), (bias, "ev_b_s"), (inv_count, "inv_count"),
                                    (w_pool, "ev_w_pool"), (mask, "even_mask")])

        @block.tensor
        def _(pe):
            pe.wait_ge(gelus.sem, gelus.at(1))
            for g in range(4):
                mm = nc.tensor.matmul(mean, core.c("ones"), v[:, g, :], start=(g == 0), stop=(g == 3))
            mm.then_inc(means.sem, 1)
            pe.wait_ge(cent.sem, cent.at(1))
            for g in range(4):
                mm = nc.tensor.matmul(var, core.c("ones"), squares[:, g, :], start=(g == 0), stop=(g == 3))
            mm.then_inc(vars_.sem, 1)

        @block.scalar
        def _(act):
            nc.scalar.activation(v, v, ACT.Gelu).then_inc(gelus.sem, 1)
            nc.scalar.activation(u, u, ACT.Gelu)
            act.wait_ge(vars_.sem, vars_.at(1))
            nc.scalar.activation(root, var, ACT.Sqrt, bias=core.c("eps"), scale=1.0 / 512).then_inc(rooted.sem, 1)

        @block.vector
        def _(dve):
            link = Chain(step, dve)
            dve.wait_ge(means.sem, means.at(1))
            link(nc.vector.scalar_tensor_tensor(out=centred, in0=mean.unsqueeze(1).to_broadcast(wide), scalar=-1.0 / 512,
                                                in1=v, op0=ALU.mult, op1=ALU.add))
            nc.vector.tensor_tensor(squares, centred, centred, ALU.mult).then_inc(cent.sem, 1)
            link(nc.vector.memset(ping[:, :, 0:16], 0.0))
            link(nc.vector.memset(pong[:, :, 0:16], 0.0))
            link(nc.vector.tensor_copy(ping[:, :, 16:], p))
            src, dst = ping, pong
            for g in range(4):
                shift = 1 << g
                link(nc.vector.tensor_tensor(dst[:, g:4, 16:], src[:, g:4, 16:], src[:, g:4, 16 - shift:16 - shift + T], ALU.add))
                link(nc.vector.tensor_tensor(pooled[:, g, :], dst[:, g, 16:], dst[:, g, 16:], ALU.max))
                src, dst = dst, src
            dve.wait_ge(loaded.sem, loaded.at(16 * 5))
            link(nc.vector.tensor_tensor(pooled, pooled, inv_count.rearrange("p (g t) -> p g t", g=4), ALU.mult))
            link(nc.vector.tensor_tensor(pooled, pooled, p, ALU.subtract))
            link(nc.vector.tensor_tensor(spatial, spatial, mask.unsqueeze(1).to_broadcast([P, 4, P]), ALU.mult))
            dve.wait_ge(rooted.sem, rooted.at(1))
            link(nc.vector.reciprocal(root, root))
            link(nc.vector.tensor_tensor(centred, centred, root.unsqueeze(1).to_broadcast(wide), ALU.mult))
            step.used = link.n
    step.close(step.used)
    for s in (means, cent, vars_, rooted, gelus):
        s.close(1)
    loaded.close(n[0])
    token_major(core, [(centred, tokens)])
    mixed, pools = sig("spatial_mixed"), sig("pool_mixed")
    with nc.Block() as block:
        @block.tensor
        def _(pe):
            for t in range(TT):
                for g in range(4):
                    mm = nc.tensor.matmul(core.bank[t][:, g * P:(g + 1) * P], tokens[:, t, g * P:(g + 1) * P],
                                          spatial[:, g, :], start=True, stop=True)
                mm.then_inc(mixed.sem, 1)
            for g in range(4):
                mm = nc.tensor.matmul(core.bank[4 + g][:, 0:T], w_pool[:, g, :], pooled[:, g, :], start=True, stop=True)
                mm.then_inc(pools.sem, 1)

        @block.vector
        def _(dve):
            link = Chain(step, dve)
            for t in range(TT):
                dve.wait_ge(mixed.sem, mixed.at(t + 1))
                for g in range(4):
                    nc.vector.scalar_tensor_tensor(out=cat[:, g, t * P:(t + 1) * P], in0=core.bank[t][:, g * P:(g + 1) * P],
                                                   scalar=core.col("ev_g_v", g), in1=bias[:, g, :], op0=ALU.mult, op1=ALU.add)
            link(nc.vector.memset(core.work[:, 500:501], 0.0))
            nc.vector.tensor_tensor(cat[:, 0:4], cat[:, 0:4], u, ALU.mult)
            step.used = link.n

        @block.scalar
        def _(act):
            for g in range(4):
                act.wait_ge(pools.sem, pools.at(g + 1))
                nc.scalar.activation(cat[:, 4 + g, :], core.bank[4 + g][:, 0:T], ACT.Identity, scale=core.col("ev_pool_scale", g))
    step.close(step.used)
    mixed.close(TT)
    pools.close(4)
    core.split(cat, core.h_high, core.h_low)
    core.linear("vector", core.add_to_x(lambda n: core.mod[:, 0, bass.ds(n + 2 * KB, 1)]))


def mixer_norm(core, layer):
    core.norm(core.x, core.gain[:, 2 * layer, :], core.mod[:, layer, 0:KB], view(core.arena, 0, 8, T))


def ffn_norm(core, layer):
    core.norm(core.x, core.gain[:, 2 * layer + 1, :], core.mod[:, layer, 3 * KB:4 * KB], view(core.arena, 0, 8, T))



def peer_queries(core, layer):
    nc, sig, A = core.nc, core.sig, core.arena
    queries, keys = view(A, 0, 16, T), view(A, 4096, 16, KEYS)
    core.linear("scalar", core.copy_to(queries))
    scored, kept, loaded = sig("keys_scored"), sig("key_scores_kept"), sig("small_loaded")
    n = [0]
    with nc.Block() as block:
        @block.sync
        def _(sp):
            n[0] = core.load(sp, [(A[:, 4096:4096 + 16 * KEYS], f"peer_keys{layer}")])

        @block.tensor
        def _(pe):
            pe.wait_ge(loaded.sem, loaded.at(16))
            for g in range(TT * 4):
                t, first = g // 4, (g % 4) * 4
                if g >= 4:
                    pe.wait_ge(kept.sem, kept.at(g - 3))
                for q in range(4):
                    mm = nc.tensor.matmul(core.bank[g % 4][:, q * KEYS:(q + 1) * KEYS],
                                          queries[:, first + q, t * P:(t + 1) * P], keys[:, first + q, :],
                                          start=True, stop=True)
                mm.then_inc(scored.sem, 1)

        @block.scalar
        def _(act):
            for g in range(TT * 4):
                act.wait_ge(scored.sem, scored.at(g + 1))
                nc.scalar.activation(core.arena[:, SCORES_AT + g * BANK:SCORES_AT + (g + 1) * BANK], core.bank[g % 4][:], ACT.Identity) \
                    .then_inc(kept.sem, 1)
    loaded.close(n[0])
    scored.close(8)
    kept.close(8)


def peer_scores(core, layer):
    nc, sig = core.nc, core.sig
    used, free, step, picked = sig("tiles_used"), sig("bank_free"), sig("dve_step"), sig("experts_picked")
    seg, k = core.take_segment()
    acts = view(core.arena, 0, P, T)
    scores = core.arena[:, SCORES_AT:SCORES_AT + 4096].rearrange("p (t h s n) -> p t h s n", t=TT, h=HEADS, s=2)
    b = core.pick
    sums = lambda t: b.sums[:, t].rearrange("p a b -> p (a b)")
    safe = SCORES_AT // T // RING
    with nc.Block() as block:
        @block.sync
        def _(sp):
            core.stream(sp, seg, k)

        @block.tensor
        def _(pe):
            with pe.Fori(0, P // RING) as turn:
                for slot in range(RING):
                    pe.wait_ge(free.sem, turn * RING + free.at(slot + 1 - RING))
                    core.wait_turn(pe, seg, turn, slot)
                    for c in range(KB):
                        mm = core.product(core.bank[slot][:, 0:T], slot, (core.h_high[:, c, :], core.h_low[:, c, :]), c,
                                          c == 0, c == KB - 1)
                    mm.then_inc(used.sem, 1)

        @block.gpsimd
        def _(pool):
            core.paced(pool, seg, RING, RING - 1, lambda i, t: core.make_low(pool, seg, i * RING + (t - t % RING), t % RING),
                       lambda i, t: None)

        @block.scalar
        def _(act):
            def high(i, t):
                core.make_high(act, seg, i * RING + (t - t % RING), t % RING)

            def gelu(i, t):
                act.wait_ge(used.sem, i * RING + (seg.first + RING + t + 1))
                nc.scalar.activation(acts[:, i * RING + t, :], core.bank[t][:, 0:T], ACT.Gelu).then_inc(free.sem, 1)

            for t in range(RING - 1):
                high(0, t)
            with act.Fori(0, safe) as i:
                for t in range(RING):
                    gelu(i, t)
                    high(i, t + RING - 1)
            act.wait_ge(picked.sem, picked.at(1))
            for i in range(safe, P // RING):
                for t in range(RING):
                    gelu(i, t)
                    if i * RING + t + RING - 1 < P:
                        high(i, t + RING - 1)

        @block.vector
        def _(dve):
            link = Chain(step, dve)
            for h in range(HEADS):
                sets = [(t, s, scores[:, t, h, s, :], b.top[:, t, s]) for t in range(TT) for s in range(2)]
                for t, s, keys, top in sets:
                    i = nc.vector.max(top[:, 0:8], keys)
                link(i)
                for t, s, keys, top in sets:
                    i = nc.vector.max_index(b.at[:, t, s, 0:8], top[:, 0:8], keys)
                for t, s, keys, top in sets:
                    i = nc.vector.match_replace(keys, top[:, 0:8], keys, LOWEST)
                link(i)
                for t, s, keys, top in sets:
                    i = nc.vector.max(top[:, 8:16], keys)
                link(i)
                for t, s, keys, top in sets:
                    i = nc.vector.max_index(b.at[:, t, s, 8:16], top[:, 8:16], keys)
                for t in range(TT):
                    i = nc.vector.tensor_tensor(b.sums[:, t], b.top[:, t, 0, :].unsqueeze(2).to_broadcast([P, 16, 16]),
                                                b.top[:, t, 1, :].unsqueeze(1).to_broadcast([P, 16, 16]), ALU.add)
                link(i)
                nc.vector.tensor_copy(b.at_f[:], b.at[:])
                for t in range(TT):
                    i = nc.vector.max(b.best[:, t, 0:8], sums(t))
                link(i)
                for t in range(TT):
                    nc.vector.max_index(b.place[:, t, 0:8], b.best[:, t, 0:8], sums(t))
                for t in range(TT):
                    i = nc.vector.match_replace(sums(t), b.best[:, t, 0:8], sums(t), LOWEST)
                link(i)
                for t in range(TT):
                    i = nc.vector.max(b.best[:, t, 8:16], sums(t))
                link(i)
                for t in range(TT):
                    i = nc.vector.max_index(b.place[:, t, 8:16], b.best[:, t, 8:16], sums(t))
                nc.vector.tensor_tensor(b.expo[:, :, h, :], b.best[:], b.best[:, :, 0:1].to_broadcast([P, TT, 16]), ALU.subtract)
                link(i)
                nc.vector.tensor_scalar(b.digit[:, 0], b.place[:], 4, None, ALU.logical_shift_right)
                link(nc.vector.tensor_scalar(b.digit[:, 1], b.place[:], 15, None, ALU.bitwise_and))
                link(nc.vector.tensor_copy(b.digit_f[:], b.digit[:]))
                iota = core.c("iota16").unsqueeze(1).to_broadcast([P, 16, 16])
                for s in range(2):
                    for t in range(TT):
                        i = nc.vector.tensor_tensor(b.sums[:, t], b.digit_f[:, s, t, :].unsqueeze(2).to_broadcast([P, 16, 16]),
                                                    iota, ALU.is_equal)
                    link(i)
                    for t in range(TT):
                        i = nc.vector.tensor_tensor(b.sums[:, t], b.sums[:, t],
                                                    b.at_f[:, t, s, :].unsqueeze(1).to_broadcast([P, 16, 16]), ALU.mult)
                    link(i)
                    for t in range(TT):
                        i = nc.vector.tensor_reduce(b.chosen[:, s, t, h * TOPK:(h + 1) * TOPK], b.sums[:, t], AX_X, ALU.add)
                    link(i)
            nc.vector.tensor_copy(b.total[:, 0:1], b.best[:, 0, 0:1]).then_inc(picked.sem, 1)
            step.used = link.n
    step.close(step.used)
    picked.close(1)
    free.close(P)


def peer_gates(core, layer):
    nc, sig, b = core.nc, core.sig, core.pick
    exped, gated, turned, step = sig("gates_exped"), sig("gates_ready"), sig("turned"), sig("dve_step")
    gates = b.expo[:].rearrange("p t h k -> p (t h) k")
    total = b.total[:]
    with nc.Block() as block:
        @block.scalar
        def _(act):
            nc.scalar.activation(b.expo[:], b.expo[:], ACT.Exp).then_inc(exped.sem, 1)

        @block.vector
        def _(dve):
            link = Chain(step, dve)
            dve.wait_ge(exped.sem, exped.at(1))
            link(nc.vector.tensor_reduce(total, gates, AX_X, ALU.add))
            link(nc.vector.reciprocal(total, total))
            nc.vector.tensor_tensor(gates, gates, total.unsqueeze(2).to_broadcast([P, TT * HEADS, TOPK]), ALU.mult) \
                .then_inc(gated.sem, 1)
            step.used = link.n
            for n in range(3):
                dve.wait_ge(turned.sem, turned.at(n + 1))
                nc.vector.tensor_copy(b.by_pick[:, n, :], core.bank[n][:, 0:T])

        @block.tensor
        def _(pe):
            for n in range(3):
                if n == 2:
                    pe.wait_ge(gated.sem, gated.at(1))
                    src = [b.expo[:, t].rearrange("p h k -> p (h k)") for t in range(TT)]
                else:
                    src = [b.chosen[:, n, t, :] for t in range(TT)]
                transposes(core, pe, src, [core.bank[n]], turned)
    step.close(step.used)
    turned.close(3)
    exped.close(1)
    gated.close(1)


def peer_weigh(core, layer):
    nc, sig, b = core.nc, core.sig, core.pick
    seconds, firsts, spread, taken = (sig(n) for n in ("seconds_ready", "firsts_ready", "gates_spread", "gates_taken"))
    distant, negated, step = sig("distances_ready"), sig("firsts_negated"), sig("dve_step")
    acts = view(core.arena, 0, P, T)
    first, second, gate = (b.by_pick[:, n, :] for n in range(3))
    hot_first, hot_second = view(core.scratch, 0, 8, P), view(core.scratch, 1024, 8, P)
    iota = core.c("iota")
    turns, groups = T // 16, 4
    beside = layer == 0
    row_summed, row_kept, row_turned, block_used = (sig(n) for n in ("next_row_ready", "next_row_kept", "next_row_turned", "next_block_used"))
    blocks = [core.spare[:, n, :] for n in range(3)]
    row, turned = core.scratch[0:32, 2048:2048 + 3 * P], core.scratch[0:32, 2560:2560 + 3 * P]
    with nc.Block() as block:
        def scatter(turn):
            parts = turned.rearrange("p (n g i) -> p n g i", n=3, g=4)
            for g in range(4):
                i = nc.vector.tensor_copy(core.mod[32 * g:32 * g + 32, 1, bass.ds(turn * 3, 3)], parts[:, :, g, 0])
            return i

        if beside:
            @block.sync
            def _(sp):
                with sp.Fori(0, turns) as turn:
                    for n in range(3):
                        sp.wait_ge(block_used.sem, turn + block_used.at(1))
                        sp.dma_start(blocks[n], core.dram["ada_w1"][turn * 3 + n]).then_inc(sig(f"next_block{n}_loaded").sem, 16)

        @block.scalar
        def _(act):
            act.wait_ge(negated.sem, negated.at(1))
            with act.Fori(0, turns) as turn:
                for g in range(groups):
                    act.wait_ge(spread.sem, turn * groups + spread.at(g + 1))
                    part = hot_first[:, 4 * (g % 2):4 * (g % 2) + 4, :]
                    for u in range(4):
                        i = nc.scalar.activation(part[:, u, :], iota, ACT.Abs, bias=first[:, bass.ds(turn * 16 + 4 * g + u, 1)])
                    i.then_inc(distant.sem, 1)
                    act.wait_ge(distant.sem, turn * groups + distant.at(g + 1))
                    nc.scalar.activation(part, part, ACT.Relu, bias=core.c("ones")[:, 0:1], scale=-1.0).then_inc(firsts.sem, 1)
                if beside:
                    act.wait_ge(row_summed.sem, turn + row_summed.at(1))
                    act.wait_ge(row_turned.sem, turn + row_turned.at(1))
                    nc.scalar.activation(row[0:1, :], core.bank[5][0:1, 0:3 * P], ACT.Identity).then_inc(row_kept.sem, 1)

        @block.vector
        def _(dve):
            link = Chain(step, dve)
            link(nc.vector.memset(row, 0.0))
            nc.vector.tensor_scalar(first, first, -1.0, None, ALU.mult).then_inc(negated.sem, 1)
            step.used = link.n

            def onehots(turn, g):
                dve.wait_ge(spread.sem, turn * groups + spread.at(g + 1))
                for u in range(4):
                    token = turn * 16 + 4 * g + u
                    i = nc.vector.tensor_scalar(hot_second[:, 4 * (g % 2) + u, :], iota, second[:, bass.ds(token, 1)],
                                                gate[:, bass.ds(token, 1)], ALU.is_equal, ALU.mult)
                i.then_inc(seconds.sem, 1)

            def weigh(turn, g):
                dve.wait_ge(spread.sem, turn * groups + spread.at(g + 3))
                part = acts[:, :, bass.ds(turn * 16 + 4 * g, 4)]
                nc.vector.tensor_tensor(part, part, core.bank[g][:].rearrange("p (u i) -> p i u", u=4), ALU.mult) \
                    .then_inc(taken.sem, 1)

            onehots(0, 0)

            def turn_body(turn, last):
                for g in range(groups):
                    if not (last and g == groups - 1):
                        onehots(turn, g + 1)
                    weigh(turn, g)

            with dve.Fori(0, turns - 1) as turn:
                turn_body(turn, False)
                if beside:
                    dve.wait_ge(row_kept.sem, turn + row_kept.at(2))
                    nc.vector.transpose(turned, row).then_inc(row_turned.sem, 1)
                    dve.wait_ge(row_turned.sem, turn + row_turned.at(2))
                    scatter(turn)
            turn_body(turns - 1, True)
            if beside:
                dve.wait_ge(row_kept.sem, row_kept.at(turns + 1))
                nc.vector.transpose(turned, row).then_inc(row_turned.sem, 1)
                dve.wait_ge(row_turned.sem, row_turned.at(turns + 1))
                link(scatter(turns - 1))
                modulation_gains(core, dve, link, 1)
                step.used = link.n

        @block.tensor
        def _(pe):
            with pe.Fori(0, turns) as turn:
                for g in range(groups):
                    pe.wait_ge(seconds.sem, turn * groups + seconds.at(g + 1))
                    pe.wait_ge(firsts.sem, turn * groups + firsts.at(g + 1))
                    pe.wait_ge(taken.sem, turn * groups + taken.at(g + 1))
                    for u in range(4):
                        mm = nc.tensor.matmul(core.bank[g][:, u * P:(u + 1) * P], hot_second[:, 4 * (g % 2) + u, :],
                                              hot_first[:, 4 * (g % 2) + u, :], start=True, stop=True)
                    mm.then_inc(spread.sem, 1)
                    if beside and g < 3:
                        pe.wait_ge(sig(f"next_block{g}_loaded").sem, turn * 16 + 16)
                        if g == 0:
                            pe.wait_ge(row_kept.sem, turn + row_kept.at(1))
                        mm = modulation_blocks(core, pe, [blocks[g]], core.bank[5][:, g * P:(g + 1) * P])
                        if g == 2:
                            mm.then_inc(row_summed.sem, 1)
                            nc.tensor.matmul(core.bank[7][0:1, 0:1], core.silu[:, 0:1], core.silu[:, 0:1], start=True, stop=True) \
                                .then_inc(block_used.sem, 1)
    step.close(step.used)
    negated.close(1)
    for s in (seconds, firsts, spread, taken, distant):
        s.close(turns * groups)


def peer_output(core, layer):
    nc, sig = core.nc, core.sig
    used, summed, rounded, split = sig("tiles_used"), sig("experts_summed"), sig("act_rounded"), sig("act_split")
    seg, k = core.take_segment()
    acts = view(core.arena, 0, P, T)
    out = [core.bank[4 + d // 2][:, (d % 2) * T:(d % 2 + 1) * T] for d in range(KB)]
    with nc.Block() as block:
        @block.sync
        def _(sp):
            core.stream(sp, seg, k)

        @block.tensor
        def _(pe):
            for d in range(4):
                nc.tensor.matmul(core.bank[4 + d][:], core.c("zeros"), core.const[:, 0:BANK], start=True, stop=False,
                                 skip_group_check=True)
            with pe.Fori(0, P // RING) as turn:
                for slot in range(RING):
                    core.wait_turn(pe, seg, turn, slot)
                    pe.wait_ge(split.sem, turn * RING + split.at(slot + 1))
                    x = (core.act_high[:, slot, :], core.act_low[:, slot, :])
                    for d in range(KB):
                        mm = core.product(out[d], slot, x, d, False, False)
                    mm.then_inc(used.sem, 1)
            for d in range(4):
                mm = nc.tensor.matmul(core.bank[4 + d][:], core.c("zeros"), core.const[:, 0:BANK], start=False, stop=True,
                                      skip_group_check=True)
            mm.then_inc(summed.sem, 1)

        def high(act):
            def make(i, t):
                core.make_high(act, seg, i * RING + (t - t % RING), t % RING)
                nc.scalar.activation(core.act_high[:, t % RING, :], acts[:, i * RING + t, :], ACT.Identity).then_inc(rounded.sem, 1)
            return make

        @block.scalar
        def _(act):
            def pace(i, t):
                act.wait_ge(used.sem, i * RING + (seg.first + RING + t + 1))
            core.paced(act, seg, RING, RING - 1, high(act), pace)

        @block.vector
        def _(dve):
            def make(i, t):
                dve.wait_ge(rounded.sem, i * RING + rounded.at(t + 1))
                slot = t % RING
                nc.vector.tensor_tensor(core.act_low[:, slot, :], acts[:, i * RING + t, :], core.act_high[:, slot, :].bitcast(F32),
                                        ALU.subtract).then_inc(split.sem, 1)
                if slot % 2 == 0:
                    core.make_low(dve, seg, i * RING + (t - slot), slot)

            core.paced(dve, seg, RING, RING - 1, make, lambda i, t: None)
            dve.wait_ge(summed.sem, summed.at(1))
            for d in range(KB):
                core.add_to_x(lambda n: core.mod[:, layer, 5 * KB + n:5 * KB + n + 1])(d, out[d])

        @block.gpsimd
        def _(pool):
            def make(i, t):
                if t % 2:
                    core.make_low(pool, seg, i * RING + (t - t % RING), t % RING)
            core.paced(pool, seg, RING, RING - 1, make, lambda i, t: None)
    summed.close(1)
    rounded.close(P)
    split.close(P)


def peer(core, layer):
    ffn_norm(core, layer)
    peer_queries(core, layer)
    peer_scores(core, layer)
    peer_gates(core, layer)
    peer_weigh(core, layer)
    peer_output(core, layer)


def rope(core, src, dst, pairs, cos, sin):
    nc, sig = core.nc, core.sig
    swapped, taken, straight = sig("halves_swapped"), sig("halves_taken"), sig("straight_ready")
    step = sig("dve_step")
    two = [P, 2, T]
    cosb, sinb = (a.unsqueeze(1).to_broadcast(two) for a in (cos, sin))
    side = core.scratch[:, 0:4 * BANK].rearrange("p (b n t) -> p b n t", b=4, n=2)
    with nc.Block() as block:
        @block.tensor
        def _(pe):
            for n in range(pairs):
                if n >= 4:
                    pe.wait_ge(taken.sem, taken.at(n - 3))
                nc.tensor.matmul(core.bank[n % 4][:], core.c("rot"), src[:, 2 * n:2 * n + 2, :], start=True, stop=True) \
                    .then_inc(swapped.sem, 1)

        @block.gpsimd
        def _(pool):
            for n in range(pairs):
                nc.gpsimd.tensor_tensor(dst[:, 2 * n:2 * n + 2, :], src[:, 2 * n:2 * n + 2, :], cosb, ALU.mult) \
                    .then_inc(straight.sem, 1)

        @block.vector
        def _(dve):
            link = Chain(step, dve)
            for n in range(pairs):
                dve.wait_ge(swapped.sem, swapped.at(n + 1))
                i = nc.vector.tensor_tensor(side[:, n % 4], core.bank[n % 4][:].rearrange("p (n t) -> p n t", n=2), sinb, ALU.mult)
                i.then_inc(taken.sem, 1)
                dve.wait_ge(taken.sem, taken.at(n + 1))
                dve.wait_ge(straight.sem, straight.at(n + 1))
                part = dst[:, 2 * n:2 * n + 2, :]
                nc.vector.tensor_tensor(part, part, side[:, n % 4], ALU.add)
            step.used = link.n
    step.close(step.used)
    for s in (swapped, taken, straight):
        s.close(pairs)


def block_rms(core, src, blocks, ones, count, eps, squares, root, centre=None):
    nc, sig = core.nc, core.sig
    step, meaned, squared, summed, rooted = (sig(n) for n in ("dve_step", "mean_ready", "squared", "square_sums", "rooted"))
    flat = lambda a: a.rearrange("p n t -> p (n t)")
    banks = blocks // 2
    src_f, squares_f, root_f = flat(src), flat(squares), flat(root)
    with nc.Block() as block:
        @block.tensor
        def _(pe):
            if centre is not None:
                for n in range(banks):
                    nc.tensor.matmul(core.bank[n][:], core.c(ones), src_f[:, n * BANK:(n + 1) * BANK], start=True, stop=True) \
                        .then_inc(meaned.sem, 1)
            for n in range(banks):
                pe.wait_ge(squared.sem, squared.at(n + 1))
                nc.tensor.matmul(core.bank[4 + n][:], core.c(ones), squares_f[:, n * BANK:(n + 1) * BANK], start=True, stop=True) \
                    .then_inc(summed.sem, 1)

        @block.scalar
        def _(act):
            for n in range(banks):
                act.wait_ge(summed.sem, summed.at(n + 1))
                nc.scalar.activation(root_f[:, n * BANK:(n + 1) * BANK], core.bank[4 + n][:], ACT.Sqrt, bias=eps,
                                     scale=1.0 / count).then_inc(rooted.sem, 1)

        @block.vector
        def _(dve):
            link = Chain(step, dve)
            for n in range(banks):
                part = slice(n * BANK, (n + 1) * BANK)
                if centre is not None:
                    dve.wait_ge(meaned.sem, meaned.at(n + 1))
                    link(nc.vector.scalar_tensor_tensor(out=flat(centre)[:, part], in0=core.bank[n][:], scalar=-1.0 / count,
                                                        in1=src_f[:, part], op0=ALU.mult, op1=ALU.add))
                    nc.vector.tensor_tensor(squares_f[:, part], flat(centre)[:, part], flat(centre)[:, part], ALU.mult) \
                        .then_inc(squared.sem, 1)
                else:
                    nc.vector.tensor_tensor(squares_f[:, part], src_f[:, part], src_f[:, part], ALU.mult).then_inc(squared.sem, 1)
            for n in range(banks):
                part = slice(n * BANK, (n + 1) * BANK)
                dve.wait_ge(rooted.sem, rooted.at(n + 1))
                nc.vector.reciprocal(root_f[:, part], root_f[:, part])
            step.used = link.n
    step.close(step.used)
    meaned.close(banks if centre is not None else 0)
    for s in (squared, summed, rooted):
        s.close(banks)


def odd_mixer(core):
    nc, sig, A = core.nc, core.sig, core.arena
    proj, turned, tokens, o = view(A, 0, 24, T), view(A, 6144, 16, T), view(A, 10240, 2, 8 * P), view(A, 12288, 8, T)
    squares, root = view(A, 14336, 8, T), view(A, 16384, 8, T)
    mask = A[:, 18432:18432 + 384]
    probs = A[:, 18816:18816 + 2 * 768].rearrange("p (b m k) -> p b m k", b=2, m=2)
    combined, combined_T = view(A, 20352, 2, 384), view(A, 21120, 2, 384)
    lam = A[:, 21888:21888 + 256].rearrange("p (n d) -> p n d", n=4)
    peak, total, minus_lam = A[:, 22144:22152], A[:, 22152:22160], A[:, 22160:22164]
    product, gain = A[:, 22164:22164 + 64], A[:, 22228:22229]
    core.linear("scalar", core.copy_to(proj))
    rope(core, proj[:, 0:16], turned, 8, core.trig[:, 1, :], core.trig[:, 0, :])
    token_major(core, [(proj[:, 16:24], tokens)])

    step, loaded, act_step = sig("dve_step"), sig("small_loaded"), sig("lam_exped")
    n = [0]
    with nc.Block() as block:
        @block.sync
        def _(sp):
            n[0] = core.load(sp, [(mask, "attn_mask"), (lam, "od_lam")])

        @block.vector
        def _(dve):
            link = Chain(step, dve)
            dve.wait_ge(loaded.sem, loaded.at(32))
            for i in range(2):
                link(nc.vector.tensor_tensor(product, lam[:, 2 * i], lam[:, 2 * i + 1], ALU.mult))
                link(nc.vector.tensor_reduce(minus_lam[:, i:i + 1], product, AX_X, ALU.add))
            nc.vector.tensor_scalar(gain, core.col("od_g_sub"), 1.0 - LAM_INIT, None, ALU.mult).then_inc(sig("lam_summed").sem, 1)
            dve.wait_ge(act_step.sem, act_step.at(1))
            link(nc.vector.tensor_tensor(minus_lam[:, 3:4], minus_lam[:, 1:2], minus_lam[:, 0:1], ALU.subtract))
            link(nc.vector.tensor_scalar(minus_lam[:, 3:4], minus_lam[:, 3:4], LAM_INIT, None, ALU.subtract))
            step.used = link.n

        @block.scalar
        def _(act):
            act.wait_ge(sig("lam_summed").sem, sig("lam_summed").at(1))
            nc.scalar.activation(minus_lam[:, 0:2], minus_lam[:, 0:2], ACT.Exp).then_inc(act_step.sem, 1)
    step.close(step.used)
    loaded.close(n[0])
    act_step.close(1)
    sig("lam_summed").close(1)

    scored, peaked, exped, weighed, flipped, kept, mixed = (sig(x) for x in (
        "heads_scored", "heads_peaked", "heads_exped", "heads_weighed", "heads_flipped", "flips_kept", "heads_mixed"))
    scored_taken, mixed_taken = sig("scores_taken"), sig("mixed_taken")
    sums = lambda m, i: total[:, 2 * i + m:2 * i + m + 1]
    minus_peak = lambda m, i: peak[:, 2 * i + m:2 * i + m + 1]
    span = (slice(0, P), slice(P, 3 * P))
    with nc.Block() as block:
        @block.tensor
        def _(pe):
            def scores(h):
                if h >= 2:
                    pe.wait_ge(scored_taken.sem, scored_taken.at(h - 1))
                for m in range(2):
                    half = slice(64 * m, 64 * m + 64)
                    for i in range(2):
                        mm = nc.tensor.matmul(core.bank[2 * (h % 2) + m][:, span[i]], turned[half, h, i * P:(i + 1) * P],
                                              turned[half, 8 + h, 0:(i + 1) * P], start=True, stop=True)
                mm.then_inc(scored.sem, 1)

            scores(0)
            for h in range(HEADS):
                if h + 1 < HEADS:
                    scores(h + 1)
                pe.wait_ge(weighed.sem, weighed.at(h + 1))
                if h >= 2:
                    pe.wait_ge(kept.sem, kept.at(h - 1))
                w = combined[:, h % 2, :]
                flips = core.bank[4 + h % 2]
                for c, at in ((0, 0), (1, 1), (2, 2)):
                    mm = nc.tensor.transpose(flips[:, at * P:(at + 1) * P], w[:, c * P:(c + 1) * P], core.c("ident"))
                mm.then_inc(flipped.sem, 1)
                pe.wait_ge(kept.sem, kept.at(h + 1))
                if h >= 2:
                    pe.wait_ge(mixed_taken.sem, mixed_taken.at(h - 1))
                out = core.bank[6 + h % 2]
                v = tokens[:, :, h * P:(h + 1) * P]
                nc.tensor.matmul(out[:, 0:T], v[:, 0, :], combined_T[:, h % 2, 0:T], start=True, stop=False)
                nc.tensor.matmul(out[:, P:T], v[:, 1, :], combined_T[:, h % 2, T:3 * P], start=False, stop=True) \
                    .then_inc(mixed.sem, 1)

        @block.vector
        def _(dve):
            link = Chain(step, dve)

            def peaks(h):
                dve.wait_ge(scored.sem, scored.at(h + 1))
                s = probs[:, h % 2]
                for m in range(2):
                    i = nc.vector.scalar_tensor_tensor(out=s[:, m], in0=core.bank[2 * (h % 2) + m][:, 0:384], scalar=0.125,
                                                       in1=mask, op0=ALU.mult, op1=ALU.add)
                i.then_inc(scored_taken.sem, 1)
                dve.wait_ge(scored_taken.sem, scored_taken.at(h + 1))
                nc.vector.tensor_reduce(peak[:, 0:2], s[:, :, 0:P], AX_X, ALU.max)
                link(nc.vector.tensor_reduce(peak[:, 2:4], s[:, :, P:3 * P], AX_X, ALU.max))
                nc.vector.tensor_scalar(peak[:, 0:4], peak[:, 0:4], -1.0, None, ALU.mult).then_inc(peaked.sem, 1)

            for h in range(HEADS):
                peaks(h)
                dve.wait_ge(exped.sem, exped.at(h + 1))
                s = probs[:, h % 2]
                link(nc.vector.reciprocal(total[:, 0:4], total[:, 0:4]))
                for i in range(2):
                    j = nc.vector.tensor_tensor(sums(1, i), sums(1, i), minus_lam[:, 3:4], ALU.mult)
                link(j)
                for i in range(2):
                    j = nc.vector.tensor_scalar(s[:, 1, span[i]], s[:, 1, span[i]], sums(1, i), None, ALU.mult)
                link(j)
                if h >= 2:
                    dve.wait_ge(flipped.sem, flipped.at(h - 1))
                for i in range(2):
                    j = nc.vector.scalar_tensor_tensor(out=combined[:, h % 2, span[i]], in0=s[:, 0, span[i]], scalar=sums(0, i),
                                                       in1=s[:, 1, span[i]], op0=ALU.mult, op1=ALU.add)
                j.then_inc(weighed.sem, 1)
            step.used = link.n

        @block.scalar
        def _(act):
            for h in range(HEADS + 1):
                if h < HEADS:
                    act.wait_ge(peaked.sem, peaked.at(h + 1))
                    s = probs[:, h % 2]
                    for m in range(2):
                        for i in range(2):
                            j = nc.scalar.activation(s[:, m, span[i]], s[:, m, span[i]], ACT.Exp, bias=minus_peak(m, i),
                                                     accum_out=sums(m, i))
                    j.then_inc(exped.sem, 1)
                if h >= 1:
                    act.wait_ge(mixed.sem, mixed.at(h))
                    nc.scalar.activation(o[:, h - 1, :], core.bank[6 + (h - 1) % 2][:, 0:T], ACT.Identity).then_inc(mixed_taken.sem, 1)
                if h < HEADS:
                    act.wait_ge(flipped.sem, flipped.at(h + 1))
                    src, dst = core.bank[4 + h % 2], combined_T[:, h % 2]
                    nc.scalar.activation(dst, src[:, 0:384], ACT.Identity).then_inc(kept.sem, 1)
    step.close(step.used)
    for s in (scored, peaked, exped, weighed, flipped, kept, mixed, scored_taken, mixed_taken):
        s.close(HEADS)

    block_rms(core, o, 8, "ones", P, core.c("eps"), squares, root)
    with nc.Block() as block:
        @block.vector
        def _(dve):
            nc.vector.scalar_tensor_tensor(out=o, in0=o, scalar=gain, in1=root, op0=ALU.mult, op1=ALU.mult)
    core.split(o, core.h_high, core.h_low)
    core.linear("vector", core.add_to_x(lambda n: core.mod[:, 1, bass.ds(n + 2 * KB, 1)]))


def norm_in_place(core, gain):
    core.norm(core.x, core.col(gain), None, view(core.arena, 0, 8, T), dst=core.x)



def second_projection(core):
    core.linear("scalar", core.copy_to(view(core.arena, 0, 32, T)))


def scaled_and_shifted(core, dst, src, gain, bias):
    for b in range(4):
        i = core.nc.vector.tensor_scalar(dst[:, b, :], src[:, b, :], core.col(gain, b), core.col(bias, b), ALU.mult, ALU.add)
    return i


def retention(core):
    nc, sig, A = core.nc, core.sig, core.arena
    proj, turned, tokens = view(A, 0, 31, T), view(A, 10496, 8, T), view(A, 12544, 2, 4 * P)
    decay, scores = view(A, 13568, 8, 3 * P), view(A, 16640, 8, 3 * P)
    y, cat = view(A, 19712, 4, T), view(A, 20736, 8, T)
    rope(core, proj[:, 0:8], turned, 4, core.trig[:, 3, :], core.trig[:, 2, :])
    token_major(core, [(proj[:, 8:12], tokens)])
    scored, decayed, mixed, loaded = sig("heads_scored"), sig("heads_weighed"), sig("heads_mixed"), sig("small_loaded")
    n = [0]
    with nc.Block() as block:
        @block.sync
        def _(sp):
            n[0] = core.load(sp, [(A[:, 13568:13568 + 8 * 384], "decay")])

        @block.tensor
        def _(pe):
            for h in range(8):
                half = slice(64 * (h % 2), 64 * (h % 2) + 64)
                if h >= 4:
                    pe.wait_ge(decayed.sem, decayed.at(h - 3))
                q, k = turned[half, h // 2, :], turned[half, 4 + h // 2, :]
                nc.tensor.matmul(core.bank[h % 4][:, 0:T], k[:, 0:P], q, start=True, stop=True)
                nc.tensor.matmul(core.bank[h % 4][:, T:3 * P], k[:, P:T], q[:, P:T], start=True, stop=True).then_inc(scored.sem, 1)
            for h in range(8):
                half = slice(64 * (h % 2), 64 * (h % 2) + 64)
                pe.wait_ge(decayed.sem, decayed.at(h + 1))
                out = core.bank[4 + h // 2][half]
                nc.tensor.matmul(out[:, 0:T], tokens[:, 0, h * 64:(h + 1) * 64], scores[:, h, 0:T], start=True, stop=False,
                                 skip_group_check=True)
                nc.tensor.matmul(out[:, P:T], tokens[:, 1, h * 64:(h + 1) * 64], scores[:, h, T:3 * P], start=False, stop=True,
                                 skip_group_check=True).then_inc(mixed.sem, 1)

        @block.vector
        def _(dve):
            dve.wait_ge(loaded.sem, loaded.at(16))
            for h in range(8):
                dve.wait_ge(scored.sem, scored.at(h + 1))
                nc.vector.tensor_tensor(scores[:, h, :], core.bank[h % 4][:, 0:3 * P], decay[:, h, :], ALU.mult) \
                    .then_inc(decayed.sem, 1)

        @block.scalar
        def _(act):
            for b in range(4):
                act.wait_ge(mixed.sem, mixed.at(2 * b + 2))
                nc.scalar.activation(y[:, b, :], core.bank[4 + b][:, 0:T], ACT.Identity)
    loaded.close(n[0])
    for s in (scored, decayed, mixed):
        s.close(8)
    centred, squares, root = view(A, 13568, 4, T), view(A, 14592, 4, T), view(A, 15616, 4, T)
    block_rms(core, y, 4, "half_ones", 64, core.c("eps_ret"), squares, root, centre=centred)
    gated, step = sig("gate_activated"), sig("dve_step")
    with nc.Block() as block:
        @block.scalar
        def _(act):
            nc.scalar.activation(squares, proj[:, 12:16], ACT.Silu).then_inc(gated.sem, 1)

        @block.vector
        def _(dve):
            link = Chain(step, dve)
            link(nc.vector.tensor_tensor(centred, centred, root, ALU.mult))
            link(scaled_and_shifted(core, centred, centred, "ret_gn_w_2", "ret_gn_b_2"))
            dve.wait_ge(gated.sem, gated.at(1))
            nc.vector.tensor_tensor(cat[:, 0:4], centred, squares, ALU.mult)
            step.used = link.n
    step.close(step.used)
    gated.close(1)


def rwkv(core):
    nc, sig, A = core.nc, core.sig, core.arena
    proj, cat = view(A, 0, 31, T), view(A, 20736, 8, T)
    step, act_step = sig("dve_step"), sig("act_step")
    spots = [8192 + 1024 * i for i in range(12)] + [22784 + 1024 * i for i in range(9)]
    area = lambda i, n=1: view(A, spots[i], 4 * n, T)
    shifted = view(A, 8192, 15, T)
    r, k, v = proj[:, 16:20], proj[:, 20:24], proj[:, 24:28]
    low = proj[:, 28]
    up, g_up, g_up_tail = A[:, 31744:31744 + 512], A[:, 32256:32768], core.scratch[0:32, 3584:4096]
    loaded = sig("small_loaded")
    n = [0]

    with nc.Block() as block:
        @block.sync
        def _(sp):
            n[0] = core.load(sp, [(up, "rwkv_up"), (g_up, "rwkv_g_up"), (g_up_tail, "rwkv_g_up_tail")])

        @block.vector
        def _(dve):
            link = Chain(step, dve)
            for blocks, rows in ((slice(0, 14), slice(0, P)), (slice(14, 15), slice(0, 32))):
                p = proj[rows, 16:31][:, blocks]
                d = shifted[rows, blocks]
                nc.vector.tensor_tensor(d[:, :, 1:T], p[:, :, 0:T - 1], p[:, :, 1:T], ALU.subtract)
                link(nc.vector.tensor_scalar(d[:, :, 0:1], p[:, :, 0:1], -1.0, None, ALU.mult))
            for b in range(15):
                rows = slice(0, P) if b < 14 else slice(0, 32)
                mu = core.col("rwkv_mu_2", b) if b < 14 else core.col("rwkv_mu_tail")
                link(nc.vector.scalar_tensor_tensor(out=proj[rows, 16 + b, :], in0=shifted[rows, b, :], scalar=mu[rows],
                                                    in1=proj[rows, 16 + b, :], op0=ALU.mult, op1=ALU.add))
            step.used = link.n
    step.close(step.used)
    loaded.close(n[0])

    sig_w, a, gate, kk, squares, norm = area(0), area(2), area(3), area(4), area(5), area(6)
    hidden, sums = sig("hidden_ready"), sig("low_rank_ready")
    with nc.Block() as block:
        @block.scalar
        def _(act):
            nc.scalar.activation(low[0:64], low[0:64], ACT.Tanh)
            nc.scalar.activation(proj[:, 29], proj[:, 29], ACT.Sigmoid)
            nc.scalar.activation(proj[0:32, 30], proj[0:32, 30], ACT.Sigmoid).then_inc(hidden.sem, 1)
            for b in range(4):
                act.wait_ge(sums.sem, sums.at(b + 1))
                nc.scalar.activation(sig_w[:, b, :], core.bank[b][:, 0:T], ACT.Sigmoid, bias=core.col("rwkv_w0_2", b))
                nc.scalar.activation(a[:, b, :], core.bank[4 + b][:, 0:T], ACT.Sigmoid, bias=core.col("rwkv_a0_2", b))
                nc.scalar.activation(gate[:, b, :], core.bank[b][:, T:2 * T], ACT.Identity)

        @block.tensor
        def _(pe):
            pe.wait_ge(hidden.sem, hidden.at(1))
            for b in range(4):
                c = slice(b * P, (b + 1) * P)
                nc.tensor.matmul(core.bank[b][:, 0:T], up[0:64, c], low[0:64], start=True, stop=True)
                nc.tensor.matmul(core.bank[4 + b][:, 0:T], up[64:P, c], low[64:P], start=True, stop=True)
                nc.tensor.matmul(core.bank[b][:, T:2 * T], g_up[:, c], proj[:, 29], start=True, stop=False)
                nc.tensor.matmul(core.bank[b][:, T:2 * T], g_up_tail[:, c], proj[0:32, 30], start=False, stop=True) \
                    .then_inc(sums.sem, 1)

        @block.vector
        def _(dve):
            for b in range(4):
                nc.vector.tensor_scalar(kk[:, b, :], k[:, b, :], core.col("rwkv_k_k_2", b), None, ALU.mult)
    hidden.close(1)
    sums.close(4)
    squared, summed, rooted = sig("squared"), sig("square_sums"), sig("rooted")
    flat = lambda x: x.rearrange("p n t -> p (n t)")
    decay_sum, decay_log = area(1), area(0)
    reset = flat(area(7))
    cols = [0]
    with nc.Block() as block:
        @block.sync
        def _(sp):
            cols[0] = core.load(sp, [(reset, "reset")])

        @block.vector
        def _(dve):
            link = Chain(step, dve)
            nc.vector.tensor_tensor(squares, kk, kk, ALU.mult).then_inc(squared.sem, 1)
            link(nc.vector.tensor_scalar(decay_log, sig_w, -math.exp(-0.5), None, ALU.mult))
            dve.wait_ge(loaded.sem, loaded.at(16))
            link(nc.vector.tensor_tensor_scan(flat(decay_sum), reset, flat(decay_log), 0.0, ALU.mult, ALU.add))
            dve.wait_ge(rooted.sem, rooted.at(1))
            link(nc.vector.tensor_scalar(norm, norm, 1e-12, None, ALU.max))
            link(nc.vector.reciprocal(norm, norm))
            link(nc.vector.tensor_tensor(kk, kk, norm, ALU.mult))
            for b in range(4):
                i = nc.vector.tensor_scalar(squares[:, b, :], a[:, b, :], 1.0, core.col("rwkv_k_a_2", b), ALU.subtract, ALU.mult)
            link(i)
            link(nc.vector.scalar_tensor_tensor(out=k, in0=squares, scalar=1.0, in1=k, op0=ALU.add, op1=ALU.mult))
            link(nc.vector.tensor_tensor(a, kk, a, ALU.mult))
            step.used = link.n

        @block.tensor
        def _(pe):
            pe.wait_ge(squared.sem, squared.at(1))
            for i in range(2):
                mm = nc.tensor.matmul(core.bank[i][:], core.c("half_ones"), flat(squares)[:, i * BANK:(i + 1) * BANK], start=True, stop=True)
            mm.then_inc(summed.sem, 1)

        @block.scalar
        def _(act):
            act.wait_ge(summed.sem, summed.at(1))
            for i in range(2):
                j = nc.scalar.activation(flat(norm)[:, i * BANK:(i + 1) * BANK], core.bank[i][:], ACT.Sqrt)
            j.then_inc(rooted.sem, 1)
    step.close(step.used)
    loaded.close(cols[0])
    for s in (squared, summed, rooted):
        s.close(1)
    b_vec = a

    upto, before, inverse, rest = area(7), area(8), area(9), area(10)
    a_in, b_out, k_out, r_in, b_end, k_end = area(5), area(6), area(9), area(7), area(11), area(12)
    logs = area(13)
    chunks = lambda x: x.rearrange("p n (c t) -> p (n c) t", t=CHUNK)
    exped = sig("decays_exped")
    with nc.Block() as block:
        @block.vector
        def _(dve):
            link = Chain(step, dve)
            link(nc.vector.tensor_tensor(before, decay_sum, decay_log, ALU.subtract))
            last = chunks(decay_sum)[:, :, CHUNK - 1:CHUNK].to_broadcast([P, 16, CHUNK])
            nc.vector.tensor_tensor(chunks(rest), last, chunks(decay_sum), ALU.subtract).then_inc(exped.sem, 1)
            dve.wait_ge(exped.sem, exped.at(5))
            link(nc.vector.scalar_tensor_tensor(out=a_in, in0=kk, scalar=-1.0, in1=before, op0=ALU.mult, op1=ALU.mult))
            link(nc.vector.tensor_tensor(b_out, b_vec, inverse, ALU.mult))
            link(nc.vector.tensor_tensor(k_out, k, inverse, ALU.mult))
            link(nc.vector.tensor_tensor(b_end, b_vec, rest, ALU.mult))
            link(nc.vector.tensor_tensor(k_end, k, rest, ALU.mult))
            link(nc.vector.tensor_copy(core.work[:, 0:16], chunks(upto)[:, :, CHUNK - 1]))
            for b in range(4):
                i = nc.vector.scalar_tensor_tensor(out=logs[:, b, :], in0=r[:, b, :], scalar=core.col("rwkv_r_k_2", b),
                                                   in1=k[:, b, :], op0=ALU.mult, op1=ALU.mult)
            link(i)
            link(nc.vector.tensor_tensor(r_in, r, upto, ALU.mult))
            step.used = link.n

        @block.scalar
        def _(act):
            act.wait_ge(exped.sem, exped.at(1))
            for dst, src, scale in ((upto, decay_sum, 1.0), (before, before, 1.0), (inverse, decay_sum, -1.0), (rest, rest, 1.0)):
                nc.scalar.activation(dst, src, ACT.Exp, scale=scale).then_inc(exped.sem, 1)
    step.close(step.used)
    exped.close(5)
    bonus_terms = logs

    a_tok, b_tok, k_tok, v_tok = (view(A, spots[i], 2, 4 * P) for i in (0, 1, 2, 14))
    token_major(core, [(a_in, a_tok), (b_end, b_tok), (k_end, k_tok), (v, v_tok)])

    wide = lambda at: view(A, at, 8, P)
    masks = view(core.scratch, 2048, 8, P)
    NT, inv, inv_T = wide(spots[8]), wide(spots[10]), wide(spots[11])
    M1, LT = wide(spots[12]), wide(spots[15])
    RB, RK = wide(spots[16]), wide(spots[17])
    LV, both = view(core.scratch, 0, 8, 64), wide(spots[18])
    M_T, Q, R2, y = area(19), area(4), area(20), view(core.scratch, 1024, 4, T)
    M_T_c = M_T.rearrange("p n (c k) -> p n c k", c=CHUNKS)
    Q_c = Q.rearrange("p n (c k) -> p n c k", c=CHUNKS)
    with nc.Block() as block:
        @block.sync
        def _(sp):
            n[0] = core.load(sp, [(core.scratch[:, 2048:2048 + 8 * P], "rwkv_masks")])
    loaded.close(n[0])
    eye2 = core.c("eye2")
    full, out_ready = sig("products_ready"), sig("products_kept")

    def tile(t):
        tk = slice(t * P, (t + 1) * P)
        half = lambda h: slice(64 * (h % 2), 64 * (h % 2) + 64)
        hc = lambda h: slice(h * 64, (h + 1) * 64)
        mask = lambda i: masks[:, i, :].unsqueeze(1).to_broadcast([P, 4, P])
        kinds = [(b_out, a_in, NT, 6), (k_out, a_in, LT, 6), (b_out, r_in, RB, 7), (k_out, r_in, RK, 7)]
        bank4 = lambda i: core.bank[i][:].rearrange("p (h k) -> p h k", h=4)
        with nc.Block() as block:
            @block.tensor
            def _(pe):
                for n, (left, right, _, _) in enumerate(kinds):
                    for g in range(2):
                        for h in range(g, 8, 2):
                            mm = nc.tensor.matmul(core.bank[2 * n + g][:, (h // 2) * P:(h // 2 + 1) * P], left[half(h), h // 2, tk],
                                                  right[half(h), h // 2, tk], start=True, stop=True)
                        mm.then_inc(full.sem, 1)

            @block.vector
            def _(dve):
                for n, (_, _, dst, which) in enumerate(kinds):
                    for g in range(2):
                        dve.wait_ge(full.sem, full.at(2 * n + g + 1))
                        nc.vector.tensor_tensor(dst[:, g:8:2, :], bank4(2 * n + g), mask(which), ALU.mult)

            @block.gpsimd
            def _(pool):
                for g in range(8):
                    nc.gpsimd.tensor_copy(inv[:, g, :], core.c("ident"))
                    nc.gpsimd.tensor_copy(inv_T[:, g, :], core.c("ident"))
        full.close(8)

        with nc.Block() as block:
            @block.tensor
            def _(pe):
                for level in range(6):
                    for g in range(2):
                        if level:
                            pe.wait_ge(out_ready.sem, out_ready.at(4 * (level - 1) + 2 + g + 1))
                        for h in range(4 * g, 4 * g + 4):
                            mm = nc.tensor.matmul(core.bank[g][:, (h % 4) * P:(h % 4 + 1) * P], NT[:, h, :], inv[:, h, :],
                                                  start=True, stop=True)
                        mm.then_inc(full.sem, 1)
                    for g in range(2):
                        pe.wait_ge(out_ready.sem, out_ready.at(4 * level + g + 1))
                        for h in range(4 * g, 4 * g + 4):
                            c = slice((h % 4) * P, (h % 4 + 1) * P)
                            nc.tensor.matmul(core.bank[2 + g][:, c], inv_T[:, h, :], M1[:, h, :], start=True, stop=True)
                            mm = nc.tensor.matmul(core.bank[4 + g][:, c], M1[:, h, :], inv_T[:, h, :], start=True, stop=True)
                        mm.then_inc(full.sem, 1)

            @block.vector
            def _(dve):
                for level in range(6):
                    for g in range(2):
                        dve.wait_ge(full.sem, full.at(4 * level + g + 1))
                        nc.vector.tensor_tensor(M1[:, 4 * g:4 * g + 4, :], bank4(g), mask(level), ALU.mult).then_inc(out_ready.sem, 1)
                    for g in range(2):
                        dve.wait_ge(full.sem, full.at(4 * level + 2 + g + 1))
                        s = slice(4 * g, 4 * g + 4)
                        nc.vector.tensor_tensor(inv[:, s, :], inv[:, s, :], bank4(2 + g), ALU.add)
                        nc.vector.tensor_tensor(inv_T[:, s, :], inv_T[:, s, :], bank4(4 + g), ALU.add).then_inc(out_ready.sem, 1)
        full.close(24)
        out_ready.close(24)

        with nc.Block() as block:
            @block.tensor
            def _(pe):
                for h in range(8):
                    mm = nc.tensor.matmul(core.bank[0][:, hc(h)], LT[:, h, :], v_tok[:, t, hc(h)], start=True, stop=True)
                mm.then_inc(full.sem, 1)
                for g in range(2):
                    for h in range(4 * g, 4 * g + 4):
                        at = (h % 4) * P
                        mm = nc.tensor.matmul(core.bank[1 + g][:, at + 64:at + P], inv_T[:, h, :], a_tok[:, t, hc(h)], start=True, stop=True)
                pe.wait_ge(out_ready.sem, out_ready.at(1))
                for g in range(2):
                    for h in range(4 * g, 4 * g + 4):
                        at = (h % 4) * P
                        mm = nc.tensor.matmul(core.bank[1 + g][:, at:at + 64], inv_T[:, h, :], LV[:, h, :], start=True, stop=True)
                    mm.then_inc(full.sem, 1)
                pe.wait_ge(out_ready.sem, out_ready.at(3))
                for c in range(2):
                    rows = slice(64 * c, 64 * c + 64)
                    for h in range(8):
                        at = slice((h // 2) * 64, (h // 2) * 64 + 64)
                        nc.tensor.matmul(core.bank[3 + c][half(h), at], both[rows, h, 64:P], b_tok[rows, t, hc(h)],
                                         start=True, stop=True, skip_group_check=True)
                    for h in range(8):
                        at = slice(T + (h // 2) * 64, T + (h // 2) * 64 + 64)
                        nc.tensor.matmul(core.bank[3 + c][half(h), at], b_tok[rows, t, hc(h)], both[rows, h, 0:64],
                                         start=True, stop=False, skip_group_check=True)
                        mm = nc.tensor.matmul(core.bank[3 + c][half(h), at], k_tok[rows, t, hc(h)], v_tok[rows, t, hc(h)],
                                              start=False, stop=True, skip_group_check=True)
                    mm.then_inc(full.sem, 1)
                for h in range(8):
                    at = slice((h // 2) * P, (h // 2 + 1) * P)
                    nc.tensor.matmul(core.bank[5][half(h), at], both[:, h, 64:P], RB[:, h, :], start=True, stop=True,
                                     skip_group_check=True)
                    nc.tensor.matmul(core.bank[6][half(h), at], both[:, h, 0:64], RB[:, h, :], start=True, stop=False,
                                     skip_group_check=True)
                    mm = nc.tensor.matmul(core.bank[6][half(h), at], v_tok[:, t, hc(h)], RK[:, h, :], start=False, stop=True,
                                          skip_group_check=True)
                mm.then_inc(full.sem, 1)

            @block.vector
            def _(dve):
                dve.wait_ge(full.sem, full.at(1))
                nc.vector.tensor_copy(LV, core.bank[0][:].rearrange("p (h k) -> p h k", h=8)).then_inc(out_ready.sem, 1)
                for g in range(2):
                    dve.wait_ge(full.sem, full.at(2 + g))
                    nc.vector.tensor_copy(both[:, 4 * g:4 * g + 4, :], bank4(1 + g)).then_inc(out_ready.sem, 1)
                for c in range(2):
                    dve.wait_ge(full.sem, full.at(4 + c))
                    chunk = 2 * t + c
                    for b in range(4):
                        nc.vector.scalar_tensor_tensor(out=M_T_c[:, b, chunk, :], in0=eye2,
                                                       scalar=core.work[:, b * CHUNKS + chunk:b * CHUNKS + chunk + 1],
                                                       in1=core.bank[3 + c][:, b * 64:(b + 1) * 64], op0=ALU.mult, op1=ALU.add)
                    nc.vector.tensor_copy(Q_c[:, :, chunk, :], core.bank[3 + c][:, T:2 * T].rearrange("p (n k) -> p n k", n=4))
                dve.wait_ge(full.sem, full.at(6))
                nc.vector.tensor_tensor(R2[:, :, tk], r_in[:, :, tk], bank4(5), ALU.add)
                nc.vector.tensor_copy(y[:, :, tk], bank4(6))
        full.close(6)
        out_ready.close(3)

    for t in range(TT):
        tile(t)

    states = view(A, spots[8], 12, 64)
    state = lambda c: states[:, 4 * (c - 1):4 * c, :]
    part = lambda h: slice(64 * (h % 2), 64 * (h % 2) + 64)
    with nc.Block() as block:
        @block.tensor
        def _(pe):
            for c in range(1, CHUNKS):
                pe.wait_ge(out_ready.sem, out_ready.at(c))
                if c < CHUNKS - 1:
                    for h in range(8):
                        mm = nc.tensor.matmul(core.bank[c][part(h), (h // 2) * 64:(h // 2) * 64 + 64], M_T_c[part(h), h // 2, c, :],
                                              state(c)[part(h), h // 2, :], start=True, stop=True, skip_group_check=True)
                    mm.then_inc(full.sem, 1)
                for h in range(8):
                    mm = nc.tensor.matmul(core.bank[3 + c][part(h), (h // 2) * 64:(h // 2) * 64 + 64], state(c)[part(h), h // 2, :],
                                          R2[part(h), h // 2, c * CHUNK:(c + 1) * CHUNK], start=True, stop=True, skip_group_check=True)
                mm.then_inc(full.sem, 1)

        @block.vector
        def _(dve):
            bank64 = lambda i: core.bank[i][:, 0:T].rearrange("p (n k) -> p n k", n=4)
            nc.vector.tensor_copy(state(1), Q_c[:, :, 0, :]).then_inc(out_ready.sem, 1)
            count = 0
            for c in range(1, CHUNKS):
                if c < CHUNKS - 1:
                    count += 1
                    dve.wait_ge(full.sem, full.at(count))
                    nc.vector.tensor_tensor(state(c + 1), bank64(c), Q_c[:, :, c, :], ALU.add).then_inc(out_ready.sem, 1)
                count += 1
                dve.wait_ge(full.sem, full.at(count))
                out = y[:, :, c * CHUNK:(c + 1) * CHUNK]
                nc.vector.tensor_tensor(out, out, bank64(3 + c), ALU.add)
    full.close(5)
    out_ready.close(3)

    centred, squares, root = area(0), area(1), area(2)
    block_rms(core, y, 4, "half_ones", 64, core.c("eps_rwkv"), squares, root, centre=centred)
    with nc.Block() as block:
        @block.tensor
        def _(pe):
            for i in range(2):
                mm = nc.tensor.matmul(core.bank[i][:], core.c("half_ones"), flat(bonus_terms)[:, i * BANK:(i + 1) * BANK],
                                      start=True, stop=True)
            mm.then_inc(full.sem, 1)

        @block.vector
        def _(dve):
            link = Chain(step, dve)
            link(nc.vector.tensor_tensor(centred, centred, root, ALU.mult))
            link(scaled_and_shifted(core, centred, centred, "rwkv_gn_w_2", "rwkv_gn_b_2"))
            dve.wait_ge(full.sem, full.at(1))
            for i in range(2):
                j = nc.vector.tensor_tensor(flat(squares)[:, i * BANK:(i + 1) * BANK], core.bank[i][:],
                                            flat(v)[:, i * BANK:(i + 1) * BANK], ALU.mult)
            link(j)
            link(nc.vector.tensor_tensor(centred, centred, squares, ALU.add))
            nc.vector.tensor_tensor(cat[:, 4:8], centred, gate, ALU.mult)
            step.used = link.n
    step.close(step.used)
    full.close(1)


def second_mixer(core):
    second_projection(core)
    retention(core)
    rwkv(core)
    core.split(view(core.arena, 20736, 8, T), core.h_high, core.h_low)
    core.linear("vector", core.add_to_x())



def cross_attention(core):
    nc, sig, A = core.nc, core.sig, core.arena
    scratch, mem, q, kv = view(A, 0, 8, T), view(A, 2048, 8, T), view(A, 4096, 8, T), view(A, 6144, 16, T)
    tokens, o = view(A, 10240, 2, D), view(A, 12288, 8, T)
    probs, probs_T = view(A, 14336, 4, T), view(A, 15360, 4, T)
    small = A[:, 16384:16384 + 16]
    loaded, step = sig("small_loaded"), sig("dve_step")
    core.norm(core.x, core.col("norm_xattn_2"), None, scratch)
    core.linear("scalar", core.copy_to(q))
    n = [0]
    with nc.Block() as block:
        @block.sync
        def _(sp):
            n[0] = core.load(sp, [(mem, "mem")])
    loaded.close(n[0])
    core.norm(mem, core.col("norm_mem_2"), None, scratch)
    core.linear("scalar", core.copy_to(kv))
    token_major(core, [(kv[:, 8:16], tokens)])
    scored, peaked, exped, weighed, flipped, kept, mixed, mixed_taken = (sig(x) for x in (
        "heads_scored", "heads_peaked", "heads_exped", "heads_weighed", "heads_flipped", "flips_kept", "heads_mixed", "mixed_taken"))
    scale = 1.0 / 16
    with nc.Block() as block:
        @block.tensor
        def _(pe):
            def scores(h):
                if h >= 2:
                    pe.wait_ge(exped.sem, exped.at(h - 1))
                for i in range(2):
                    for b in range(2):
                        mm = nc.tensor.matmul(core.bank[h % 2][:, i * T:(i + 1) * T], q[:, 2 * h + b, i * P:(i + 1) * P],
                                              kv[:, 2 * h + b, :], start=(b == 0), stop=(b == 1))
                mm.then_inc(scored.sem, 1)

            scores(0)
            for h in range(4):
                if h + 1 < 4:
                    scores(h + 1)
                pe.wait_ge(weighed.sem, weighed.at(h + 1))
                if h >= 2:
                    pe.wait_ge(kept.sem, kept.at(h - 1))
                for m in range(2):
                    for i in range(2):
                        mm = nc.tensor.transpose(core.bank[2 + h % 2][:, m * T + i * P:m * T + (i + 1) * P],
                                                 probs[:, 2 * (h % 2) + i, m * P:(m + 1) * P], core.c("ident"))
                mm.then_inc(flipped.sem, 1)
                pe.wait_ge(kept.sem, kept.at(h + 1))
                if h >= 2:
                    pe.wait_ge(mixed_taken.sem, mixed_taken.at(h - 1))
                for b in range(2):
                    for m in range(2):
                        mm = nc.tensor.matmul(core.bank[4 + h % 2][:, b * T:(b + 1) * T],
                                              tokens[:, m, (2 * h + b) * P:(2 * h + b + 1) * P], probs_T[:, 2 * (h % 2) + m, :],
                                              start=(m == 0), stop=(m == 1))
                mm.then_inc(mixed.sem, 1)

        @block.vector
        def _(dve):
            link = Chain(step, dve)
            for h in range(4):
                dve.wait_ge(scored.sem, scored.at(h + 1))
                link(nc.vector.tensor_reduce(small[:, 0:2], core.bank[h % 2][:].rearrange("p (i m) -> p i m", i=2), AX_X, ALU.max))
                nc.vector.tensor_scalar(small[:, 2:4], small[:, 0:2], -scale, None, ALU.mult).then_inc(peaked.sem, 1)
                dve.wait_ge(exped.sem, exped.at(h + 1))
                link(nc.vector.reciprocal(small[:, 4:6], small[:, 4:6]))
                for i in range(2):
                    p = probs[:, 2 * (h % 2) + i, :]
                    j = nc.vector.tensor_scalar(p, p, small[:, 4 + i:5 + i], None, ALU.mult)
                j.then_inc(weighed.sem, 1)
            step.used = link.n

        @block.scalar
        def _(act):
            for h in range(5):
                if h < 4:
                    act.wait_ge(peaked.sem, peaked.at(h + 1))
                    if h >= 2:
                        act.wait_ge(flipped.sem, flipped.at(h - 1))
                    for i in range(2):
                        j = nc.scalar.activation(probs[:, 2 * (h % 2) + i, :], core.bank[h % 2][:, i * T:(i + 1) * T], ACT.Exp,
                                                 bias=small[:, 2 + i:3 + i], scale=scale, accum_out=small[:, 4 + i:5 + i])
                    j.then_inc(exped.sem, 1)
                if h >= 1:
                    act.wait_ge(mixed.sem, mixed.at(h))
                    nc.scalar.activation(o[:, 2 * h - 2:2 * h, :], core.bank[4 + (h - 1) % 2][:].rearrange("p (b t) -> p b t", b=2),
                                         ACT.Identity).then_inc(mixed_taken.sem, 1)
                if h < 4:
                    act.wait_ge(flipped.sem, flipped.at(h + 1))
                    s = slice(2 * (h % 2), 2 * (h % 2) + 2)
                    nc.scalar.activation(probs_T[:, s, :], core.bank[2 + h % 2][:].rearrange("p (m t) -> p m t", m=2),
                                         ACT.Identity).then_inc(kept.sem, 1)
    step.close(step.used)
    for s in (scored, peaked, exped, weighed, flipped, kept, mixed, mixed_taken):
        s.close(4)
    core.split(o, core.h_high, core.h_low)
    core.linear("vector", core.add_to_x())


def mlp(core):
    nc = core.nc
    hidden = view(core.arena, 2048, 32, T)
    core.norm(core.x, core.col("norm_mlp_2"), None, view(core.arena, 0, 8, T))
    positive = core.sig("positive_part")

    def squared_relu(n, bank):
        part = hidden[:, n, :]
        nc.vector.tensor_scalar(part, bank, 0.0, None, ALU.max).then_inc(positive.sem, 1)
        nc.vector.wait_ge(positive.sem, n + positive.at(1))
        return nc.vector.tensor_tensor(part, part, bank, ALU.mult)

    core.linear("vector", squared_relu)
    positive.close(32)
    core.split(hidden, core.hidden_high, core.hidden_low)
    core.linear("vector", core.add_to_x(), groups=4, rhs=(core.hidden_high, core.hidden_low))
    core.norm(core.x, core.col("norm_final_2"), None, view(core.arena, 0, 8, T), dst=core.x)


def column_blocks(w):

    k, n = w.shape
    w = w.reshape(k // D, KB, P, n // P, P).transpose(3, 0, 2, 1, 4)
    return np.ascontiguousarray(w.reshape(-1, P, KB * P))


def columns(*vectors):
    return np.concatenate([np.asarray(v).reshape(-1, P).T for v in vectors], axis=1)


def tokens_last(a):
    return np.ascontiguousarray(a.reshape(T, KB, P).transpose(2, 1, 0))


def layouts(i):
    out = dict(shape_constants())
    names = []

    def add(name, v):
        v = np.asarray(v).reshape(-1, P).T
        at = COLS_AT[0]
        COLS[name] = (at, at + v.shape[1])
        COLS_AT[0] += v.shape[1]
        names.append(v)

    COLS_AT = [0]
    add("c", i["c"])
    for layer in range(2):
        add(f"ada_b{layer}", i["ada_b"][layer])
        add(f"norm_mix{layer}", i["norm_mix"][layer])
        add(f"norm_ffn{layer}", i["norm_ffn"][layer])
    add("ev_g_v", i["ev_g_v"])
    add("ev_pool_scale", i["ev_pool_scale"])
    add("od_g_sub", i["od_g_sub"])
    for name in ("final_norm", "norm_mix_2", "ret_gn_w_2", "ret_gn_b_2", "rwkv_w0_2", "rwkv_a0_2", "rwkv_k_k_2",
                 "rwkv_k_a_2", "rwkv_r_k_2", "rwkv_gn_w_2", "rwkv_gn_b_2", "norm_xattn_2", "norm_mem_2", "norm_mlp_2",
                 "norm_final_2"):
        add(name, i[name])
    mu = np.asarray(i["rwkv_mu_2"]).reshape(-1)
    add("rwkv_mu_2", mu[:14 * P])
    add("rwkv_mu_tail", np.concatenate([mu[14 * P:]] * 4))
    out["cols"] = np.ascontiguousarray(np.concatenate(names, axis=1))
    out["x"] = tokens_last(i["x"])
    out["mem"] = tokens_last(i["mem_2"])
    out["positions"] = np.ascontiguousarray(np.tile(np.concatenate(
        [i["positions"].reshape(1, T), i["positions_2"].reshape(1, T)], axis=1), (P, 1)))
    for layer in range(2):
        out[f"ada_w{layer}"] = column_blocks(i["ada_w"][layer])
        out[f"peer_w_q{layer}"] = column_blocks(i["peer_w_q"][layer].reshape(D, -1))
        out[f"peer_keys{layer}"] = np.ascontiguousarray(i["peer_sub_keys"][layer].transpose(3, 0, 1, 2)).reshape(P, -1)
        out[f"peer_u{layer}"] = column_blocks(i["peer_u"][layer].T)
        out[f"peer_v{layer}"] = np.ascontiguousarray(i["peer_v"][layer].reshape(P, P, D))
    out["ev_w_in"] = column_blocks(i["ev_w_in"][0])
    out["ev_w_s"] = np.ascontiguousarray(i["ev_w_s"][0].transpose(2, 0, 1))
    out["ev_b_s"] = np.ascontiguousarray(np.tile(i["ev_b_s"].reshape(1, 4, P), (P, 1, 1)))
    out["ev_w_pool"] = np.ascontiguousarray(i["ev_w_pool"][0].transpose(1, 0, 2))
    out["ev_w_out"] = column_blocks(i["ev_w_out"][0])
    out["od_w_in"] = column_blocks(i["od_w_in"][0])
    out["od_w_out"] = column_blocks(i["od_w_out"][0])
    out["od_lam"] = np.ascontiguousarray(np.tile(np.stack(
        [i[f"od_lam_{n}"].reshape(64) for n in ("q1", "k1", "q2", "k2")])[None], (P, 1, 1)))
    w_in = np.asarray(i["w_in_2"][0])
    out["w_in_2"] = column_blocks(np.pad(w_in, ((0, 0), (0, 32 * P - w_in.shape[1]))))
    out["rwkv_up"] = np.ascontiguousarray(np.concatenate([i["rwkv_w_up_2"][0], i["rwkv_a_up_2"][0]]))
    out["rwkv_g_up"] = np.ascontiguousarray(i["rwkv_g_up_2"][0][:P])
    out["rwkv_g_up_tail"] = np.ascontiguousarray(i["rwkv_g_up_2"][0][P:])
    out["w_out_2"] = column_blocks(i["w_out_2"][0])
    out["xattn_w_q"] = column_blocks(i["xattn_w_q_2"][0])
    out["xattn_w_kv"] = column_blocks(i["xattn_w_kv_2"][0])
    out["xattn_w_o"] = column_blocks(i["xattn_w_o_2"][0])
    out["mlp_w_up"] = column_blocks(i["mlp_w_up_2"][0])
    out["mlp_w_down"] = column_blocks(i["mlp_w_down_2"][0])
    return out


SEGMENTS = ["ev_w_in", "ev_w_out", "peer_w_q0", "peer_u0", "peer_v0", "od_w_in", "od_w_out",
            "peer_w_q1", "peer_u1", "peer_v1", "w_in_2", "w_out_2", "xattn_w_q", "xattn_w_kv", "xattn_w_o",
            "mlp_w_up", "mlp_w_down"]

STEPS = [
    ("setup", setup),
    ("modulation", modulation),
    ("norm0", lambda core: mixer_norm(core, 0)),
    ("even", even_mixer),
    ("peer0", lambda core: peer(core, 0)),
    ("norm1", lambda core: mixer_norm(core, 1)),
    ("odd", odd_mixer),
    ("peer1", lambda core: peer(core, 1)),
    ("first_end", lambda core: norm_in_place(core, "final_norm")),
    ("norm2", lambda core: core.norm(core.x, core.col("norm_mix_2"), None, view(core.arena, 0, 8, T))),
    ("second_mixer", second_mixer),
    ("cross", cross_attention),
    ("mlp", mlp),
]


def store(core, out):
    nc = core.nc
    stored = core.sig("stored")
    with nc.Block() as block:
        @block.sync
        def _(sp):
            sp.dma_start(out, core.x[:]).then_inc(stored.sem, 16)
            sp.wait_ge(stored.sem, 16)


def program(nc, dram, out, steps=STEPS, source=None):
    core = Core(nc, dram)
    for name in SEGMENTS:
        core.add_segment(name)
    for _, step in steps:
        step(core)
    if source is not None:
        source(core)
    store(core, out)
    return core


def kernel(**inputs):
    import numpy as _np
    import concourse.bacc as _bacc
    from concourse import mybir as _mybir
    from concourse.bass_utils import run_bass_kernel_spmd as _run

    nc = _bacc.Bacc("TRN2", target_bir_lowering=False, num_devices=1)
    arrays, dram = {}, {}
    for name, a in layouts({k: _np.asarray(v) for k, v in inputs.items()}).items():
        arrays[f"{name}_dram"] = a
        dram[name] = nc.dram_tensor(f"{name}_dram", a.shape, _mybir.dt.from_np(a.dtype), kind="ExternalInput").ap()
    out = nc.dram_tensor("out_dram", (P, KB, T), F32, kind="ExternalOutput").ap()
    program(nc, dram, out)
    r = _run(nc, [arrays], core_ids=[0])
    return _np.ascontiguousarray(r.results[0]["out_dram"].transpose(2, 1, 0)).reshape(1, T, D)
```

```python
import math

import numpy as np

import concourse.bass as bass
from concourse import mybir

F32 = mybir.dt.float32
F32R = mybir.dt.float32r
I32 = mybir.dt.int32
U32 = mybir.dt.uint32
ALU = mybir.AluOpType
ACT = mybir.ActivationFunctionType
AX_X = mybir.AxisListType.X

P = 128
D = 1024
KB = D // P
T = 256
TT = T // P
BANK = 512
RING = 4
HEADS, TOPK, KEYS = 8, 16, 128
CHUNK = 64
CHUNKS = T // CHUNK
EPS = 1e-6
LAM_INIT = 0.8 - 0.6 * math.exp(-0.3)
LOWEST = -3.0e38
NORM_IDLE = 8
POOL_LOWS = (1, 3, 5)
ROUND = 1.5 * 2.0 ** 23

CONST = {}
COLS = {}


def shape_constants():
    eye = np.eye(P, dtype=np.float32)
    p = np.arange(P)
    same_half = (p[:, None] // 64 == p[None, :] // 64)
    rot = np.zeros((P, P), np.float32)
    for m in range(P):
        if m % 64 < 32:
            rot[m + 32, m] = -1.0
        else:
            rot[m - 32, m] = 1.0
    half = (p % 32).astype(np.float32)
    inv_a = (np.float32(1.0) / (np.float32(10000.0) ** ((2 * half).astype(np.float32) / np.float32(64)))).astype(np.float32)
    inv_b = (np.float32(10000.0) ** (-(half / np.float32(32)))).astype(np.float32)
    parts = [
        ("ident", eye), ("ones", np.ones((P, P))), ("half_ones", same_half), ("rot", rot),
        ("iota", np.tile(p, (P, 1))), ("iota16", np.tile(np.arange(16), (P, 1))),
        ("eye2", np.concatenate([np.eye(64), np.eye(64)])),
        ("inv_freq_a", inv_a[:, None]), ("inv_freq_b", inv_b[:, None]),
        ("eps", np.full((P, 1), EPS)), ("eps_ret", np.full((P, 1), 1e-5)), ("eps_rwkv", np.full((P, 1), 64e-5)),
        ("zeros", np.zeros((P, P))),
    ]
    at = 0
    for name, a in parts:
        CONST[name] = (at, at + a.shape[1])
        at += a.shape[1]
    resident = np.concatenate([np.asarray(a, np.float32) for _, a in parts], axis=1)

    s, t = p[:, None], p[None, :]
    even_mask = (s <= t).astype(np.float32)
    inv_count = np.zeros((P, 4, T), np.float32)
    for g, w in enumerate((2, 4, 8, 16)):
        inv_count[:, g, :] = 1.0 / np.minimum(np.arange(T) + 1, w)
    diag = np.where(t <= s, 0.0, LOWEST).astype(np.float32)
    attn_mask = np.concatenate([diag, np.zeros((P, P), np.float32), diag], axis=1)
    decay = np.zeros((P, 8, 3 * P), np.float64)
    j = p[:, None]
    for h in range(8):
        lg = np.log(1.0 - 2.0 ** (-5.0 - h))
        i0 = np.arange(T)[None, :]
        decay[:, h, 0:T] = np.where(i0 >= j, np.exp(lg * np.maximum(i0 - j, 0)), 0.0) / 8.0
        i1 = np.arange(P)[None, :]
        decay[:, h, T:] = np.where(i1 >= j, np.exp(lg * np.maximum(i1 - j, 0)), 0.0) / 8.0
    levels = []
    for lv in range(6):
        b = 2 ** lv
        levels.append((t // (2 * b) == s // (2 * b)) & (s // b == t // b + 1) & (s // CHUNK == t // CHUNK))
    chunk_same = s // CHUNK == t // CHUNK
    before = (s < t) & chunk_same
    upto = (s <= t) & chunk_same
    rwkv_masks = np.concatenate([np.concatenate(levels, 1), before, upto], 1).astype(np.float32)
    reset = np.ones((P, 4 * T), np.float32)
    reset[:, ::CHUNK] = 0.0
    return {
        "resident": resident, "even_mask": even_mask, "inv_count": inv_count.reshape(P, -1),
        "attn_mask": attn_mask, "decay": decay.reshape(P, -1).astype(np.float32),
        "rwkv_masks": rwkv_masks, "reset": reset,
    }


class Signal:

    def __init__(self, nc, name):
        self.sem = nc.alloc_semaphore(name)
        self.base = 0

    def at(self, n):
        return n + self.base

    def close(self, raised):
        self.base += raised


class Chain:

    def __init__(self, signal, engine):
        self.steps, self.engine, self.n = signal, engine, 0

    def __call__(self, instruction):
        self.n += 1
        instruction.then_inc(self.steps.sem, 1)
        self.engine.wait_ge(self.steps.sem, self.steps.at(self.n))


class Segment:

    def __init__(self, tiles, count, first):
        self.tiles, self.count, self.first = tiles, count, first


def view(t, at, n, w):
    return t[:, at:at + n * w].rearrange("p (n w) -> p n w", w=w)


class Picks:

    def __init__(self, sb):
        self.top = sb("pick_top", [P, TT, 2, TOPK])
        self.at = sb("pick_at", [P, TT, 2, TOPK], U32)
        self.at_f = sb("pick_at_f", [P, TT, 2, TOPK])
        self.sums = sb("pick_sums", [P, TT, TOPK, TOPK])
        self.best = sb("pick_best", [P, TT, TOPK])
        self.place = sb("pick_place", [P, TT, TOPK], U32)
        self.digit = sb("pick_digit", [P, 2, TT, TOPK], U32)
        self.digit_f = sb("pick_digit_f", [P, 2, TT, TOPK])
        self.chosen = sb("pick_chosen", [P, 2, TT, HEADS * TOPK])
        self.expo = sb("pick_expo", [P, TT, HEADS, TOPK])
        self.total = sb("pick_total", [P, TT * HEADS])
        self.by_pick = sb("by_pick", [P, 3, T])


SCORES_AT = 112 * T


class Core:

    def __init__(self, nc, dram):
        self.nc, self.dram = nc, dram
        sb = lambda name, shape, dt=F32: nc.alloc_sbuf_tensor(name, shape, dt)
        aligned = lambda: (nc.sbuf_base + 31) // 32 * 32

        def over(name, shape, dt, start):
            return nc.alloc_sbuf_tensor_at(name, shape, dt, offset=start)

        arena_at = aligned()
        self.arena = sb("arena", [P, P * T])
        self.x = sb("x_T", [P, KB, T])
        h_at = aligned()
        self.h_high = sb("h_high", [P, KB, T], F32R)
        self.h_low = sb("h_low", [P, KB, T], F32R)
        self.scratch = over("scratch", [P, 2 * KB * T], F32, h_at)
        self.act_high = over("act_high", [P, RING, T], F32R, h_at)
        self.act_low = over("act_low", [P, RING, T], F32R, h_at + RING * T * 4)
        self.hidden_high = over("hidden_high", [P, 32, T], F32R, arena_at + 4 * 10240)
        self.hidden_low = over("hidden_low", [P, 32, T], F32R, arena_at + 4 * 18432)
        raw_at = aligned()
        self.raw = sb("weight_raw", [P, RING, KB * P])
        self.low = over("weight_low", [P, RING, KB * P], F32R, raw_at)
        high_at = aligned()
        self.high = sb("weight_high", [P, RING, KB * P], F32R)
        self.spare = over("spare", [P, RING, KB * P], F32, high_at)
        self.work = sb("work", [P, 512])
        self.silu = sb("silu", [P, KB])
        self.const = sb("const", [P, dram["resident"].shape[1]])
        self.cols = sb("cols", [P, dram["cols"].shape[1]])
        self.mod = sb("mod", [P, 2, 48])
        self.gain = sb("gain", [P, 4, KB])
        self.trig = sb("trig", [P, 4, T])
        self.pick = Picks(sb)
        self.bank = [nc.alloc_psum_tensor(f"bank{i}", [P, BANK], F32) for i in range(8)]
        self.flags = {}
        self.segments = []
        self.next_segment = 0

    def sig(self, name):
        if name not in self.flags:
            self.flags[name] = Signal(self.nc, name)
        return self.flags[name]

    def c(self, name):
        a, b = CONST[name]
        return self.const[:, a:b]

    def col(self, name, n=None):
        a, b = COLS[name]
        return self.cols[:, a:b] if n is None else self.cols[:, a + n:a + n + 1]

    def keep_warm(self, count, bank=7):
        for _ in range(count):
            self.nc.tensor.matmul(self.bank[bank][:], self.c("zeros"), self.const[:, 0:BANK], start=True, stop=True)

    def add_segment(self, name):
        tiles = self.dram[name]
        first = self.segments[-1].first + self.segments[-1].count if self.segments else 0
        self.segments.append(Segment(tiles, tiles.shape[0], first))

    def load_tile(self, sp, seg, n, slot):
        sp.wait_ge(self.sig("tiles_used").sem, n + (seg.first + 1))
        sp.dma_start(self.raw[:, slot, :], seg.tiles[n]).then_inc(self.sig(f"slot{slot}_loaded").sem, 16)

    def first_tiles(self, sp, k):
        if k < len(self.segments):
            for slot in range(RING):
                self.load_tile(sp, self.segments[k], slot, slot)

    def stream(self, sp, seg, k):
        if seg.count > RING:
            with sp.Fori(1, seg.count // RING) as g:
                for slot in range(RING):
                    self.load_tile(sp, seg, g * RING + slot, slot)
        self.first_tiles(sp, k + 1)

    def take_segment(self):
        k = self.next_segment
        self.next_segment += 1
        return self.segments[k], k

    def make_high(self, act, seg, n, slot):
        act.wait_ge(self.sig(f"slot{slot}_loaded").sem, n * (16 // RING) + 16 * (seg.first // RING + 1))
        self.nc.scalar.activation(self.high[:, slot, :], self.raw[:, slot, :], ACT.Identity) \
            .then_inc(self.sig("high_ready").sem, 1)

    def make_low(self, eng, seg, n, slot):
        eng.wait_ge(self.sig("high_ready").sem, n + (seg.first + slot + 1))
        eng.tensor_tensor(self.low[:, slot, :], self.raw[:, slot, :], self.high[:, slot, :].bitcast(F32), ALU.subtract) \
            .then_inc(self.sig(f"low{slot}_ready").sem, 1)

    def wait_turn(self, pe, seg, turn, slot):
        pe.wait_ge(self.sig(f"low{slot}_ready").sem, turn + (seg.first // RING + 1))

    def first_parts(self, eng, kind):
        seg = self.segments[self.next_segment]
        for slot in range(RING - 1):
            if kind == "high":
                self.make_high(eng, seg, 0, slot)
            elif slot % 2 == (kind == "odd lows"):
                self.make_low(eng, seg, 0, slot)

    def paced(self, eng, seg, per_turn, ahead, make, finish, every=1, prepared=False):
        turns = seg.count // per_turn
        if not prepared:
            for n in range(ahead):
                make(0, n)

        def turn(i, last):
            for t in range(per_turn):
                if (t + 1) % every == 0:
                    finish(i, t)
                if not (last and t + ahead >= per_turn):
                    make(i, t + ahead)

        if turns > 1:
            with eng.Fori(0, turns - 1) as i:
                turn(i, False)
        turn(turns - 1, True)

    def norm(self, src, gain, shift, scaled, dst=None):
        nc, sig = self.nc, self.sig
        squared, square_act, summed, rooted, step = (sig(n) for n in (
            "squared", "squared_on_act", "square_sums", "rooted", "dve_step"))
        multiplied, rounded = sig("norm_scaled"), sig("norm_rounded")
        sums = self.bank[4][:, 0:T]
        root = self.work[:, 0:T]
        out = scaled if dst is None else dst
        pool_lows = POOL_LOWS if shift is None else ()

        def low(eng, k):
            eng.wait_ge(rounded.sem, rounded.at(k + 1))
            high = self.h_high[:, k, :].bitcast(F32)
            if shift is None:
                eng.tensor_tensor(self.h_low[:, k, :], scaled[:, k, :], high, ALU.subtract)
            else:
                eng.scalar_tensor_tensor(out=self.h_low[:, k, :], in0=scaled[:, k, :], scalar=shift[:, k:k + 1], in1=high,
                                         op0=ALU.add, op1=ALU.subtract)

        with nc.Block() as block:
            @block.vector
            def _(dve):
                link = Chain(step, dve)
                nc.vector.tensor_tensor(scaled[:, 0:2], src[:, 0:2], src[:, 0:2], ALU.mult).then_inc(squared.sem, 1)
                nc.vector.tensor_tensor(scaled[:, 2:5], src[:, 2:5], src[:, 2:5], ALU.mult).then_inc(squared.sem, 1)
                if dst is None:
                    self.first_parts(dve, "even lows")
                dve.wait_ge(rooted.sem, rooted.at(1))
                link(nc.vector.reciprocal(root, root))
                for k in range(KB):
                    nc.vector.scalar_tensor_tensor(out=out[:, k, :], in0=src[:, k, :], scalar=gain[:, k:k + 1], in1=root,
                                                   op0=ALU.mult, op1=ALU.mult).then_inc(multiplied.sem, 1)
                    if dst is None and k >= 2 and k - 2 not in pool_lows:
                        low(dve, k - 2)
                if dst is None:
                    for k in range(KB - 2, KB):
                        if k not in pool_lows:
                            low(dve, k)
                step.used = link.n

            @block.tensor
            def _(pe):
                for k in (0, 1, 5, 6, 7, 2, 3, 4):
                    if k == 0:
                        pe.wait_ge(squared.sem, squared.at(1))
                    elif k == 5:
                        pe.wait_ge(square_act.sem, square_act.at(1))
                    elif k == 2:
                        pe.wait_ge(squared.sem, squared.at(2))
                    mm = nc.tensor.matmul(sums, self.c("ones"), scaled[:, k, :], start=(k == 0), stop=(k == 4))
                mm.then_inc(summed.sem, 1)
                self.keep_warm(NORM_IDLE)

            @block.scalar
            def _(act):
                nc.scalar.activation(scaled[:, 5:8], src[:, 5:8], ACT.Square).then_inc(square_act.sem, 1)
                if dst is None:
                    self.first_parts(act, "high")
                act.wait_ge(summed.sem, summed.at(1))
                nc.scalar.activation(root, sums, ACT.Sqrt, bias=self.c("eps"), scale=1.0 / D).then_inc(rooted.sem, 1)
                if dst is None:
                    for k in range(KB):
                        act.wait_ge(multiplied.sem, multiplied.at(k + 1))
                        bias = 0.0 if shift is None else shift[:, k:k + 1]
                        nc.scalar.activation(self.h_high[:, k, :], scaled[:, k, :], ACT.Identity, bias=bias).then_inc(rounded.sem, 1)

            if dst is None:
                @block.gpsimd
                def _(pool):
                    self.first_parts(pool, "odd lows")
                    for k in pool_lows:
                        low(pool, k)
        step.close(step.used)
        for s, n in ((squared, 2), (square_act, 1), (summed, 1), (rooted, 1), (multiplied, KB)):
            s.close(n)
        if dst is None:
            rounded.close(KB)

    def split(self, src, high, low):
        nc, rounded = self.nc, self.sig("norm_rounded")
        pairs = src.shape[1] // 2
        with nc.Block() as block:
            @block.scalar
            def _(act):
                self.first_parts(act, "high")
                for n in range(pairs):
                    nc.scalar.activation(high[:, 2 * n:2 * n + 2, :], src[:, 2 * n:2 * n + 2, :], ACT.Identity).then_inc(rounded.sem, 1)

            @block.vector
            def _(dve):
                self.first_parts(dve, "even lows")
                for n in range(pairs):
                    dve.wait_ge(rounded.sem, rounded.at(n + 1))
                    nc.vector.tensor_tensor(low[:, 2 * n:2 * n + 2, :], src[:, 2 * n:2 * n + 2, :],
                                            high[:, 2 * n:2 * n + 2, :].bitcast(F32), ALU.subtract)

            @block.gpsimd
            def _(pool):
                self.first_parts(pool, "odd lows")

            @block.tensor
            def _(pe):
                self.keep_warm(3)
        rounded.close(pairs)

    def product(self, out, slot, rhs, k, start, stop):
        high, low = self.high[:, slot, k * P:(k + 1) * P], self.low[:, slot, k * P:(k + 1) * P]
        skip = not (start or stop)
        mm = None
        for i, (w, x) in enumerate(((high, rhs[0]), (high, rhs[1]), (low, rhs[0]))):
            mm = self.nc.tensor.matmul(out, w, x, start=(start and i == 0), stop=(stop and i == 2), skip_group_check=skip)
        return mm

    def linear(self, engine, take, groups=1, rhs=None, loads=()):
        nc, sig = self.nc, self.sig
        free, used, loaded = sig("bank_free"), sig("tiles_used"), sig("small_loaded")
        rhs_high, rhs_low = rhs or (self.h_high, self.h_low)
        seg, k = self.take_segment()
        blocks = seg.count // groups
        per_turn = RING * groups
        with nc.Block() as block:
            @block.sync
            def _(sp):
                for dst, name in loads:
                    sp.dma_start(dst, self.dram[name]).then_inc(loaded.sem, 16)
                self.stream(sp, seg, k)
                if loads:
                    sp.wait_ge(loaded.sem, loaded.at(16 * len(loads)))

            @block.tensor
            def _(pe):
                with pe.Fori(0, blocks // RING) as turn:
                    for b in range(RING):
                        pe.wait_ge(free.sem, turn * RING + free.at(b + 1 - RING))
                        for g in range(groups):
                            slot = (b * groups + g) % RING
                            pe.wait_ge(sig(f"low{slot}_ready").sem,
                                       turn * groups + ((b * groups + g) // RING + seg.first // RING + 1))
                            for c in range(KB):
                                x = (rhs_high[:, g * KB + c, :], rhs_low[:, g * KB + c, :])
                                mm = self.product(self.bank[b][:, 0:T], slot, x, c, g + c == 0, g == groups - 1 and c == KB - 1)
                            mm.then_inc(used.sem, 1)

            def take_out(eng):
                def finish(i, t):
                    b = t // groups
                    eng.wait_ge(used.sem, i * per_turn + (seg.first + RING + t + 1))
                    take(i * RING + b, self.bank[b][:, 0:T]).then_inc(free.sem, 1)
                return finish

            def make_high(act):
                return lambda i, t: self.make_high(act, seg, i * per_turn + (t - t % RING), t % RING)

            def make_low(eng, slots):
                def make(i, t):
                    if t % RING in slots:
                        self.make_low(eng, seg, i * per_turn + (t - t % RING), t % RING)
                return make

            nothing = lambda i, t: None

            @block.scalar
            def _(act):
                self.paced(act, seg, per_turn, RING - 1, make_high(act), take_out(act) if engine == "scalar" else nothing, groups,
                           prepared=True)

            @block.vector
            def _(dve):
                self.paced(dve, seg, per_turn, RING - 1, make_low(dve, (0, 2)), take_out(dve) if engine == "vector" else nothing, groups,
                           prepared=True)

            @block.gpsimd
            def _(pool):
                self.paced(pool, seg, per_turn, RING - 1, make_low(pool, (1, 3)), nothing, prepared=True)
        free.close(blocks)
        loaded.close(16 * len(loads))

    def copy_to(self, dst, func=ACT.Identity, offset=0):
        return lambda n, bank: self.nc.scalar.activation(dst[:, n + offset, :], bank, func)

    def add_to_x(self, gate=None):
        def fn(n, bank):
            x = self.x[:, n, :]
            if gate is None:
                return self.nc.vector.tensor_tensor(x, bank, x, ALU.add)
            return self.nc.vector.scalar_tensor_tensor(out=x, in0=bank, scalar=gate(n), in1=x, op0=ALU.mult, op1=ALU.add)
        return fn

    def load(self, eng, pairs):
        loaded = self.sig("small_loaded")
        for dst, name in pairs:
            eng.dma_start(dst, self.dram[name]).then_inc(loaded.sem, 16)
        eng.wait_ge(loaded.sem, loaded.at(16 * len(pairs)))
        return 16 * len(pairs)


def modulation_blocks(core, pe, tiles, row):
    mm = None
    for n, tile in enumerate(tiles):
        for c in range(KB):
            mm = core.nc.tensor.matmul(row[0:1, n * P:(n + 1) * P], core.silu[:, c:c + 1], tile[:, c * P:(c + 1) * P],
                                       start=(c == 0), stop=(c == KB - 1))
    return mm


def row_to_columns(core, link, row, turned, mod, first, blocks):
    nc = core.nc
    link(nc.vector.transpose(turned[0:32, 0:blocks * P], row[0:32, 0:blocks * P]))
    parts = turned[0:32, 0:blocks * P].rearrange("p (n g i) -> p n g i", n=blocks, g=4)
    for g in range(4):
        i = nc.vector.tensor_copy(mod[32 * g:32 * g + 32, bass.ds(first, blocks)], parts[:, :, g, 0])
    return i


def modulation_gains(core, dve, link, layer):
    nc = core.nc
    mod = core.mod[:, layer, :]
    link(nc.vector.tensor_tensor(mod, mod, core.col(f"ada_b{layer}"), ALU.add))
    for which, name in enumerate(("norm_mix", "norm_ffn")):
        scale = mod[:, (3 * which + 1) * KB:(3 * which + 2) * KB]
        link(nc.vector.scalar_tensor_tensor(out=core.gain[:, 2 * layer + which, :], in0=scale, scalar=1.0,
                                            in1=core.col(f"{name}{layer}"), op0=ALU.add, op1=ALU.mult))


def setup(core):
    nc, sig = core.nc, core.sig
    step, silu_kept, used, summed, kept, turned_ = (sig(n) for n in (
        "dve_step", "silu_kept", "chunk_used", "row_ready", "row_kept", "row_turned"))
    cols_loaded, tables, sined = sig("cols_loaded"), sig("tables_loaded"), sig("angles_ready")
    pos = core.scratch[:, 0:2 * T].bitcast(I32)
    pos_f = view(core.scratch, 2 * T, 2, T)
    turns = core.scratch[:, 4 * T:5 * T]
    angle = view(core.scratch, 5 * T, 4, T)
    chunks = 48 // 4
    tiles = core.dram["ada_w0"].rearrange("(q n) p c -> q p n c", n=4)
    buffers = [core.arena[:, 4096 * b:4096 * (b + 1)].rearrange("p (n c) -> p n c", n=4) for b in range(4)]
    weighed = view(core.spare[:, 3, :], 0, KB, P)
    partials = view(core.arena, 16384, 2, P)
    part_ready = sig("partial_ready")
    rows = core.spare[0:32, 0:2, :].rearrange("p a (b n) -> p (a b) n", b=2)
    turned = core.spare[0:32, 2, 0:BANK]
    with nc.Block() as block:
        @block.sync
        def _(sp):
            with sp.Fori(0, chunks // 4) as turn:
                for b in range(4):
                    sp.wait_ge(used.sem, turn * 4 + used.at(b + 1))
                    sp.dma_start(buffers[b], tiles[turn * 4 + b]).then_inc(sig(f"chunk{b}_loaded").sem, 16)
            core.first_tiles(sp, 0)

        @block.scalar
        def _(act):
            act.dma_start(core.cols[:], core.dram["cols"]).then_inc(cols_loaded.sem, 16)
            for dst, name in ((pos, "positions"), (core.const[:], "resident")):
                act.dma_start(dst, core.dram[name]).then_inc(tables.sem, 16)
            act.dma_start(core.x[:], core.dram["x"]).then_inc(sig("x_loaded").sem, 16)
            act.wait_ge(cols_loaded.sem, 16)
            nc.scalar.activation(core.silu[:], core.col("c"), ACT.Silu).then_inc(silu_kept.sem, 1)
            act.wait_ge(sig("rows_cleared").sem, 1)
            with act.Fori(0, chunks // 4) as turn:
                for b in range(4):
                    act.wait_ge(summed.sem, turn * 4 + summed.at(b + 1))
                    act.wait_ge(turned_.sem, turn * 4 + turned_.at(b + 1))
                    nc.scalar.activation(rows[0:1, b, :], core.bank[b][0:1, :], ACT.Identity).then_inc(kept.sem, 1)
            act.wait_ge(sined.sem, sined.at(1))
            nc.scalar.activation(core.trig[:], angle, ACT.Sin)
            act.wait_ge(sig("x_loaded").sem, 16)

        @block.tensor
        def _(pe):
            pe.wait_ge(silu_kept.sem, silu_kept.at(1))
            pe.wait_ge(tables.sem, tables.at(16 * 2))
            with pe.Fori(0, chunks // 4) as turn:
                for b in range(4):
                    pe.wait_ge(sig(f"chunk{b}_loaded").sem, turn * 16 + 16)
                    pe.wait_ge(kept.sem, turn * 4 + kept.at(b + 1))
                    modulation_blocks(core, pe, [buffers[b][:, n] for n in range(3)], core.bank[b])
                    pe.wait_ge(part_ready.sem, turn * 4 + part_ready.at(b + 1))
                    nc.tensor.matmul(core.bank[b][0:1, 3 * P:4 * P], core.c("ones")[:, 0:1], partials[:, b % 2, :],
                                     start=True, stop=True).then_inc(summed.sem, 1)
                    nc.tensor.matmul(core.bank[7][0:1, 0:1], core.silu[:, 0:1], core.silu[:, 0:1], start=True, stop=True) \
                        .then_inc(used.sem, 1)

        @block.vector
        def _(dve):
            link = Chain(step, dve)
            nc.vector.memset(core.scratch[:, 9 * T:9 * T + 1], 0.0).then_inc(sig("bank_free").sem, RING)
            for i, name in enumerate(("next_row_kept", "next_row_turned", "next_row_ready", "next_block0_used", "next_block1_used")):
                nc.vector.memset(core.scratch[:, 15 * T + i:15 * T + i + 1], 0.0).then_inc(sig(name).sem, 1)
            for i, name in enumerate(("chunk_used", "row_kept", "row_turned")):
                nc.vector.memset(core.scratch[:, 14 * T + i:14 * T + i + 1], 0.0).then_inc(sig(name).sem, 4)
            nc.vector.memset(core.scratch[:, 12 * T:12 * T + 1], 0.0).then_inc(sig("gates_taken").sem, 4)
            nc.vector.memset(core.scratch[:, 13 * T:13 * T + 1], 0.0).then_inc(sig("gates_spread").sem, 4)
            nc.vector.memset(core.scratch[:, 10 * T:10 * T + 1], 0.0).then_inc(sig("tiles_used").sem, RING)
            nc.vector.memset(rows, 0.0).then_inc(sig("rows_cleared").sem, 1)

            def angles(which, quarter):
                freq = ("inv_freq_a", "inv_freq_b")[which]
                out = angle[:, 2 * which + quarter, :]
                link(nc.vector.tensor_scalar(out, pos_f[:, which, :], core.c(freq), None, ALU.mult))
                link(nc.vector.tensor_scalar(turns, out, 1.0 / (2 * math.pi), 0.25 * quarter, ALU.mult, ALU.add))
                link(nc.vector.tensor_scalar(turns, turns, ROUND, None, ALU.add))
                link(nc.vector.tensor_scalar(turns, turns, ROUND, None, ALU.subtract))
                high = 6.28125
                mid = float(np.float32(np.round((2 * math.pi - high) * 2 ** 20) / 2 ** 20))
                low = 2 * math.pi - high - mid
                for part in (high, mid, low):
                    link(nc.vector.scalar_tensor_tensor(out=out, in0=turns, scalar=-part, in1=out,
                                                        op0=ALU.mult, op1=ALU.add))
                if quarter:
                    link(nc.vector.tensor_scalar(out, out, math.pi / 2, None, ALU.add))
                link(nc.vector.tensor_scalar(out, out, 3.1415925, -3.1415925, ALU.min, ALU.max))

            def partial(n):
                dve.wait_ge(sig(f"chunk{n % 4}_loaded").sem, 16 * (n // 4 + 1))
                if n >= 2:
                    dve.wait_ge(used.sem, used.at(4 + n - 1))
                last = buffers[n % 4][:, 3].rearrange("p (c n) -> p c n", c=KB)
                link(nc.vector.tensor_tensor(weighed, last, core.silu[:].unsqueeze(2).to_broadcast([P, KB, P]), ALU.mult))
                nc.vector.tensor_reduce(partials[:, n % 2, :], weighed.rearrange("p c n -> p n c"), AX_X, ALU.add) \
                    .then_inc(part_ready.sem, 1)

            def turn_row(n):
                dve.wait_ge(kept.sem, kept.at(4 + n + 1))
                link(row_to_columns(core, link, rows[:, n % 4, :], turned, core.mod[:, 0, :], 4 * n, 4))
                nc.vector.memset(core.scratch[:, 11 * T + 1 + n:11 * T + 2 + n], 0.0).then_inc(turned_.sem, 1)

            dve.wait_ge(silu_kept.sem, silu_kept.at(1))
            for n in range(chunks):
                partial(n)
                if n == 0:
                    dve.wait_ge(tables.sem, tables.at(16 * 2))
                    link(nc.vector.tensor_copy(pos_f, pos.rearrange("p (n t) -> p n t", n=2)))
                if 1 <= n <= 4:
                    angles((n - 1) // 2, (n - 1) % 2)
                if n == 4:
                    nc.vector.memset(core.scratch[:, 11 * T:11 * T + 1], 0.0).then_inc(sined.sem, 1)
                if n >= 1:
                    turn_row(n - 1)
            turn_row(chunks - 1)
            modulation_gains(core, dve, link, 0)
            step.used = link.n
    step.close(step.used)
    sined.close(1)
    silu_kept.close(1)
    for s in (used, summed, kept, turned_, part_ready):
        s.close(chunks)
    sig("bank_free").close(RING)


def transposes(core, pe, src, dst_banks, raised):
    for n, block in enumerate(src):
        mm = core.nc.tensor.transpose(dst_banks[n // 4][:, (n % 4) * P:(n % 4 + 1) * P], block, core.c("ident"))
        if n % 4 == 3 or n == len(src) - 1:
            mm.then_inc(raised.sem, 1)


def token_major(core, jobs):
    nc, sig = core.nc, core.sig
    turned, kept = sig("turned"), sig("turned_kept")
    groups = []
    for src, dst in jobs:
        blocks = src.shape[1]
        for t in range(TT):
            for b in range(0, blocks, 4):
                groups.append((src, dst, t, b))
    with nc.Block() as block:
        @block.tensor
        def _(pe):
            for n, (src, dst, t, b) in enumerate(groups):
                if n >= 4:
                    pe.wait_ge(kept.sem, kept.at(n - 3))
                transposes(core, pe, [src[:, b + i, t * P:(t + 1) * P] for i in range(4)], [core.bank[n % 4]], turned)

        @block.scalar
        def _(act):
            for n, (src, dst, t, b) in enumerate(groups):
                act.wait_ge(turned.sem, turned.at(n + 1))
                nc.scalar.activation(dst[:, t, b * P:(b + 4) * P], core.bank[n % 4][:], ACT.Identity).then_inc(kept.sem, 1)
    turned.close(len(groups))
    kept.close(len(groups))


def even_mixer(core):
    nc, sig, A = core.nc, core.sig, core.arena
    proj = view(A, 2048, 12, T)
    core.linear("scalar", core.copy_to(proj))
    u, v, p = proj[:, 0:4], proj[:, 4:8], proj[:, 8:12]
    gelus = sig("gelus_ready")
    centred, squares, tokens = view(A, 5120, 4, T), view(A, 6144, 4, T), view(A, 7168, 2, 4 * P)
    spatial, bias = view(A, 8192, 4, P), view(A, 8704, 4, P)
    ping, pong = view(A, 9216, 4, T + 16), view(A, 10304, 4, T + 16)
    pooled, inv_count, w_pool = view(A, 11392, 4, T), A[:, 12416:13440], view(A, 13440, 4, P)
    mask, cat = A[:, 13952:14080], view(A, 14336, 8, T)
    step, loaded = sig("dve_step"), sig("small_loaded")
    n = [0]
    mean, var = core.bank[4][:, 0:T], core.bank[5][:, 0:T]
    means, cent, vars_, rooted = sig("mean_ready"), sig("centred_squared"), sig("variance_ready"), sig("rooted")
    wide = [P, 4, T]
    root = core.work[:, 0:T]
    with nc.Block() as block:
        @block.sync
        def _(sp):
            n[0] = core.load(sp, [(spatial, "ev_w_s"), (bias, "ev_b_s"), (inv_count, "inv_count"),
                                    (w_pool, "ev_w_pool"), (mask, "even_mask")])

        @block.tensor
        def _(pe):
            pe.wait_ge(gelus.sem, gelus.at(1))
            for g in range(4):
                mm = nc.tensor.matmul(mean, core.c("ones"), v[:, g, :], start=(g == 0), stop=(g == 3))
            mm.then_inc(means.sem, 1)
            core.keep_warm(2)
            pe.wait_ge(cent.sem, cent.at(1))
            for g in range(4):
                mm = nc.tensor.matmul(var, core.c("ones"), squares[:, g, :], start=(g == 0), stop=(g == 3))
            mm.then_inc(vars_.sem, 1)
            core.keep_warm(6)

        @block.scalar
        def _(act):
            nc.scalar.activation(v, v, ACT.Gelu).then_inc(gelus.sem, 1)
            nc.scalar.activation(u, u, ACT.Gelu)
            act.wait_ge(vars_.sem, vars_.at(1))
            nc.scalar.activation(root, var, ACT.Sqrt, bias=core.c("eps"), scale=1.0 / 512).then_inc(rooted.sem, 1)

        @block.vector
        def _(dve):
            link = Chain(step, dve)
            dve.wait_ge(means.sem, means.at(1))
            link(nc.vector.scalar_tensor_tensor(out=centred, in0=mean.unsqueeze(1).to_broadcast(wide), scalar=-1.0 / 512,
                                                in1=v, op0=ALU.mult, op1=ALU.add))
            nc.vector.tensor_tensor(squares, centred, centred, ALU.mult).then_inc(cent.sem, 1)
            link(nc.vector.memset(ping[:, :, 0:16], 0.0))
            link(nc.vector.memset(pong[:, :, 0:16], 0.0))
            link(nc.vector.tensor_copy(ping[:, :, 16:], p))
            src, dst = ping, pong
            for g in range(4):
                shift = 1 << g
                link(nc.vector.tensor_tensor(dst[:, g:4, 16:], src[:, g:4, 16:], src[:, g:4, 16 - shift:16 - shift + T], ALU.add))
                link(nc.vector.tensor_tensor(pooled[:, g, :], dst[:, g, 16:], dst[:, g, 16:], ALU.max))
                src, dst = dst, src
            dve.wait_ge(loaded.sem, loaded.at(16 * 5))
            link(nc.vector.tensor_tensor(pooled, pooled, inv_count.rearrange("p (g t) -> p g t", g=4), ALU.mult))
            link(nc.vector.tensor_tensor(pooled, pooled, p, ALU.subtract))
            link(nc.vector.tensor_tensor(spatial, spatial, mask.unsqueeze(1).to_broadcast([P, 4, P]), ALU.mult))
            dve.wait_ge(rooted.sem, rooted.at(1))
            link(nc.vector.reciprocal(root, root))
            link(nc.vector.tensor_tensor(centred, centred, root.unsqueeze(1).to_broadcast(wide), ALU.mult))
            step.used = link.n
    step.close(step.used)
    for s in (means, cent, vars_, rooted, gelus):
        s.close(1)
    loaded.close(n[0])
    token_major(core, [(centred, tokens)])
    mixed, pools = sig("spatial_mixed"), sig("pool_mixed")
    with nc.Block() as block:
        @block.tensor
        def _(pe):
            for t in range(TT):
                for g in range(4):
                    mm = nc.tensor.matmul(core.bank[t][:, g * P:(g + 1) * P], tokens[:, t, g * P:(g + 1) * P],
                                          spatial[:, g, :], start=True, stop=True)
                mm.then_inc(mixed.sem, 1)
            for g in range(4):
                mm = nc.tensor.matmul(core.bank[4 + g][:, 0:T], w_pool[:, g, :], pooled[:, g, :], start=True, stop=True)
                mm.then_inc(pools.sem, 1)

        @block.vector
        def _(dve):
            link = Chain(step, dve)
            for t in range(TT):
                dve.wait_ge(mixed.sem, mixed.at(t + 1))
                for g in range(4):
                    nc.vector.scalar_tensor_tensor(out=cat[:, g, t * P:(t + 1) * P], in0=core.bank[t][:, g * P:(g + 1) * P],
                                                   scalar=core.col("ev_g_v", g), in1=bias[:, g, :], op0=ALU.mult, op1=ALU.add)
            link(nc.vector.memset(core.work[:, 500:501], 0.0))
            nc.vector.tensor_tensor(cat[:, 0:4], cat[:, 0:4], u, ALU.mult)
            step.used = link.n

        @block.scalar
        def _(act):
            for g in range(4):
                act.wait_ge(pools.sem, pools.at(g + 1))
                nc.scalar.activation(cat[:, 4 + g, :], core.bank[4 + g][:, 0:T], ACT.Identity, scale=core.col("ev_pool_scale", g))
    step.close(step.used)
    mixed.close(TT)
    pools.close(4)
    core.split(cat, core.h_high, core.h_low)
    core.linear("vector", core.add_to_x(lambda n: core.mod[:, 0, bass.ds(n + 2 * KB, 1)]))


def mixer_norm(core, layer):
    core.norm(core.x, core.gain[:, 2 * layer, :], core.mod[:, layer, 0:KB], view(core.arena, 0, 8, T))


def ffn_norm(core, layer):
    core.norm(core.x, core.gain[:, 2 * layer + 1, :], core.mod[:, layer, 3 * KB:4 * KB], view(core.arena, 0, 8, T))



def peer_queries(core, layer):
    nc, sig, A = core.nc, core.sig, core.arena
    queries, keys = view(A, 0, 16, T), view(A, 4096, 16, KEYS)
    core.linear("scalar", core.copy_to(queries), loads=[(A[:, 4096:4096 + 16 * KEYS], f"peer_keys{layer}")])
    scored, kept = sig("keys_scored"), sig("key_scores_kept")
    with nc.Block() as block:
        @block.tensor
        def _(pe):
            for g in range(TT * 4):
                t, first = g // 4, (g % 4) * 4
                if g >= 4:
                    pe.wait_ge(kept.sem, kept.at(g - 3))
                for q in range(4):
                    mm = nc.tensor.matmul(core.bank[g % 4][:, q * KEYS:(q + 1) * KEYS],
                                          queries[:, first + q, t * P:(t + 1) * P], keys[:, first + q, :],
                                          start=True, stop=True)
                mm.then_inc(scored.sem, 1)

        @block.scalar
        def _(act):
            for g in range(TT * 4):
                act.wait_ge(scored.sem, scored.at(g + 1))
                nc.scalar.activation(core.arena[:, SCORES_AT + g * BANK:SCORES_AT + (g + 1) * BANK], core.bank[g % 4][:], ACT.Identity) \
                    .then_inc(kept.sem, 1)
            core.first_parts(act, "high")

        @block.vector
        def _(dve):
            core.first_parts(dve, "even lows")

        @block.gpsimd
        def _(pool):
            core.first_parts(pool, "odd lows")
    scored.close(8)
    kept.close(8)


def peer_scores(core, layer):
    nc, sig = core.nc, core.sig
    used, free, step, picked = sig("tiles_used"), sig("bank_free"), sig("dve_step"), sig("experts_picked")
    seg, k = core.take_segment()
    acts = view(core.arena, 0, P, T)
    scores = core.arena[:, SCORES_AT:SCORES_AT + 4096].rearrange("p (t h s n) -> p t h s n", t=TT, h=HEADS, s=2)
    b = core.pick
    sums = lambda t: b.sums[:, t].rearrange("p a b -> p (a b)")
    safe = SCORES_AT // T // RING
    with nc.Block() as block:
        @block.sync
        def _(sp):
            core.stream(sp, seg, k)

        @block.tensor
        def _(pe):
            with pe.Fori(0, P // RING) as turn:
                for slot in range(RING):
                    pe.wait_ge(free.sem, turn * RING + free.at(slot + 1 - RING))
                    core.wait_turn(pe, seg, turn, slot)
                    for c in range(KB):
                        mm = core.product(core.bank[slot][:, 0:T], slot, (core.h_high[:, c, :], core.h_low[:, c, :]), c,
                                          c == 0, c == KB - 1)
                    mm.then_inc(used.sem, 1)

        @block.gpsimd
        def _(pool):
            core.paced(pool, seg, RING, RING - 1, lambda i, t: core.make_low(pool, seg, i * RING + (t - t % RING), t % RING),
                       lambda i, t: None, prepared=True)

        @block.scalar
        def _(act):
            def high(i, t):
                core.make_high(act, seg, i * RING + (t - t % RING), t % RING)

            def gelu(i, t):
                act.wait_ge(used.sem, i * RING + (seg.first + RING + t + 1))
                nc.scalar.activation(acts[:, i * RING + t, :], core.bank[t][:, 0:T], ACT.Gelu).then_inc(free.sem, 1)

            with act.Fori(0, safe) as i:
                for t in range(RING):
                    gelu(i, t)
                    high(i, t + RING - 1)
            act.wait_ge(picked.sem, picked.at(1))
            for i in range(safe, P // RING):
                for t in range(RING):
                    gelu(i, t)
                    if i * RING + t + RING - 1 < P:
                        high(i, t + RING - 1)

        @block.vector
        def _(dve):
            link = Chain(step, dve)
            for h in range(HEADS):
                sets = [(t, s, scores[:, t, h, s, :], b.top[:, t, s]) for t in range(TT) for s in range(2)]
                for t, s, keys, top in sets:
                    i = nc.vector.max(top[:, 0:8], keys)
                link(i)
                for t, s, keys, top in sets:
                    i = nc.vector.max_index(b.at[:, t, s, 0:8], top[:, 0:8], keys)
                for t, s, keys, top in sets:
                    i = nc.vector.match_replace(keys, top[:, 0:8], keys, LOWEST)
                link(i)
                for t, s, keys, top in sets:
                    i = nc.vector.max(top[:, 8:16], keys)
                link(i)
                for t, s, keys, top in sets:
                    i = nc.vector.max_index(b.at[:, t, s, 8:16], top[:, 8:16], keys)
                for t in range(TT):
                    i = nc.vector.tensor_tensor(b.sums[:, t], b.top[:, t, 0, :].unsqueeze(2).to_broadcast([P, 16, 16]),
                                                b.top[:, t, 1, :].unsqueeze(1).to_broadcast([P, 16, 16]), ALU.add)
                link(i)
                nc.vector.tensor_copy(b.at_f[:], b.at[:])
                for t in range(TT):
                    i = nc.vector.max(b.best[:, t, 0:8], sums(t))
                link(i)
                for t in range(TT):
                    nc.vector.max_index(b.place[:, t, 0:8], b.best[:, t, 0:8], sums(t))
                for t in range(TT):
                    i = nc.vector.match_replace(sums(t), b.best[:, t, 0:8], sums(t), LOWEST)
                link(i)
                for t in range(TT):
                    i = nc.vector.max(b.best[:, t, 8:16], sums(t))
                link(i)
                for t in range(TT):
                    i = nc.vector.max_index(b.place[:, t, 8:16], b.best[:, t, 8:16], sums(t))
                nc.vector.tensor_tensor(b.expo[:, :, h, :], b.best[:], b.best[:, :, 0:1].to_broadcast([P, TT, 16]), ALU.subtract)
                link(i)
                nc.vector.tensor_scalar(b.digit[:, 0], b.place[:], 4, None, ALU.logical_shift_right)
                link(nc.vector.tensor_scalar(b.digit[:, 1], b.place[:], 15, None, ALU.bitwise_and))
                link(nc.vector.tensor_copy(b.digit_f[:], b.digit[:]))
                iota = core.c("iota16").unsqueeze(1).to_broadcast([P, 16, 16])
                for s in range(2):
                    for t in range(TT):
                        i = nc.vector.tensor_tensor(b.sums[:, t], b.digit_f[:, s, t, :].unsqueeze(2).to_broadcast([P, 16, 16]),
                                                    iota, ALU.is_equal)
                    link(i)
                    for t in range(TT):
                        i = nc.vector.tensor_tensor(b.sums[:, t], b.sums[:, t],
                                                    b.at_f[:, t, s, :].unsqueeze(1).to_broadcast([P, 16, 16]), ALU.mult)
                    link(i)
                    for t in range(TT):
                        i = nc.vector.tensor_reduce(b.chosen[:, s, t, h * TOPK:(h + 1) * TOPK], b.sums[:, t], AX_X, ALU.add)
                    link(i)
            nc.vector.tensor_copy(b.total[:, 0:1], b.best[:, 0, 0:1]).then_inc(picked.sem, 1)
            step.used = link.n
    step.close(step.used)
    picked.close(1)
    free.close(P)


def peer_gates(core, layer):
    nc, sig, b = core.nc, core.sig, core.pick
    exped, gated, turned, step = sig("gates_exped"), sig("gates_ready"), sig("turned"), sig("dve_step")
    gates = b.expo[:].rearrange("p t h k -> p (t h) k")
    total = b.total[:]
    with nc.Block() as block:
        @block.scalar
        def _(act):
            nc.scalar.activation(b.expo[:], b.expo[:], ACT.Exp).then_inc(exped.sem, 1)

        @block.vector
        def _(dve):
            link = Chain(step, dve)
            dve.wait_ge(exped.sem, exped.at(1))
            link(nc.vector.tensor_reduce(total, gates, AX_X, ALU.add))
            link(nc.vector.reciprocal(total, total))
            nc.vector.tensor_tensor(gates, gates, total.unsqueeze(2).to_broadcast([P, TT * HEADS, TOPK]), ALU.mult) \
                .then_inc(gated.sem, 1)
            step.used = link.n
            for n in range(3):
                dve.wait_ge(turned.sem, turned.at(n + 1))
                nc.vector.tensor_copy(b.by_pick[:, n, :], core.bank[n][:, 0:T])

        @block.tensor
        def _(pe):
            for n in range(3):
                if n == 2:
                    core.keep_warm(3)
                    pe.wait_ge(gated.sem, gated.at(1))
                    src = [b.expo[:, t].rearrange("p h k -> p (h k)") for t in range(TT)]
                else:
                    src = [b.chosen[:, n, t, :] for t in range(TT)]
                transposes(core, pe, src, [core.bank[n]], turned)
    step.close(step.used)
    turned.close(3)
    exped.close(1)
    gated.close(1)


def peer_weigh(core, layer):
    nc, sig, b = core.nc, core.sig, core.pick
    seconds, firsts, spread, taken = (sig(n) for n in ("seconds_ready", "firsts_ready", "gates_spread", "gates_taken"))
    differ, distant, step = sig("differences_ready"), sig("distances_ready"), sig("dve_step")
    acts = view(core.arena, 0, P, T)
    first, second, gate = (b.by_pick[:, n, :] for n in range(3))
    turns, groups = T // 16, 4
    hot_first, hot_second = view(core.scratch, 0, 16, P), view(core.scratch, 2048, 16, P)
    group = lambda hot, g: hot[:, 4 * g:4 * g + 4, :]
    iota = core.c("iota")
    beside = layer == 0
    row_summed, row_kept, row_turned = (sig(n) for n in ("next_row_ready", "next_row_kept", "next_row_turned"))
    blocks = [core.spare[:, n, :] for n in range(3)]
    used = [sig("next_block0_used"), sig("next_block1_used"), row_summed]
    row, turned = core.spare[0:32, 3, 0:3 * P], core.spare[0:32, 3, BANK:BANK + 3 * P]

    def scatter(turn):
        parts = turned.rearrange("p (n g i) -> p n g i", n=3, g=4)
        for g in range(4):
            i = nc.vector.tensor_copy(core.mod[32 * g:32 * g + 32, 1, bass.ds(turn * 3, 3)], parts[:, :, g, 0])
        return i

    with nc.Block() as block:
        if beside:
            @block.sync
            def _(sp):
                with sp.Fori(0, turns) as turn:
                    for n in range(3):
                        sp.wait_ge(used[n].sem, turn + used[n].at(1))
                        sp.dma_start(blocks[n], core.dram["ada_w1"][turn * 3 + n]).then_inc(sig(f"next_block{n}_loaded").sem, 16)

        @block.gpsimd
        def _(pool):
            with pool.Fori(0, turns) as turn:
                for g in range(groups):
                    pool.wait_ge(spread.sem, turn * groups + spread.at(g + 1))
                    mine = first[:, bass.ds(turn * 16 + 4 * g, 4)].unsqueeze(2).to_broadcast([P, 4, P])
                    nc.gpsimd.tensor_tensor(group(hot_first, g), iota.unsqueeze(1).to_broadcast([P, 4, P]), mine, ALU.subtract) \
                        .then_inc(differ.sem, 1)

        @block.scalar
        def _(act):
            def onehots(turn, g):
                act.wait_ge(differ.sem, turn * groups + differ.at(g + 1))
                nc.scalar.activation(group(hot_first, g), group(hot_first, g), ACT.Abs).then_inc(distant.sem, 1)
                act.wait_ge(distant.sem, turn * groups + distant.at(g + 1))
                nc.scalar.activation(group(hot_first, g), group(hot_first, g), ACT.Relu, bias=core.c("ones")[:, 0:1],
                                     scale=-1.0).then_inc(firsts.sem, 1)

            def turn_body(turn, last):
                for g in range(groups):
                    if not (last and g + 2 >= groups):
                        onehots(turn + (g + 2) // groups, (g + 2) % groups)
                if beside:
                    act.wait_ge(row_summed.sem, turn + row_summed.at(2))
                    act.wait_ge(row_turned.sem, turn + row_turned.at(1))
                    nc.scalar.activation(row[0:1, :], core.bank[5][0:1, 0:3 * P], ACT.Identity).then_inc(row_kept.sem, 1)

            onehots(0, 0)
            onehots(0, 1)
            with act.Fori(0, turns - 1) as turn:
                turn_body(turn, False)
            turn_body(turns - 1, True)

        @block.vector
        def _(dve):
            link = Chain(step, dve)
            if beside:
                link(nc.vector.memset(row, 0.0))
            step.used = link.n

            def onehots(turn, g):
                dve.wait_ge(spread.sem, turn * groups + spread.at(g + 1))
                for u in range(4):
                    token = turn * 16 + 4 * g + u
                    i = nc.vector.tensor_scalar(group(hot_second, g)[:, u, :], iota, second[:, bass.ds(token, 1)],
                                                gate[:, bass.ds(token, 1)], ALU.is_equal, ALU.mult)
                i.then_inc(seconds.sem, 1)

            def weigh(turn, g):
                dve.wait_ge(spread.sem, turn * groups + spread.at(groups + g + 1))
                part = acts[:, :, bass.ds(turn * 16 + 4 * g, 4)]
                nc.vector.tensor_tensor(part, part, core.bank[g][:].rearrange("p (u i) -> p i u", u=4), ALU.mult) \
                    .then_inc(taken.sem, 1)

            def turn_body(turn, last):
                for g in range(groups):
                    if not (last and g + 2 >= groups):
                        onehots(turn + (g + 2) // groups, (g + 2) % groups)
                    weigh(turn, g)
                if beside:
                    dve.wait_ge(row_kept.sem, turn + row_kept.at(2))
                    nc.vector.transpose(turned, row).then_inc(row_turned.sem, 1)
                    dve.wait_ge(row_turned.sem, turn + row_turned.at(2))
                    return scatter(turn)

            onehots(0, 0)
            onehots(0, 1)
            with dve.Fori(0, turns - 1) as turn:
                turn_body(turn, False)
            i = turn_body(turns - 1, True)
            if beside:
                link(i)
                modulation_gains(core, dve, link, 1)
                step.used = link.n

        @block.tensor
        def _(pe):
            with pe.Fori(0, turns) as turn:
                for g in range(groups):
                    pe.wait_ge(seconds.sem, turn * groups + seconds.at(g + 1))
                    pe.wait_ge(firsts.sem, turn * groups + firsts.at(g + 1))
                    pe.wait_ge(taken.sem, turn * groups + taken.at(g + 1))
                    for u in range(4):
                        mm = nc.tensor.matmul(core.bank[g][:, u * P:(u + 1) * P], group(hot_second, g)[:, u, :],
                                              group(hot_first, g)[:, u, :], start=True, stop=True)
                    mm.then_inc(spread.sem, 1)
                    if beside and g < 3:
                        pe.wait_ge(sig(f"next_block{g}_loaded").sem, turn * 16 + 16)
                        if g == 0:
                            pe.wait_ge(row_kept.sem, turn + row_kept.at(1))
                        modulation_blocks(core, pe, [blocks[g]], core.bank[5][:, g * P:(g + 1) * P]).then_inc(used[g].sem, 1)
    step.close(step.used)
    for s in (seconds, firsts, spread, taken, differ, distant):
        s.close(turns * groups)


def peer_output(core, layer):
    nc, sig = core.nc, core.sig
    used, summed, rounded, split = sig("tiles_used"), sig("experts_summed"), sig("act_rounded"), sig("act_split")
    seg, k = core.take_segment()
    acts = view(core.arena, 0, P, T)
    out = [core.bank[4 + d // 2][:, (d % 2) * T:(d % 2 + 1) * T] for d in range(KB)]
    with nc.Block() as block:
        @block.sync
        def _(sp):
            core.stream(sp, seg, k)

        @block.tensor
        def _(pe):
            for d in range(4):
                nc.tensor.matmul(core.bank[4 + d][:], core.c("zeros"), core.const[:, 0:BANK], start=True, stop=False,
                                 skip_group_check=True)
            with pe.Fori(0, P // RING) as turn:
                for slot in range(RING):
                    core.wait_turn(pe, seg, turn, slot)
                    pe.wait_ge(split.sem, turn * RING + split.at(slot + 1))
                    x = (core.act_high[:, slot, :], core.act_low[:, slot, :])
                    for d in range(KB):
                        mm = core.product(out[d], slot, x, d, False, False)
                    mm.then_inc(used.sem, 1)
            for d in range(4):
                mm = nc.tensor.matmul(core.bank[4 + d][:], core.c("zeros"), core.const[:, 0:BANK], start=False, stop=True,
                                      skip_group_check=True)
            mm.then_inc(summed.sem, 1)

        def high(act):
            def make(i, t):
                core.make_high(act, seg, i * RING + (t - t % RING), t % RING)
                nc.scalar.activation(core.act_high[:, t % RING, :], acts[:, i * RING + t, :], ACT.Identity).then_inc(rounded.sem, 1)
            return make

        @block.scalar
        def _(act):
            def pace(i, t):
                act.wait_ge(used.sem, i * RING + (seg.first + RING + t + 1))
            core.paced(act, seg, RING, RING - 1, high(act), pace)

        @block.vector
        def _(dve):
            def make(i, t):
                dve.wait_ge(rounded.sem, i * RING + rounded.at(t + 1))
                slot = t % RING
                nc.vector.tensor_tensor(core.act_low[:, slot, :], acts[:, i * RING + t, :], core.act_high[:, slot, :].bitcast(F32),
                                        ALU.subtract).then_inc(split.sem, 1)
                if slot % 2 == 0:
                    core.make_low(dve, seg, i * RING + (t - slot), slot)

            core.paced(dve, seg, RING, RING - 1, make, lambda i, t: None)
            dve.wait_ge(summed.sem, summed.at(1))
            for d in range(KB):
                core.add_to_x(lambda n: core.mod[:, layer, 5 * KB + n:5 * KB + n + 1])(d, out[d])

        @block.gpsimd
        def _(pool):
            def make(i, t):
                if t % 2:
                    core.make_low(pool, seg, i * RING + (t - t % RING), t % RING)
            core.paced(pool, seg, RING, RING - 1, make, lambda i, t: None)
    summed.close(1)
    rounded.close(P)
    split.close(P)


def peer(core, layer):
    ffn_norm(core, layer)
    peer_queries(core, layer)
    peer_scores(core, layer)
    peer_gates(core, layer)
    peer_weigh(core, layer)
    peer_output(core, layer)


def rope(core, src, dst, pairs, cos, sin):
    nc, sig = core.nc, core.sig
    swapped, taken, straight = sig("halves_swapped"), sig("halves_taken"), sig("straight_ready")
    step = sig("dve_step")
    two = [P, 2, T]
    cosb, sinb = (a.unsqueeze(1).to_broadcast(two) for a in (cos, sin))
    side = core.scratch[:, 0:4 * BANK].rearrange("p (b n t) -> p b n t", b=4, n=2)
    with nc.Block() as block:
        @block.tensor
        def _(pe):
            for n in range(pairs):
                if n >= 4:
                    pe.wait_ge(taken.sem, taken.at(n - 3))
                nc.tensor.matmul(core.bank[n % 4][:], core.c("rot"), src[:, 2 * n:2 * n + 2, :], start=True, stop=True) \
                    .then_inc(swapped.sem, 1)
            core.keep_warm(2)

        @block.gpsimd
        def _(pool):
            for n in range(pairs):
                nc.gpsimd.tensor_tensor(dst[:, 2 * n:2 * n + 2, :], src[:, 2 * n:2 * n + 2, :], cosb, ALU.mult) \
                    .then_inc(straight.sem, 1)

        @block.vector
        def _(dve):
            link = Chain(step, dve)
            for n in range(pairs):
                dve.wait_ge(swapped.sem, swapped.at(n + 1))
                i = nc.vector.tensor_tensor(side[:, n % 4], core.bank[n % 4][:].rearrange("p (n t) -> p n t", n=2), sinb, ALU.mult)
                i.then_inc(taken.sem, 1)
                dve.wait_ge(taken.sem, taken.at(n + 1))
                dve.wait_ge(straight.sem, straight.at(n + 1))
                part = dst[:, 2 * n:2 * n + 2, :]
                nc.vector.tensor_tensor(part, part, side[:, n % 4], ALU.add)
            step.used = link.n
    step.close(step.used)
    for s in (swapped, taken, straight):
        s.close(pairs)


def block_rms(core, src, blocks, ones, count, eps, squares, root, centre=None):
    nc, sig = core.nc, core.sig
    step, meaned, squared, summed, logged = (sig(n) for n in ("dve_step", "mean_ready", "squared", "square_sums", "logged"))
    flat = lambda a: a.rearrange("p n t -> p (n t)")
    banks = blocks // 2
    src_f, squares_f, root_f = flat(src), flat(squares), flat(root)
    with nc.Block() as block:
        @block.tensor
        def _(pe):
            if centre is not None:
                for n in range(banks):
                    nc.tensor.matmul(core.bank[n][:], core.c(ones), src_f[:, n * BANK:(n + 1) * BANK], start=True, stop=True) \
                        .then_inc(meaned.sem, 1)
            for n in range(banks):
                pe.wait_ge(squared.sem, squared.at(n + 1))
                nc.tensor.matmul(core.bank[4 + n][:], core.c(ones), squares_f[:, n * BANK:(n + 1) * BANK], start=True, stop=True) \
                    .then_inc(summed.sem, 1)
            core.keep_warm(banks + 1, bank=3)

        @block.scalar
        def _(act):
            for n in range(banks):
                act.wait_ge(summed.sem, summed.at(n + 1))
                nc.scalar.activation(root_f[:, n * BANK:(n + 1) * BANK], core.bank[4 + n][:], ACT.Ln, bias=eps,
                                     scale=1.0 / count).then_inc(logged.sem, 1)
            act.wait_ge(logged.sem, logged.at(banks))
            nc.scalar.activation(root_f, root_f, ACT.Exp, scale=-0.5)

        @block.vector
        def _(dve):
            link = Chain(step, dve)
            for n in range(banks):
                part = slice(n * BANK, (n + 1) * BANK)
                if centre is not None:
                    dve.wait_ge(meaned.sem, meaned.at(n + 1))
                    link(nc.vector.scalar_tensor_tensor(out=flat(centre)[:, part], in0=core.bank[n][:], scalar=-1.0 / count,
                                                        in1=src_f[:, part], op0=ALU.mult, op1=ALU.add))
                    nc.vector.tensor_tensor(squares_f[:, part], flat(centre)[:, part], flat(centre)[:, part], ALU.mult) \
                        .then_inc(squared.sem, 1)
                else:
                    nc.vector.tensor_tensor(squares_f[:, part], src_f[:, part], src_f[:, part], ALU.mult).then_inc(squared.sem, 1)
            step.used = link.n
    step.close(step.used)
    meaned.close(banks if centre is not None else 0)
    for s in (squared, summed, logged):
        s.close(banks)


def odd_mixer(core):
    nc, sig, A = core.nc, core.sig, core.arena
    proj, turned, tokens, o = view(A, 0, 24, T), view(A, 6144, 16, T), view(A, 10240, 2, 8 * P), view(A, 12288, 8, T)
    squares, root = view(A, 14336, 8, T), view(A, 16384, 8, T)
    mask = A[:, 18432:18432 + 384]
    probs = A[:, 18816:18816 + 2 * 768].rearrange("p (b m k) -> p b m k", b=2, m=2)
    combined, combined_T = view(A, 20352, 2, 384), view(A, 21120, 2, 384)
    lam = A[:, 21888:21888 + 256].rearrange("p (n d) -> p n d", n=4)
    peak, total, minus_lam = A[:, 22144:22152], A[:, 22152:22160], A[:, 22160:22164]
    product, gain = A[:, 22164:22164 + 64], A[:, 22228:22229]
    core.linear("scalar", core.copy_to(proj), loads=[(mask, "attn_mask"), (lam, "od_lam")])
    rope(core, proj[:, 0:16], turned, 8, core.trig[:, 1, :], core.trig[:, 0, :])
    token_major(core, [(proj[:, 16:24], tokens)])

    step, act_step = sig("dve_step"), sig("lam_exped")
    with nc.Block() as block:
        @block.tensor
        def _(pe):
            core.keep_warm(3)

        @block.vector
        def _(dve):
            link = Chain(step, dve)
            for i in range(2):
                link(nc.vector.tensor_tensor(product, lam[:, 2 * i], lam[:, 2 * i + 1], ALU.mult))
                link(nc.vector.tensor_reduce(minus_lam[:, i:i + 1], product, AX_X, ALU.add))
            nc.vector.tensor_scalar(gain, core.col("od_g_sub"), 1.0 - LAM_INIT, None, ALU.mult).then_inc(sig("lam_summed").sem, 1)
            dve.wait_ge(act_step.sem, act_step.at(1))
            link(nc.vector.tensor_tensor(minus_lam[:, 3:4], minus_lam[:, 1:2], minus_lam[:, 0:1], ALU.subtract))
            link(nc.vector.tensor_scalar(minus_lam[:, 3:4], minus_lam[:, 3:4], LAM_INIT, None, ALU.subtract))
            step.used = link.n

        @block.scalar
        def _(act):
            act.wait_ge(sig("lam_summed").sem, sig("lam_summed").at(1))
            nc.scalar.activation(minus_lam[:, 0:2], minus_lam[:, 0:2], ACT.Exp).then_inc(act_step.sem, 1)
    step.close(step.used)
    act_step.close(1)
    sig("lam_summed").close(1)

    scored, peaked, exped, weighed, flipped, kept, mixed = (sig(x) for x in (
        "heads_scored", "heads_peaked", "heads_exped", "heads_weighed", "heads_flipped", "flips_kept", "heads_mixed"))
    scored_taken, mixed_taken = sig("scores_taken"), sig("mixed_taken")
    of = lambda a, h, m, i: a[:, 4 * (h % 2) + 2 * i + m:4 * (h % 2) + 2 * i + m + 1]
    sums = lambda h, m, i: of(total, h, m, i)
    minus_peak = lambda h, m, i: of(peak, h, m, i)
    span = (slice(0, P), slice(P, 3 * P))
    with nc.Block() as block:
        @block.tensor
        def _(pe):
            def scores(h):
                if h >= 2:
                    pe.wait_ge(scored_taken.sem, scored_taken.at(h - 1))
                for m in range(2):
                    half = slice(64 * m, 64 * m + 64)
                    for i in range(2):
                        mm = nc.tensor.matmul(core.bank[2 * (h % 2) + m][:, span[i]], turned[half, h, i * P:(i + 1) * P],
                                              turned[half, 8 + h, 0:(i + 1) * P], start=True, stop=True)
                mm.then_inc(scored.sem, 1)

            scores(0)
            scores(1)
            for h in range(HEADS):
                if h + 2 < HEADS:
                    scores(h + 2)
                pe.wait_ge(weighed.sem, weighed.at(h + 1))
                if h >= 2:
                    pe.wait_ge(kept.sem, kept.at(h - 1))
                w = combined[:, h % 2, :]
                flips = core.bank[4 + h % 2]
                for c, at in ((0, 0), (1, 1), (2, 2)):
                    mm = nc.tensor.transpose(flips[:, at * P:(at + 1) * P], w[:, c * P:(c + 1) * P], core.c("ident"))
                mm.then_inc(flipped.sem, 1)
                pe.wait_ge(kept.sem, kept.at(h + 1))
                if h >= 2:
                    pe.wait_ge(mixed_taken.sem, mixed_taken.at(h - 1))
                out = core.bank[6 + h % 2]
                v = tokens[:, :, h * P:(h + 1) * P]
                nc.tensor.matmul(out[:, 0:T], v[:, 0, :], combined_T[:, h % 2, 0:T], start=True, stop=False)
                nc.tensor.matmul(out[:, P:T], v[:, 1, :], combined_T[:, h % 2, T:3 * P], start=False, stop=True) \
                    .then_inc(mixed.sem, 1)

        @block.vector
        def _(dve):
            link = Chain(step, dve)

            def peaks(h):
                dve.wait_ge(scored.sem, scored.at(h + 1))
                if h >= 2:
                    dve.wait_ge(weighed.sem, weighed.at(h - 1))
                s = probs[:, h % 2]
                for m in range(2):
                    i = nc.vector.scalar_tensor_tensor(out=s[:, m], in0=core.bank[2 * (h % 2) + m][:, 0:384], scalar=0.125,
                                                       in1=mask, op0=ALU.mult, op1=ALU.add)
                i.then_inc(scored_taken.sem, 1)
                dve.wait_ge(scored_taken.sem, scored_taken.at(h + 1))
                mine = peak[:, 4 * (h % 2):4 * (h % 2) + 4]
                nc.vector.tensor_reduce(mine[:, 0:2], s[:, :, 0:P], AX_X, ALU.max)
                link(nc.vector.tensor_reduce(mine[:, 2:4], s[:, :, P:3 * P], AX_X, ALU.max))
                nc.vector.tensor_scalar(mine, mine, -1.0, None, ALU.mult).then_inc(peaked.sem, 1)

            peaks(0)
            for h in range(HEADS):
                if h + 1 < HEADS:
                    peaks(h + 1)
                dve.wait_ge(exped.sem, exped.at(h + 1))
                s = probs[:, h % 2]
                mine = total[:, 4 * (h % 2):4 * (h % 2) + 4]
                link(nc.vector.reciprocal(mine, mine))
                for i in range(2):
                    j = nc.vector.tensor_tensor(sums(h, 1, i), sums(h, 1, i), minus_lam[:, 3:4], ALU.mult)
                link(j)
                for i in range(2):
                    j = nc.vector.tensor_scalar(s[:, 1, span[i]], s[:, 1, span[i]], sums(h, 1, i), None, ALU.mult)
                link(j)
                if h >= 2:
                    dve.wait_ge(flipped.sem, flipped.at(h - 1))
                for i in range(2):
                    j = nc.vector.scalar_tensor_tensor(out=combined[:, h % 2, span[i]], in0=s[:, 0, span[i]], scalar=sums(h, 0, i),
                                                       in1=s[:, 1, span[i]], op0=ALU.mult, op1=ALU.add)
                j.then_inc(weighed.sem, 1)
            step.used = link.n

        @block.scalar
        def _(act):
            for h in range(HEADS + 1):
                if h < HEADS:
                    act.wait_ge(peaked.sem, peaked.at(h + 1))
                    s = probs[:, h % 2]
                    for m in range(2):
                        for i in range(2):
                            j = nc.scalar.activation(s[:, m, span[i]], s[:, m, span[i]], ACT.Exp, bias=minus_peak(h, m, i),
                                                     accum_out=sums(h, m, i))
                    j.then_inc(exped.sem, 1)
                if h >= 1:
                    act.wait_ge(mixed.sem, mixed.at(h))
                    nc.scalar.activation(o[:, h - 1, :], core.bank[6 + (h - 1) % 2][:, 0:T], ACT.Identity).then_inc(mixed_taken.sem, 1)
                if h < HEADS:
                    act.wait_ge(flipped.sem, flipped.at(h + 1))
                    src, dst = core.bank[4 + h % 2], combined_T[:, h % 2]
                    nc.scalar.activation(dst, src[:, 0:384], ACT.Identity).then_inc(kept.sem, 1)
    step.close(step.used)
    for s in (scored, peaked, exped, weighed, flipped, kept, mixed, scored_taken, mixed_taken):
        s.close(HEADS)

    block_rms(core, o, 8, "ones", P, core.c("eps"), squares, root)
    with nc.Block() as block:
        @block.vector
        def _(dve):
            nc.vector.scalar_tensor_tensor(out=o, in0=o, scalar=gain, in1=root, op0=ALU.mult, op1=ALU.mult)
    core.split(o, core.h_high, core.h_low)
    core.linear("vector", core.add_to_x(lambda n: core.mod[:, 1, bass.ds(n + 2 * KB, 1)]))


def norm_in_place(core, gain):
    core.norm(core.x, core.col(gain), None, view(core.arena, 0, 8, T), dst=core.x)



def second_projection(core):
    core.linear("scalar", core.copy_to(view(core.arena, 0, 32, T)))


def scaled_and_shifted(core, dst, src, gain, bias):
    for b in range(4):
        i = core.nc.vector.tensor_scalar(dst[:, b, :], src[:, b, :], core.col(gain, b), core.col(bias, b), ALU.mult, ALU.add)
    return i


def retention(core):
    nc, sig, A = core.nc, core.sig, core.arena
    proj, turned, tokens = view(A, 0, 31, T), view(A, 10496, 8, T), view(A, 12544, 2, 4 * P)
    decay, scores = view(A, 13568, 8, 3 * P), view(A, 16640, 8, 3 * P)
    y, cat = view(A, 19712, 4, T), view(A, 20736, 8, T)
    rope(core, proj[:, 0:8], turned, 4, core.trig[:, 3, :], core.trig[:, 2, :])
    token_major(core, [(proj[:, 8:12], tokens)])
    scored, decayed, mixed, loaded = sig("heads_scored"), sig("heads_weighed"), sig("heads_mixed"), sig("small_loaded")
    differ, scaled, shift = sig("shift_differences"), sig("shifts_scaled"), view(A, 22784, 15, T)
    on_pool = range(8, 15)
    mu = lambda b: core.col("rwkv_mu_2", b) if b < 14 else core.col("rwkv_mu_tail")[0:32]
    rows = lambda x, b: x[0:P if b < 14 else 32, b, :]
    p = proj[:, 16:31]
    later = [(A[:, 31744:31744 + 512], "rwkv_up"), (A[:, 32256:32768], "rwkv_g_up"), (core.scratch[0:32, 3584:4096], "rwkv_g_up_tail"),
             (core.scratch[:, 2048:2048 + 8 * P], "rwkv_masks")]
    n = [0]
    with nc.Block() as block:
        @block.sync
        def _(sp):
            n[0] = core.load(sp, [(A[:, 13568:13568 + 8 * 384], "decay")] + later)

        @block.gpsimd
        def _(pool):
            pool.wait_ge(differ.sem, differ.at(4))
            for b in on_pool:
                i = nc.gpsimd.tensor_scalar(rows(shift, b), rows(shift, b), mu(b), None, ALU.mult)
            i.then_inc(scaled.sem, 1)
            pool.wait_ge(scaled.sem, scaled.at(1))
            for b in on_pool:
                nc.gpsimd.tensor_tensor(rows(p, b), rows(p, b), rows(shift, b), ALU.add)

        @block.tensor
        def _(pe):
            for h in range(8):
                half = slice(64 * (h % 2), 64 * (h % 2) + 64)
                if h >= 4:
                    pe.wait_ge(decayed.sem, decayed.at(h - 3))
                q, k = turned[half, h // 2, :], turned[half, 4 + h // 2, :]
                nc.tensor.matmul(core.bank[h % 4][:, 0:T], k[:, 0:P], q, start=True, stop=True)
                nc.tensor.matmul(core.bank[h % 4][:, T:3 * P], k[:, P:T], q[:, P:T], start=True, stop=True).then_inc(scored.sem, 1)
            for h in range(8):
                half = slice(64 * (h % 2), 64 * (h % 2) + 64)
                pe.wait_ge(decayed.sem, decayed.at(h + 1))
                out = core.bank[4 + h // 2][half]
                nc.tensor.matmul(out[:, 0:T], tokens[:, 0, h * 64:(h + 1) * 64], scores[:, h, 0:T], start=True, stop=False,
                                 skip_group_check=True)
                nc.tensor.matmul(out[:, P:T], tokens[:, 1, h * 64:(h + 1) * 64], scores[:, h, T:3 * P], start=False, stop=True,
                                 skip_group_check=True).then_inc(mixed.sem, 1)

        @block.vector
        def _(dve):
            for blocks, channels in ((slice(0, 14), slice(0, P)), (slice(14, 15), slice(0, 32))):
                before, d = p[channels, blocks], shift[channels, blocks]
                nc.vector.tensor_tensor(d[:, :, 1:T], before[:, :, 0:T - 1], before[:, :, 1:T], ALU.subtract).then_inc(differ.sem, 1)
                nc.vector.tensor_scalar(d[:, :, 0:1], before[:, :, 0:1], -1.0, None, ALU.mult).then_inc(differ.sem, 1)
            dve.wait_ge(differ.sem, differ.at(4))
            dve.wait_ge(loaded.sem, loaded.at(16 * (1 + len(later))))
            for h in range(8):
                nc.vector.scalar_tensor_tensor(out=rows(p, h), in0=rows(shift, h), scalar=mu(h), in1=rows(p, h),
                                               op0=ALU.mult, op1=ALU.add)
                dve.wait_ge(scored.sem, scored.at(h + 1))
                nc.vector.tensor_tensor(scores[:, h, :], core.bank[h % 4][:, 0:3 * P], decay[:, h, :], ALU.mult) \
                    .then_inc(decayed.sem, 1)

        @block.scalar
        def _(act):
            for b in range(4):
                act.wait_ge(mixed.sem, mixed.at(2 * b + 2))
                nc.scalar.activation(y[:, b, :], core.bank[4 + b][:, 0:T], ACT.Identity)
    loaded.close(n[0])
    differ.close(4)
    scaled.close(1)
    for s in (scored, decayed, mixed):
        s.close(8)
    centred, squares, root = view(A, 13568, 4, T), view(A, 14592, 4, T), view(A, 15616, 4, T)
    block_rms(core, y, 4, "half_ones", 64, core.c("eps_ret"), squares, root, centre=centred)
    gated, step = sig("gate_activated"), sig("dve_step")
    with nc.Block() as block:
        @block.tensor
        def _(pe):
            core.keep_warm(3)

        @block.scalar
        def _(act):
            nc.scalar.activation(squares, proj[:, 12:16], ACT.Silu).then_inc(gated.sem, 1)

        @block.vector
        def _(dve):
            link = Chain(step, dve)
            link(nc.vector.tensor_tensor(centred, centred, root, ALU.mult))
            link(scaled_and_shifted(core, centred, centred, "ret_gn_w_2", "ret_gn_b_2"))
            dve.wait_ge(gated.sem, gated.at(1))
            nc.vector.tensor_tensor(cat[:, 0:4], centred, squares, ALU.mult)
            step.used = link.n
    step.close(step.used)
    gated.close(1)


def rwkv(core):
    nc, sig, A = core.nc, core.sig, core.arena
    proj, cat = view(A, 0, 31, T), view(A, 20736, 8, T)
    step = sig("dve_step")
    spots = [8192 + 1024 * i for i in range(12)] + [22784 + 1024 * i for i in range(9)]
    area = lambda i, n=1: view(A, spots[i], 4 * n, T)
    r, k, v = proj[:, 16:20], proj[:, 20:24], proj[:, 24:28]
    low = proj[:, 28]
    up, g_up, g_up_tail = A[:, 31744:31744 + 512], A[:, 32256:32768], core.scratch[0:32, 3584:4096]
    loaded = sig("small_loaded")

    sig_w, a, gate, kk, squares, norm = area(0), area(2), area(3), area(4), area(5), area(6)
    hidden, sums = sig("hidden_ready"), sig("low_rank_ready")
    with nc.Block() as block:
        @block.scalar
        def _(act):
            nc.scalar.activation(low[0:64], low[0:64], ACT.Tanh)
            nc.scalar.activation(proj[:, 29], proj[:, 29], ACT.Sigmoid)
            nc.scalar.activation(proj[0:32, 30], proj[0:32, 30], ACT.Sigmoid).then_inc(hidden.sem, 1)
            for b in range(4):
                act.wait_ge(sums.sem, sums.at(b + 1))
                nc.scalar.activation(sig_w[:, b, :], core.bank[b][:, 0:T], ACT.Sigmoid, bias=core.col("rwkv_w0_2", b))
                nc.scalar.activation(a[:, b, :], core.bank[4 + b][:, 0:T], ACT.Sigmoid, bias=core.col("rwkv_a0_2", b))
                nc.scalar.activation(gate[:, b, :], core.bank[b][:, T:2 * T], ACT.Identity)

        @block.tensor
        def _(pe):
            core.keep_warm(2)
            pe.wait_ge(hidden.sem, hidden.at(1))
            for b in range(4):
                c = slice(b * P, (b + 1) * P)
                nc.tensor.matmul(core.bank[b][:, 0:T], up[0:64, c], low[0:64], start=True, stop=True)
                nc.tensor.matmul(core.bank[4 + b][:, 0:T], up[64:P, c], low[64:P], start=True, stop=True)
                nc.tensor.matmul(core.bank[b][:, T:2 * T], g_up[:, c], proj[:, 29], start=True, stop=False)
                nc.tensor.matmul(core.bank[b][:, T:2 * T], g_up_tail[:, c], proj[0:32, 30], start=False, stop=True) \
                    .then_inc(sums.sem, 1)

        @block.vector
        def _(dve):
            for b in range(4):
                nc.vector.tensor_scalar(kk[:, b, :], k[:, b, :], core.col("rwkv_k_k_2", b), None, ALU.mult)
    hidden.close(1)
    sums.close(4)
    squared, summed, bounded, logged, rooted = (sig(x) for x in (
        "squared", "square_sums", "squares_bounded", "logged", "rooted"))
    flat = lambda x: x.rearrange("p n t -> p (n t)")
    decay_sum, decay_log = area(1), area(0)
    reset = flat(area(7))
    cols = [0]
    with nc.Block() as block:
        @block.sync
        def _(sp):
            cols[0] = core.load(sp, [(reset, "reset")])

        @block.vector
        def _(dve):
            link = Chain(step, dve)
            nc.vector.tensor_tensor(squares, kk, kk, ALU.mult).then_inc(squared.sem, 1)
            link(nc.vector.tensor_scalar(decay_log, sig_w, -math.exp(-0.5), None, ALU.mult))
            dve.wait_ge(loaded.sem, loaded.at(16))
            link(nc.vector.tensor_tensor_scan(flat(decay_sum), reset, flat(decay_log), 0.0, ALU.mult, ALU.add))
            dve.wait_ge(summed.sem, summed.at(1))
            for i in range(2):
                nc.vector.tensor_scalar(flat(norm)[:, i * BANK:(i + 1) * BANK], core.bank[i][:], 1e-24, None, ALU.max) \
                    .then_inc(bounded.sem, 1)
            dve.wait_ge(rooted.sem, rooted.at(1))
            link(nc.vector.tensor_tensor(kk, kk, norm, ALU.mult))
            for b in range(4):
                i = nc.vector.tensor_scalar(squares[:, b, :], a[:, b, :], 1.0, core.col("rwkv_k_a_2", b), ALU.subtract, ALU.mult)
            link(i)
            link(nc.vector.scalar_tensor_tensor(out=k, in0=squares, scalar=1.0, in1=k, op0=ALU.add, op1=ALU.mult))
            link(nc.vector.tensor_tensor(a, kk, a, ALU.mult))
            step.used = link.n

        @block.tensor
        def _(pe):
            pe.wait_ge(squared.sem, squared.at(1))
            for i in range(2):
                mm = nc.tensor.matmul(core.bank[i][:], core.c("half_ones"), flat(squares)[:, i * BANK:(i + 1) * BANK], start=True, stop=True)
            mm.then_inc(summed.sem, 1)
            core.keep_warm(7)

        @block.scalar
        def _(act):
            for i in range(2):
                part = flat(norm)[:, i * BANK:(i + 1) * BANK]
                act.wait_ge(bounded.sem, bounded.at(i + 1))
                nc.scalar.activation(part, part, ACT.Ln).then_inc(logged.sem, 1)
            act.wait_ge(logged.sem, logged.at(2))
            nc.scalar.activation(norm, norm, ACT.Exp, scale=-0.5).then_inc(rooted.sem, 1)
    step.close(step.used)
    loaded.close(cols[0])
    for s, count in ((squared, 1), (summed, 1), (bounded, 2), (logged, 2), (rooted, 1)):
        s.close(count)
    b_vec = a

    upto, before, inverse, rest = area(7), area(8), area(9), area(10)
    a_in, b_out, k_out, r_in, b_end, k_end = area(5), area(6), area(9), area(7), area(11), area(12)
    logs = area(13)
    chunks = lambda x: x.rearrange("p n (c t) -> p (n c) t", t=CHUNK)
    exped = sig("decays_exped")
    with nc.Block() as block:
        @block.tensor
        def _(pe):
            core.keep_warm(12)

        @block.vector
        def _(dve):
            link = Chain(step, dve)
            link(nc.vector.tensor_tensor(before, decay_sum, decay_log, ALU.subtract))
            last = chunks(decay_sum)[:, :, CHUNK - 1:CHUNK].to_broadcast([P, 16, CHUNK])
            nc.vector.tensor_tensor(chunks(rest), last, chunks(decay_sum), ALU.subtract).then_inc(exped.sem, 1)
            dve.wait_ge(exped.sem, exped.at(5))
            link(nc.vector.scalar_tensor_tensor(out=a_in, in0=kk, scalar=-1.0, in1=before, op0=ALU.mult, op1=ALU.mult))
            link(nc.vector.tensor_tensor(b_out, b_vec, inverse, ALU.mult))
            link(nc.vector.tensor_tensor(k_out, k, inverse, ALU.mult))
            link(nc.vector.tensor_tensor(b_end, b_vec, rest, ALU.mult))
            link(nc.vector.tensor_tensor(k_end, k, rest, ALU.mult))
            link(nc.vector.tensor_copy(core.work[:, 0:16], chunks(upto)[:, :, CHUNK - 1]))
            for b in range(4):
                i = nc.vector.scalar_tensor_tensor(out=logs[:, b, :], in0=r[:, b, :], scalar=core.col("rwkv_r_k_2", b),
                                                   in1=k[:, b, :], op0=ALU.mult, op1=ALU.mult)
            link(i)
            link(nc.vector.tensor_tensor(r_in, r, upto, ALU.mult))
            step.used = link.n

        @block.scalar
        def _(act):
            act.wait_ge(exped.sem, exped.at(1))
            for dst, src, scale in ((upto, decay_sum, 1.0), (before, before, 1.0), (inverse, decay_sum, -1.0), (rest, rest, 1.0)):
                nc.scalar.activation(dst, src, ACT.Exp, scale=scale).then_inc(exped.sem, 1)
    step.close(step.used)
    exped.close(5)
    bonus_terms = logs

    a_tok, b_tok, k_tok, v_tok = (view(A, spots[i], 2, 4 * P) for i in (0, 1, 2, 14))
    token_major(core, [(a_in, a_tok), (b_end, b_tok), (k_end, k_tok), (v, v_tok)])

    wide = lambda at: view(A, at, 8, P)
    masks = view(core.scratch, 2048, 8, P)
    NT, inv, inv_T = wide(spots[8]), wide(spots[10]), wide(spots[11])
    M1, LT = wide(spots[12]), wide(spots[15])
    RB, RK = wide(spots[16]), wide(spots[17])
    LV, both = view(core.scratch, 0, 8, 64), wide(spots[18])
    M_T, Q, R2, y = area(19), area(4), area(20), view(core.scratch, 1024, 4, T)
    M_T_c = M_T.rearrange("p n (c k) -> p n c k", c=CHUNKS)
    Q_c = Q.rearrange("p n (c k) -> p n c k", c=CHUNKS)
    eye2 = core.c("eye2")
    full, out_ready = sig("products_ready"), sig("products_kept")

    def tile(t):
        tk = slice(t * P, (t + 1) * P)
        half = lambda h: slice(64 * (h % 2), 64 * (h % 2) + 64)
        hc = lambda h: slice(h * 64, (h + 1) * 64)
        mask = lambda i: masks[:, i, :].unsqueeze(1).to_broadcast([P, 4, P])
        kinds = [(b_out, a_in, NT, 6), (k_out, a_in, LT, 6), (b_out, r_in, RB, 7), (k_out, r_in, RK, 7)]
        bank4 = lambda i: core.bank[i][:].rearrange("p (h k) -> p h k", h=4)
        with nc.Block() as block:
            @block.tensor
            def _(pe):
                for n, (left, right, _, _) in enumerate(kinds):
                    for g in range(2):
                        for h in range(g, 8, 2):
                            mm = nc.tensor.matmul(core.bank[2 * n + g][:, (h // 2) * P:(h // 2 + 1) * P], left[half(h), h // 2, tk],
                                                  right[half(h), h // 2, tk], start=True, stop=True)
                        mm.then_inc(full.sem, 1)

            @block.vector
            def _(dve):
                for n, (_, _, dst, which) in enumerate(kinds):
                    for g in range(2):
                        dve.wait_ge(full.sem, full.at(2 * n + g + 1))
                        nc.vector.tensor_tensor(dst[:, g:8:2, :], bank4(2 * n + g), mask(which), ALU.mult)

            @block.gpsimd
            def _(pool):
                for g in range(8):
                    nc.gpsimd.tensor_copy(inv[:, g, :], core.c("ident"))
                    nc.gpsimd.tensor_copy(inv_T[:, g, :], core.c("ident"))
        full.close(8)

        with nc.Block() as block:
            @block.tensor
            def _(pe):
                for level in range(6):
                    for g in range(2):
                        if level:
                            pe.wait_ge(out_ready.sem, out_ready.at(4 * (level - 1) + 2 + g + 1))
                        for h in range(4 * g, 4 * g + 4):
                            mm = nc.tensor.matmul(core.bank[g][:, (h % 4) * P:(h % 4 + 1) * P], NT[:, h, :], inv[:, h, :],
                                                  start=True, stop=True)
                        mm.then_inc(full.sem, 1)
                    for g in range(2):
                        pe.wait_ge(out_ready.sem, out_ready.at(4 * level + g + 1))
                        for h in range(4 * g, 4 * g + 4):
                            c = slice((h % 4) * P, (h % 4 + 1) * P)
                            if 0 < level < 5:
                                nc.tensor.matmul(core.bank[2 + g][:, c], inv_T[:, h, :], M1[:, h, :], start=True, stop=True)
                            mm = nc.tensor.matmul(core.bank[4 + g][:, c], M1[:, h, :], inv_T[:, h, :], start=True, stop=True)
                        mm.then_inc(full.sem, 1)

            @block.vector
            def _(dve):
                for level in range(6):
                    for g in range(2):
                        dve.wait_ge(full.sem, full.at(4 * level + g + 1))
                        nc.vector.tensor_tensor(M1[:, 4 * g:4 * g + 4, :], bank4(g), mask(level), ALU.mult).then_inc(out_ready.sem, 1)
                    for g in range(2):
                        dve.wait_ge(full.sem, full.at(4 * level + 2 + g + 1))
                        s = slice(4 * g, 4 * g + 4)
                        if level < 5:
                            nc.vector.tensor_tensor(inv[:, s, :], inv[:, s, :], bank4(2 + g) if level else M1[:, s, :], ALU.add)
                        nc.vector.tensor_tensor(inv_T[:, s, :], inv_T[:, s, :], bank4(4 + g), ALU.add).then_inc(out_ready.sem, 1)
        full.close(24)
        out_ready.close(24)

        with nc.Block() as block:
            @block.tensor
            def _(pe):
                for h in range(8):
                    mm = nc.tensor.matmul(core.bank[0][:, hc(h)], LT[:, h, :], v_tok[:, t, hc(h)], start=True, stop=True)
                mm.then_inc(full.sem, 1)
                for g in range(2):
                    for h in range(4 * g, 4 * g + 4):
                        at = (h % 4) * P
                        mm = nc.tensor.matmul(core.bank[1 + g][:, at + 64:at + P], inv_T[:, h, :], a_tok[:, t, hc(h)], start=True, stop=True)
                core.keep_warm(1)
                pe.wait_ge(out_ready.sem, out_ready.at(1))
                for g in range(2):
                    for h in range(4 * g, 4 * g + 4):
                        at = (h % 4) * P
                        mm = nc.tensor.matmul(core.bank[1 + g][:, at:at + 64], inv_T[:, h, :], LV[:, h, :], start=True, stop=True)
                    mm.then_inc(full.sem, 1)
                core.keep_warm(1)
                pe.wait_ge(out_ready.sem, out_ready.at(3))
                for c in range(2):
                    rows = slice(64 * c, 64 * c + 64)
                    for h in range(8):
                        at = slice((h // 2) * 64, (h // 2) * 64 + 64)
                        nc.tensor.matmul(core.bank[3 + c][half(h), at], both[rows, h, 64:P], b_tok[rows, t, hc(h)],
                                         start=True, stop=True, skip_group_check=True)
                    for h in range(8):
                        at = slice(T + (h // 2) * 64, T + (h // 2) * 64 + 64)
                        nc.tensor.matmul(core.bank[3 + c][half(h), at], b_tok[rows, t, hc(h)], both[rows, h, 0:64],
                                         start=True, stop=False, skip_group_check=True)
                        mm = nc.tensor.matmul(core.bank[3 + c][half(h), at], k_tok[rows, t, hc(h)], v_tok[rows, t, hc(h)],
                                              start=False, stop=True, skip_group_check=True)
                    mm.then_inc(full.sem, 1)
                for h in range(8):
                    at = slice((h // 2) * P, (h // 2 + 1) * P)
                    nc.tensor.matmul(core.bank[5][half(h), at], both[:, h, 64:P], RB[:, h, :], start=True, stop=True,
                                     skip_group_check=True)
                    nc.tensor.matmul(core.bank[6][half(h), at], both[:, h, 0:64], RB[:, h, :], start=True, stop=False,
                                     skip_group_check=True)
                    mm = nc.tensor.matmul(core.bank[6][half(h), at], v_tok[:, t, hc(h)], RK[:, h, :], start=False, stop=True,
                                          skip_group_check=True)
                mm.then_inc(full.sem, 1)

            @block.vector
            def _(dve):
                dve.wait_ge(full.sem, full.at(1))
                nc.vector.tensor_copy(LV, core.bank[0][:].rearrange("p (h k) -> p h k", h=8)).then_inc(out_ready.sem, 1)
                for g in range(2):
                    dve.wait_ge(full.sem, full.at(2 + g))
                    nc.vector.tensor_copy(both[:, 4 * g:4 * g + 4, :], bank4(1 + g)).then_inc(out_ready.sem, 1)
                for c in range(2):
                    dve.wait_ge(full.sem, full.at(4 + c))
                    chunk = 2 * t + c
                    for b in range(4):
                        nc.vector.scalar_tensor_tensor(out=M_T_c[:, b, chunk, :], in0=eye2,
                                                       scalar=core.work[:, b * CHUNKS + chunk:b * CHUNKS + chunk + 1],
                                                       in1=core.bank[3 + c][:, b * 64:(b + 1) * 64], op0=ALU.mult, op1=ALU.add)
                    nc.vector.tensor_copy(Q_c[:, :, chunk, :], core.bank[3 + c][:, T:2 * T].rearrange("p (n k) -> p n k", n=4))
                dve.wait_ge(full.sem, full.at(6))
                nc.vector.tensor_tensor(R2[:, :, tk], r_in[:, :, tk], bank4(5), ALU.add)
                nc.vector.tensor_copy(y[:, :, tk], bank4(6))
        full.close(6)
        out_ready.close(3)

    for t in range(TT):
        tile(t)

    states = view(A, spots[8], 12, 64)
    state = lambda c: states[:, 4 * (c - 1):4 * c, :]
    part = lambda h: slice(64 * (h % 2), 64 * (h % 2) + 64)
    with nc.Block() as block:
        @block.tensor
        def _(pe):
            for c in range(1, CHUNKS):
                pe.wait_ge(out_ready.sem, out_ready.at(c))
                if c < CHUNKS - 1:
                    for h in range(8):
                        mm = nc.tensor.matmul(core.bank[c][part(h), (h // 2) * 64:(h // 2) * 64 + 64], M_T_c[part(h), h // 2, c, :],
                                              state(c)[part(h), h // 2, :], start=True, stop=True, skip_group_check=True)
                    mm.then_inc(full.sem, 1)
                for h in range(8):
                    mm = nc.tensor.matmul(core.bank[3 + c][part(h), (h // 2) * 64:(h // 2) * 64 + 64], state(c)[part(h), h // 2, :],
                                          R2[part(h), h // 2, c * CHUNK:(c + 1) * CHUNK], start=True, stop=True, skip_group_check=True)
                mm.then_inc(full.sem, 1)

        @block.vector
        def _(dve):
            bank64 = lambda i: core.bank[i][:, 0:T].rearrange("p (n k) -> p n k", n=4)
            nc.vector.tensor_copy(state(1), Q_c[:, :, 0, :]).then_inc(out_ready.sem, 1)
            count = 0
            for c in range(1, CHUNKS):
                if c < CHUNKS - 1:
                    count += 1
                    dve.wait_ge(full.sem, full.at(count))
                    nc.vector.tensor_tensor(state(c + 1), bank64(c), Q_c[:, :, c, :], ALU.add).then_inc(out_ready.sem, 1)
                count += 1
                dve.wait_ge(full.sem, full.at(count))
                out = y[:, :, c * CHUNK:(c + 1) * CHUNK]
                nc.vector.tensor_tensor(out, out, bank64(3 + c), ALU.add)
    full.close(5)
    out_ready.close(3)

    centred, squares, root = area(0), area(1), area(2)
    block_rms(core, y, 4, "half_ones", 64, core.c("eps_rwkv"), squares, root, centre=centred)
    with nc.Block() as block:
        @block.tensor
        def _(pe):
            for i in range(2):
                mm = nc.tensor.matmul(core.bank[i][:], core.c("half_ones"), flat(bonus_terms)[:, i * BANK:(i + 1) * BANK],
                                      start=True, stop=True)
            mm.then_inc(full.sem, 1)
            core.keep_warm(5)

        @block.vector
        def _(dve):
            link = Chain(step, dve)
            link(nc.vector.tensor_tensor(centred, centred, root, ALU.mult))
            link(scaled_and_shifted(core, centred, centred, "rwkv_gn_w_2", "rwkv_gn_b_2"))
            dve.wait_ge(full.sem, full.at(1))
            for i in range(2):
                j = nc.vector.tensor_tensor(flat(squares)[:, i * BANK:(i + 1) * BANK], core.bank[i][:],
                                            flat(v)[:, i * BANK:(i + 1) * BANK], ALU.mult)
            link(j)
            link(nc.vector.tensor_tensor(centred, centred, squares, ALU.add))
            nc.vector.tensor_tensor(cat[:, 4:8], centred, gate, ALU.mult)
            step.used = link.n
    step.close(step.used)
    full.close(1)


def second_mixer(core):
    second_projection(core)
    retention(core)
    rwkv(core)
    core.split(view(core.arena, 20736, 8, T), core.h_high, core.h_low)
    core.linear("vector", core.add_to_x())



def cross_attention(core):
    nc, sig, A = core.nc, core.sig, core.arena
    scratch, mem, q, kv = view(A, 0, 8, T), view(A, 2048, 8, T), view(A, 4096, 8, T), view(A, 6144, 16, T)
    tokens, o = view(A, 10240, 2, D), view(A, 12288, 8, T)
    probs, probs_T = view(A, 14336, 4, T), view(A, 15360, 4, T)
    small = A[:, 16384:16384 + 16]
    step = sig("dve_step")
    core.norm(core.x, core.col("norm_xattn_2"), None, scratch)
    core.linear("scalar", core.copy_to(q), loads=[(mem, "mem")])
    core.norm(mem, core.col("norm_mem_2"), None, scratch)
    core.linear("scalar", core.copy_to(kv))
    token_major(core, [(kv[:, 8:16], tokens)])
    scored, peaked, exped, weighed, flipped, kept, mixed, mixed_taken = (sig(x) for x in (
        "heads_scored", "heads_peaked", "heads_exped", "heads_weighed", "heads_flipped", "flips_kept", "heads_mixed", "mixed_taken"))
    scale = 1.0 / 16
    with nc.Block() as block:
        @block.tensor
        def _(pe):
            def scores(h):
                if h >= 2:
                    pe.wait_ge(exped.sem, exped.at(h - 1))
                for i in range(2):
                    for b in range(2):
                        mm = nc.tensor.matmul(core.bank[h % 2][:, i * T:(i + 1) * T], q[:, 2 * h + b, i * P:(i + 1) * P],
                                              kv[:, 2 * h + b, :], start=(b == 0), stop=(b == 1))
                mm.then_inc(scored.sem, 1)

            scores(0)
            for h in range(4):
                if h + 1 < 4:
                    scores(h + 1)
                pe.wait_ge(weighed.sem, weighed.at(h + 1))
                if h >= 2:
                    pe.wait_ge(kept.sem, kept.at(h - 1))
                for m in range(2):
                    for i in range(2):
                        mm = nc.tensor.transpose(core.bank[2 + h % 2][:, m * T + i * P:m * T + (i + 1) * P],
                                                 probs[:, 2 * (h % 2) + i, m * P:(m + 1) * P], core.c("ident"))
                mm.then_inc(flipped.sem, 1)
                pe.wait_ge(kept.sem, kept.at(h + 1))
                if h >= 2:
                    pe.wait_ge(mixed_taken.sem, mixed_taken.at(h - 1))
                for b in range(2):
                    for m in range(2):
                        mm = nc.tensor.matmul(core.bank[4 + h % 2][:, b * T:(b + 1) * T],
                                              tokens[:, m, (2 * h + b) * P:(2 * h + b + 1) * P], probs_T[:, 2 * (h % 2) + m, :],
                                              start=(m == 0), stop=(m == 1))
                mm.then_inc(mixed.sem, 1)

        @block.vector
        def _(dve):
            link = Chain(step, dve)
            for h in range(4):
                dve.wait_ge(scored.sem, scored.at(h + 1))
                link(nc.vector.tensor_reduce(small[:, 0:2], core.bank[h % 2][:].rearrange("p (i m) -> p i m", i=2), AX_X, ALU.max))
                nc.vector.tensor_scalar(small[:, 2:4], small[:, 0:2], -scale, None, ALU.mult).then_inc(peaked.sem, 1)
                dve.wait_ge(exped.sem, exped.at(h + 1))
                link(nc.vector.reciprocal(small[:, 4:6], small[:, 4:6]))
                for i in range(2):
                    p = probs[:, 2 * (h % 2) + i, :]
                    j = nc.vector.tensor_scalar(p, p, small[:, 4 + i:5 + i], None, ALU.mult)
                j.then_inc(weighed.sem, 1)
            step.used = link.n

        @block.scalar
        def _(act):
            for h in range(5):
                if h < 4:
                    act.wait_ge(peaked.sem, peaked.at(h + 1))
                    if h >= 2:
                        act.wait_ge(flipped.sem, flipped.at(h - 1))
                    for i in range(2):
                        j = nc.scalar.activation(probs[:, 2 * (h % 2) + i, :], core.bank[h % 2][:, i * T:(i + 1) * T], ACT.Exp,
                                                 bias=small[:, 2 + i:3 + i], scale=scale, accum_out=small[:, 4 + i:5 + i])
                    j.then_inc(exped.sem, 1)
                if h >= 1:
                    act.wait_ge(mixed.sem, mixed.at(h))
                    nc.scalar.activation(o[:, 2 * h - 2:2 * h, :], core.bank[4 + (h - 1) % 2][:].rearrange("p (b t) -> p b t", b=2),
                                         ACT.Identity).then_inc(mixed_taken.sem, 1)
                if h < 4:
                    act.wait_ge(flipped.sem, flipped.at(h + 1))
                    s = slice(2 * (h % 2), 2 * (h % 2) + 2)
                    nc.scalar.activation(probs_T[:, s, :], core.bank[2 + h % 2][:].rearrange("p (m t) -> p m t", m=2),
                                         ACT.Identity).then_inc(kept.sem, 1)
    step.close(step.used)
    for s in (scored, peaked, exped, weighed, flipped, kept, mixed, mixed_taken):
        s.close(4)
    core.split(o, core.h_high, core.h_low)
    core.linear("vector", core.add_to_x())


def mlp(core):
    nc = core.nc
    hidden = view(core.arena, 2048, 32, T)
    core.norm(core.x, core.col("norm_mlp_2"), None, view(core.arena, 0, 8, T))
    positive = core.sig("positive_part")

    def squared_relu(n, bank):
        part = hidden[:, n, :]
        nc.vector.tensor_scalar(part, bank, 0.0, None, ALU.max).then_inc(positive.sem, 1)
        nc.vector.wait_ge(positive.sem, n + positive.at(1))
        return nc.vector.tensor_tensor(part, part, bank, ALU.mult)

    core.linear("vector", squared_relu)
    positive.close(32)
    core.split(hidden, core.hidden_high, core.hidden_low)
    core.linear("vector", core.add_to_x(), groups=4, rhs=(core.hidden_high, core.hidden_low))
    core.norm(core.x, core.col("norm_final_2"), None, view(core.arena, 0, 8, T), dst=core.x)


def column_blocks(w):

    k, n = w.shape
    w = w.reshape(k // D, KB, P, n // P, P).transpose(3, 0, 2, 1, 4)
    return np.ascontiguousarray(w.reshape(-1, P, KB * P))


def columns(*vectors):
    return np.concatenate([np.asarray(v).reshape(-1, P).T for v in vectors], axis=1)


def tokens_last(a):
    return np.ascontiguousarray(a.reshape(T, KB, P).transpose(2, 1, 0))


def layouts(i):
    out = dict(shape_constants())
    names = []

    def add(name, v):
        v = np.asarray(v).reshape(-1, P).T
        at = COLS_AT[0]
        COLS[name] = (at, at + v.shape[1])
        COLS_AT[0] += v.shape[1]
        names.append(v)

    COLS_AT = [0]
    add("c", i["c"])
    for layer in range(2):
        add(f"ada_b{layer}", i["ada_b"][layer])
        add(f"norm_mix{layer}", i["norm_mix"][layer])
        add(f"norm_ffn{layer}", i["norm_ffn"][layer])
    add("ev_g_v", i["ev_g_v"])
    add("ev_pool_scale", i["ev_pool_scale"])
    add("od_g_sub", i["od_g_sub"])
    for name in ("final_norm", "norm_mix_2", "ret_gn_w_2", "ret_gn_b_2", "rwkv_w0_2", "rwkv_a0_2", "rwkv_k_k_2",
                 "rwkv_k_a_2", "rwkv_r_k_2", "rwkv_gn_w_2", "rwkv_gn_b_2", "norm_xattn_2", "norm_mem_2", "norm_mlp_2",
                 "norm_final_2"):
        add(name, i[name])
    mu = np.asarray(i["rwkv_mu_2"]).reshape(-1)
    add("rwkv_mu_2", mu[:14 * P])
    add("rwkv_mu_tail", np.concatenate([mu[14 * P:]] * 4))
    out["cols"] = np.ascontiguousarray(np.concatenate(names, axis=1))
    out["x"] = tokens_last(i["x"])
    out["mem"] = tokens_last(i["mem_2"])
    out["positions"] = np.ascontiguousarray(np.tile(np.concatenate(
        [i["positions"].reshape(1, T), i["positions_2"].reshape(1, T)], axis=1), (P, 1)))
    for layer in range(2):
        out[f"ada_w{layer}"] = column_blocks(i["ada_w"][layer])
        out[f"peer_w_q{layer}"] = column_blocks(i["peer_w_q"][layer].reshape(D, -1))
        out[f"peer_keys{layer}"] = np.ascontiguousarray(i["peer_sub_keys"][layer].transpose(3, 0, 1, 2)).reshape(P, -1)
        out[f"peer_u{layer}"] = column_blocks(i["peer_u"][layer].T)
        out[f"peer_v{layer}"] = np.ascontiguousarray(i["peer_v"][layer].reshape(P, P, D))
    out["ev_w_in"] = column_blocks(i["ev_w_in"][0])
    out["ev_w_s"] = np.ascontiguousarray(i["ev_w_s"][0].transpose(2, 0, 1))
    out["ev_b_s"] = np.ascontiguousarray(np.tile(i["ev_b_s"].reshape(1, 4, P), (P, 1, 1)))
    out["ev_w_pool"] = np.ascontiguousarray(i["ev_w_pool"][0].transpose(1, 0, 2))
    out["ev_w_out"] = column_blocks(i["ev_w_out"][0])
    out["od_w_in"] = column_blocks(i["od_w_in"][0])
    out["od_w_out"] = column_blocks(i["od_w_out"][0])
    out["od_lam"] = np.ascontiguousarray(np.tile(np.stack(
        [i[f"od_lam_{n}"].reshape(64) for n in ("q1", "k1", "q2", "k2")])[None], (P, 1, 1)))
    w_in = np.asarray(i["w_in_2"][0])
    out["w_in_2"] = column_blocks(np.pad(w_in, ((0, 0), (0, 32 * P - w_in.shape[1]))))
    out["rwkv_up"] = np.ascontiguousarray(np.concatenate([i["rwkv_w_up_2"][0], i["rwkv_a_up_2"][0]]))
    out["rwkv_g_up"] = np.ascontiguousarray(i["rwkv_g_up_2"][0][:P])
    out["rwkv_g_up_tail"] = np.ascontiguousarray(i["rwkv_g_up_2"][0][P:])
    out["w_out_2"] = column_blocks(i["w_out_2"][0])
    out["xattn_w_q"] = column_blocks(i["xattn_w_q_2"][0])
    out["xattn_w_kv"] = column_blocks(i["xattn_w_kv_2"][0])
    out["xattn_w_o"] = column_blocks(i["xattn_w_o_2"][0])
    out["mlp_w_up"] = column_blocks(i["mlp_w_up_2"][0])
    out["mlp_w_down"] = column_blocks(i["mlp_w_down_2"][0])
    return out


SEGMENTS = ["ev_w_in", "ev_w_out", "peer_w_q0", "peer_u0", "peer_v0", "od_w_in", "od_w_out",
            "peer_w_q1", "peer_u1", "peer_v1", "w_in_2", "w_out_2", "xattn_w_q", "xattn_w_kv", "xattn_w_o",
            "mlp_w_up", "mlp_w_down"]

STEPS = [
    ("setup", setup),
    ("norm0", lambda core: mixer_norm(core, 0)),
    ("even", even_mixer),
    ("peer0", lambda core: peer(core, 0)),
    ("norm1", lambda core: mixer_norm(core, 1)),
    ("odd", odd_mixer),
    ("peer1", lambda core: peer(core, 1)),
    ("first_end", lambda core: norm_in_place(core, "final_norm")),
    ("norm2", lambda core: core.norm(core.x, core.col("norm_mix_2"), None, view(core.arena, 0, 8, T))),
    ("second_mixer", second_mixer),
    ("cross", cross_attention),
    ("mlp", mlp),
]


def store(core, out):
    nc = core.nc
    stored = core.sig("stored")
    with nc.Block() as block:
        @block.sync
        def _(sp):
            sp.dma_start(out, core.x[:]).then_inc(stored.sem, 16)
            sp.wait_ge(stored.sem, 16)


def program(nc, dram, out, steps=STEPS, source=None):
    core = Core(nc, dram)
    for name in SEGMENTS:
        core.add_segment(name)
    for _, step in steps:
        step(core)
    if source is not None:
        source(core)
    store(core, out)
    return core


def kernel(**inputs):
    import numpy as _np
    import concourse.bacc as _bacc
    from concourse import mybir as _mybir
    from concourse.bass_utils import run_bass_kernel_spmd as _run

    nc = _bacc.Bacc("TRN2", target_bir_lowering=False, num_devices=1)
    arrays, dram = {}, {}
    for name, a in layouts({k: _np.asarray(v) for k, v in inputs.items()}).items():
        arrays[f"{name}_dram"] = a
        dram[name] = nc.dram_tensor(f"{name}_dram", a.shape, _mybir.dt.from_np(a.dtype), kind="ExternalInput").ap()
    out = nc.dram_tensor("out_dram", (P, KB, T), F32, kind="ExternalOutput").ap()
    program(nc, dram, out)
    r = _run(nc, [arrays], core_ids=[0])
    return _np.ascontiguousarray(r.results[0]["out_dram"].transpose(2, 1, 0)).reshape(1, T, D)
```
